# Optimizing a Trainium2 kernel written in Bass

```python
import math
import jax, jax.numpy as jnp
from jax import lax
import numpy as np

D_MODEL = 1024
BATCH = 1
SEQ = 512
DEPTH = 1
DEC_BATCH = 8
DEC_SEQ = 1
PAST_LEN = 4096
PAGE_SIZE = 128

ATT_GROUPS = ((128, 1), (512, 4), (2048, 16))
HEADS_PER_GROUP = 4
HEAD_DIM = 64
N_ATT_GROUPS = len(ATT_GROUPS)
N_ATT_HEADS = N_ATT_GROUPS * HEADS_PER_GROUP
ATT_OUT = HEADS_PER_GROUP * HEAD_DIM
QKV_GROUP = 3 * ATT_OUT
Q_BLOCK = 128

SSM_WIDTH = D_MODEL // 2
SSM_GROUP_CH = 16
SSM_GROUPS = SSM_WIDTH // SSM_GROUP_CH
SSM_STATE = 64
DT_MIN = 1e-3
DT_MAX = 1e-1

MEM_TOKENS = 256
MEM_HEADS = 4
MEM_HEAD_DIM = D_MODEL // 8
MEM_WIDTH = MEM_HEADS * MEM_HEAD_DIM

N_BRANCHES = 3
SSM_COL = N_ATT_GROUPS * QKV_GROUP
MEMQ_COL = SSM_COL + SSM_WIDTH
GATE_COL = MEMQ_COL + MEM_WIDTH
IN_COLS = GATE_COL + N_BRANCHES * D_MODEL

MOE_GROUPS = 4
EXPERTS_PER_GROUP = 8
N_EXPERTS = MOE_GROUPS * EXPERTS_PER_GROUP
TOP_K = 2
D_EXPERT = D_MODEL // 2
MOE_BLOCK = 128

RMS_EPS = 1e-6

kernel_name = 'hybrid_dilated_s5_hmoe_decode_step'

def rmsnorm(x, g):
    xf = x.astype(jnp.float32)
    xf = xf * lax.rsqrt(jnp.mean(xf * xf, axis=-1, keepdims=True) + RMS_EPS)
    return xf.astype(x.dtype) * g

def alibi_slopes():
    h = jnp.arange(1, N_ATT_HEADS + 1, dtype=jnp.float32)
    return jnp.exp2(-8.0 * h / N_ATT_HEADS)

def dilated_attention(q, k, v, q_start, dilation, n_keys, slopes):
    bsz, lq, nh, dh = q.shape
    qb = lq if lq <= Q_BLOCK else math.gcd(lq, Q_BLOCK)
    n_blocks = lq // qb
    steps = jnp.arange(n_keys)
    bias = -slopes[:, None] * (steps * dilation).astype(jnp.float32)[None, :]
    scale = dh ** -0.5

    def one_block(bi):
        q_blk = lax.dynamic_slice_in_dim(q, bi * qb, qb, axis=1)
        rows = q_start + bi * qb + jnp.arange(qb)[:, None] - dilation * steps[None, :]
        valid = rows >= 0
        rows = jnp.maximum(rows, 0)
        k_g = k[:, rows]
        v_g = v[:, rows]
        s = jnp.einsum('bqhd,bqkhd->bqhk', q_blk, k_g).astype(jnp.float32) * scale + bias
        s = jnp.where(valid[None, :, None, :], s, -jnp.inf)
        m = jnp.max(s, axis=-1, keepdims=True)
        p = jnp.exp(s - m)
        den = jnp.sum(p, axis=-1, keepdims=True)
        o = jnp.einsum('bqhk,bqkhd->bqhd', (p / den).astype(v.dtype), v_g)
        return o, (m + jnp.log(den))[..., 0]

    o, lse = lax.map(one_block, jnp.arange(n_blocks))
    o = jnp.moveaxis(o, 0, 1).reshape(bsz, lq, nh, dh)
    lse = jnp.moveaxis(lse, 0, 1).reshape(bsz, lq, nh)
    return o, lse

def s5_branch(u, h0_re, h0_im, lam_re, lam_im, log_dt, b_re, b_im, c_re, c_im, d_skip, w_glu, b_glu):
    bsz, seq, _ = u.shape
    f32 = jnp.float32
    uf = u.astype(f32)
    ug = uf.reshape(bsz, seq, SSM_GROUPS, SSM_GROUP_CH)
    lr = lam_re.astype(f32)
    li = lam_im.astype(f32)
    dt = jnp.exp(log_dt.astype(f32))[:, None]
    mag = jnp.exp(lr * dt)
    ab_re = mag * jnp.cos(li * dt)
    ab_im = mag * jnp.sin(li * dt)
    den = lr * lr + li * li
    nr = ab_re - 1.0
    ni = ab_im
    z_re = ((nr * lr + ni * li) / den)[..., None]
    z_im = ((ni * lr - nr * li) / den)[..., None]
    br = b_re.astype(f32)
    bi = b_im.astype(f32)
    bb_re = z_re * br - z_im * bi
    bb_im = z_re * bi + z_im * br
    bu_re = jnp.einsum('blgc,gpc->blgp', ug, bb_re)
    bu_im = jnp.einsum('blgc,gpc->blgp', ug, bb_im)
    a_re = jnp.broadcast_to(ab_re, (1, seq, SSM_GROUPS, SSM_STATE))
    a_im = jnp.broadcast_to(ab_im, (1, seq, SSM_GROUPS, SSM_STATE))

    def combine(e1, e2):
        a1r, a1i, b1r, b1i = e1
        a2r, a2i, b2r, b2i = e2
        return (a2r * a1r - a2i * a1i, a2r * a1i + a2i * a1r,
                a2r * b1r - a2i * b1i + b2r, a2r * b1i + a2i * b1r + b2i)

    ac_re, ac_im, s_re, s_im = lax.associative_scan(combine, (a_re, a_im, bu_re, bu_im), axis=1)
    h0r = h0_re.astype(f32)[:, None]
    h0i = h0_im.astype(f32)[:, None]
    s_re = ac_re * h0r - ac_im * h0i + s_re
    s_im = ac_re * h0i + ac_im * h0r + s_im
    y = (jnp.einsum('gcp,blgp->blgc', c_re.astype(f32), s_re)
         - jnp.einsum('gcp,blgp->blgc', c_im.astype(f32), s_im))
    y = y.reshape(bsz, seq, SSM_WIDTH) + d_skip.astype(f32) * uf
    z = jax.nn.gelu(y)
    out = z * jax.nn.sigmoid(z @ w_glu.astype(f32) + b_glu.astype(f32))
    return out.astype(u.dtype), s_re[:, -1].astype(h0_re.dtype), s_im[:, -1].astype(h0_im.dtype)

def memory_kv(mem, g, w_mk, w_mv):
    bsz, n_mem, _ = mem.shape
    mn = rmsnorm(mem, g)
    k = (mn @ w_mk).reshape(bsz, n_mem, MEM_HEADS, MEM_HEAD_DIM)
    v = (mn @ w_mv).reshape(bsz, n_mem, MEM_HEADS, MEM_HEAD_DIM)
    return k, v

def memory_attention(q, mk, mv):
    s = jnp.einsum('blhd,bmhd->bhlm', q, mk).astype(jnp.float32) * (MEM_HEAD_DIM ** -0.5)
    p = jax.nn.softmax(s, axis=-1).astype(mv.dtype)
    return jnp.einsum('bhlm,bmhd->blhd', p, mv)

def hier_moe(h, w_grp, b_grp, w_exp, b_exp, w1, w3, w2):
    n_tok, d = h.shape
    grp_logits = (h @ w_grp).astype(jnp.float32) + b_grp.astype(jnp.float32)
    grp_prob = jax.nn.softmax(grp_logits, axis=-1)
    grp = jnp.argmax(grp_logits, axis=-1)
    p_grp = jnp.take_along_axis(grp_prob, grp[:, None], axis=-1)
    exp_logits = ((h @ w_exp).astype(jnp.float32) + b_exp.astype(jnp.float32)).reshape(
        n_tok, MOE_GROUPS, EXPERTS_PER_GROUP)
    in_grp = jnp.take_along_axis(exp_logits, grp[:, None, None], axis=1)[:, 0]
    top_val, top_idx = lax.top_k(in_grp, TOP_K)
    gate = jax.nn.softmax(top_val, axis=-1) * p_grp
    expert = grp[:, None] * EXPERTS_PER_GROUP + top_idx
    n_pairs = n_tok * TOP_K
    e_flat = expert.reshape(n_pairs)
    tok = jnp.repeat(jnp.arange(n_tok), TOP_K)
    order = jnp.argsort(e_flat)
    e_s = e_flat[order]
    tok_s = tok[order]
    w_s = gate.reshape(n_pairs)[order]
    counts = jnp.bincount(e_flat, length=N_EXPERTS)
    starts = jnp.cumsum(counts) - counts
    padded = (counts + MOE_BLOCK - 1) // MOE_BLOCK * MOE_BLOCK
    pad_ends = jnp.cumsum(padded)
    pad_starts = pad_ends - padded
    dest = pad_starts[e_s] + jnp.arange(n_pairs) - starts[e_s]
    n_blocks = -(-n_pairs // MOE_BLOCK) + N_EXPERTS
    xp = jnp.zeros((n_blocks * MOE_BLOCK, d), h.dtype).at[dest].set(h[tok_s])
    block_expert = jnp.minimum(
        jnp.searchsorted(pad_ends, jnp.arange(n_blocks) * MOE_BLOCK, side='right'), N_EXPERTS - 1)

    def expert_block(args):
        xb, e = args
        return (jax.nn.silu(xb @ w1[e]) * (xb @ w3[e])) @ w2[e]

    yp = lax.map(expert_block, (xp.reshape(n_blocks, MOE_BLOCK, d), block_expert))
    ys = yp.reshape(n_blocks * MOE_BLOCK, d)[dest] * w_s[:, None].astype(h.dtype)
    return jax.ops.segment_sum(ys, tok_s, num_segments=n_tok)

def decoder_layer(x, mem_k, mem_v, k_bufs, v_bufs, h0_re, h0_im, lw):
    bsz, seq, _ = x.shape
    xn = rmsnorm(x, lw['norm1'])
    proj = xn @ lw['w_in']
    slopes = alibi_slopes()
    outs, lses, new_k, new_v = [], [], [], []
    for gi, (window, dilation) in enumerate(ATT_GROUPS):
        c0 = gi * QKV_GROUP
        q = proj[..., c0:c0 + ATT_OUT].reshape(bsz, seq, HEADS_PER_GROUP, HEAD_DIM)
        k = proj[..., c0 + ATT_OUT:c0 + 2 * ATT_OUT].reshape(bsz, seq, HEADS_PER_GROUP, HEAD_DIM)
        v = proj[..., c0 + 2 * ATT_OUT:c0 + QKV_GROUP].reshape(bsz, seq, HEADS_PER_GROUP, HEAD_DIM)
        k_ext = jnp.concatenate([k_bufs[gi], k], axis=1)
        v_ext = jnp.concatenate([v_bufs[gi], v], axis=1)
        o, lse = dilated_attention(q, k_ext, v_ext, k_bufs[gi].shape[1], dilation, window // dilation + 1,
                                   slopes[gi * HEADS_PER_GROUP:(gi + 1) * HEADS_PER_GROUP])
        outs.append(o)
        lses.append(lse)
        n_ext = k_ext.shape[1]
        keep = min(window, n_ext)
        new_k.append(k_ext[:, n_ext - keep:])
        new_v.append(v_ext[:, n_ext - keep:])
    grp_w = jax.nn.softmax(jnp.stack(lses, axis=0), axis=0).astype(x.dtype)
    att = jnp.sum(grp_w[..., None] * jnp.stack(outs, axis=0), axis=0).reshape(bsz, seq, ATT_OUT)
    ssm, h_re, h_im = s5_branch(proj[..., SSM_COL:MEMQ_COL], h0_re, h0_im, lw['lam_re'], lw['lam_im'],
                                lw['log_dt'], lw['ssm_b_re'], lw['ssm_b_im'], lw['ssm_c_re'], lw['ssm_c_im'],
                                lw['ssm_d'], lw['w_glu'], lw['b_glu'])
    mq = proj[..., MEMQ_COL:GATE_COL].reshape(bsz, seq, MEM_HEADS, MEM_HEAD_DIM)
    mem = memory_attention(mq, mem_k, mem_v).reshape(bsz, seq, MEM_WIDTH)
    gates = jax.nn.sigmoid(proj[..., GATE_COL:].astype(jnp.float32)).astype(x.dtype).reshape(
        bsz, seq, N_BRANCHES, D_MODEL)
    merged = (gates[:, :, 0] * (att @ lw['w_att_out'])
              + gates[:, :, 1] * (ssm @ lw['w_ssm_out'])
              + gates[:, :, 2] * (mem @ lw['w_mem_out']))
    h = x + merged @ lw['w_o']
    hn = rmsnorm(h, lw['norm2']).reshape(bsz * seq, D_MODEL)
    h = h + hier_moe(hn, lw['w_grp'], lw['b_grp'], lw['w_exp'], lw['b_exp'],
                     lw['w1'], lw['w3'], lw['w2']).reshape(bsz, seq, D_MODEL)
    return h, tuple(new_k), tuple(new_v), h_re, h_im

def setup_inputs(seed: int = 0) -> dict:
    key = jax.random.key(seed)
    ks = iter(jax.random.split(key, 64))
    f32 = jnp.float32

    def nrm(shape, scale):
        return jax.random.normal(next(ks), shape, f32) * scale

    def gain(shape):
        return 1.0 + nrm(shape, 0.02)

    inp = {}
    inp['x_prompt'] = nrm((BATCH, SEQ, D_MODEL), 1.0)
    inp['x_sample'] = nrm((DEC_BATCH, DEC_SEQ, D_MODEL), 1.0)
    for g, (window, _) in enumerate(ATT_GROUPS):
        buf = min(window, PAST_LEN)
        inp[f'cache_swa{g}_k'] = nrm((DEPTH, DEC_BATCH, buf, HEADS_PER_GROUP, HEAD_DIM), 1.0)
        inp[f'cache_swa{g}_v'] = nrm((DEPTH, DEC_BATCH, buf, HEADS_PER_GROUP, HEAD_DIM), 1.0)
    inp['cache_mem_k'] = nrm((DEPTH, DEC_BATCH, MEM_TOKENS, MEM_HEADS, MEM_HEAD_DIM), 1.0)
    inp['cache_mem_v'] = nrm((DEPTH, DEC_BATCH, MEM_TOKENS, MEM_HEADS, MEM_HEAD_DIM), 1.0)
    inp['state_ssm_re'] = nrm((DEPTH, DEC_BATCH, SSM_GROUPS, SSM_STATE), 1.0)
    inp['state_ssm_im'] = nrm((DEPTH, DEC_BATCH, SSM_GROUPS, SSM_STATE), 1.0)
    inp['mem_prompt'] = nrm((BATCH, MEM_TOKENS, D_MODEL), 1.0)
    inp['norm1'] = gain((DEPTH, D_MODEL))
    inp['w_in'] = nrm((DEPTH, D_MODEL, IN_COLS), D_MODEL ** -0.5)
    inp['lam_re'] = -0.5 + nrm((DEPTH, SSM_GROUPS, SSM_STATE), 0.01)
    inp['lam_im'] = jnp.pi * jnp.arange(SSM_STATE, dtype=f32) + nrm((DEPTH, SSM_GROUPS, SSM_STATE), 0.01)
    inp['log_dt'] = jax.random.uniform(next(ks), (DEPTH, SSM_GROUPS), f32, math.log(DT_MIN), math.log(DT_MAX))
    inp['ssm_b_re'] = nrm((DEPTH, SSM_GROUPS, SSM_STATE, SSM_GROUP_CH), (2 * SSM_GROUP_CH) ** -0.5)
    inp['ssm_b_im'] = nrm((DEPTH, SSM_GROUPS, SSM_STATE, SSM_GROUP_CH), (2 * SSM_GROUP_CH) ** -0.5)
    inp['ssm_c_re'] = nrm((DEPTH, SSM_GROUPS, SSM_GROUP_CH, SSM_STATE), SSM_STATE ** -0.5)
    inp['ssm_c_im'] = nrm((DEPTH, SSM_GROUPS, SSM_GROUP_CH, SSM_STATE), SSM_STATE ** -0.5)
    inp['ssm_d'] = nrm((DEPTH, SSM_WIDTH), 0.5)
    inp['w_glu'] = nrm((DEPTH, SSM_WIDTH, SSM_WIDTH), SSM_WIDTH ** -0.5)
    inp['b_glu'] = nrm((DEPTH, SSM_WIDTH), 0.01)
    inp['w_att_out'] = nrm((DEPTH, ATT_OUT, D_MODEL), ATT_OUT ** -0.5)
    inp['w_ssm_out'] = nrm((DEPTH, SSM_WIDTH, D_MODEL), SSM_WIDTH ** -0.5)
    inp['w_mem_out'] = nrm((DEPTH, MEM_WIDTH, D_MODEL), MEM_WIDTH ** -0.5)
    inp['w_o'] = nrm((DEPTH, D_MODEL, D_MODEL), D_MODEL ** -0.5)
    inp['norm_mem'] = gain((DEPTH, D_MODEL))
    inp['w_mk'] = nrm((DEPTH, D_MODEL, MEM_WIDTH), D_MODEL ** -0.5)
    inp['w_mv'] = nrm((DEPTH, D_MODEL, MEM_WIDTH), D_MODEL ** -0.5)
    inp['norm2'] = gain((DEPTH, D_MODEL))
    inp['w_grp'] = nrm((DEPTH, D_MODEL, MOE_GROUPS), D_MODEL ** -0.5)
    inp['b_grp'] = nrm((DEPTH, MOE_GROUPS), 0.01)
    inp['w_exp'] = nrm((DEPTH, D_MODEL, N_EXPERTS), D_MODEL ** -0.5)
    inp['b_exp'] = nrm((DEPTH, N_EXPERTS), 0.01)
    inp['w1'] = nrm((DEPTH, N_EXPERTS, D_MODEL, D_EXPERT), D_MODEL ** -0.5)
    inp['w3'] = nrm((DEPTH, N_EXPERTS, D_MODEL, D_EXPERT), D_MODEL ** -0.5)
    inp['w2'] = nrm((DEPTH, N_EXPERTS, D_EXPERT, D_MODEL), D_EXPERT ** -0.5)
    inp['norm_f'] = gain((D_MODEL,))
    return inp

def reference(x_prompt, x_sample, cache_swa0_k, cache_swa0_v, cache_swa1_k, cache_swa1_v,
              cache_swa2_k, cache_swa2_v, cache_mem_k, cache_mem_v, state_ssm_re, state_ssm_im,
              mem_prompt, norm1, w_in, lam_re, lam_im, log_dt, ssm_b_re, ssm_b_im, ssm_c_re, ssm_c_im,
              ssm_d, w_glu, b_glu, w_att_out, w_ssm_out, w_mem_out, w_o, norm_mem, w_mk, w_mv,
              norm2, w_grp, b_grp, w_exp, b_exp, w1, w3, w2, norm_f):
    cache_k = (cache_swa0_k, cache_swa1_k, cache_swa2_k)
    cache_v = (cache_swa0_v, cache_swa1_v, cache_swa2_v)
    hp = x_prompt
    hs = x_sample
    pk = [[] for _ in ATT_GROUPS]
    pv = [[] for _ in ATT_GROUPS]
    sk = [[] for _ in ATT_GROUPS]
    sv = [[] for _ in ATT_GROUPS]
    p_mk, p_mv, p_re, p_im, s_re, s_im = [], [], [], [], [], []
    for l in range(DEPTH):
        lw = dict(norm1=norm1[l], w_in=w_in[l], lam_re=lam_re[l], lam_im=lam_im[l], log_dt=log_dt[l],
                  ssm_b_re=ssm_b_re[l], ssm_b_im=ssm_b_im[l], ssm_c_re=ssm_c_re[l], ssm_c_im=ssm_c_im[l],
                  ssm_d=ssm_d[l], w_glu=w_glu[l], b_glu=b_glu[l], w_att_out=w_att_out[l],
                  w_ssm_out=w_ssm_out[l], w_mem_out=w_mem_out[l], w_o=w_o[l], norm2=norm2[l],
                  w_grp=w_grp[l], b_grp=b_grp[l], w_exp=w_exp[l], b_exp=b_exp[l],
                  w1=w1[l], w3=w3[l], w2=w2[l])
        mk, mv = memory_kv(mem_prompt, norm_mem[l], w_mk[l], w_mv[l])
        empty = jnp.zeros((hp.shape[0], 0, HEADS_PER_GROUP, HEAD_DIM), hp.dtype)
        h0 = jnp.zeros((hp.shape[0], SSM_GROUPS, SSM_STATE), hp.dtype)
        hp, kp, vp, hr, hi = decoder_layer(hp, mk, mv, (empty, empty, empty), (empty, empty, empty), h0, h0, lw)
        hs, ks_, vs_, sr, si = decoder_layer(hs, cache_mem_k[l], cache_mem_v[l],
                                             (cache_k[0][l], cache_k[1][l], cache_k[2][l]),
                                             (cache_v[0][l], cache_v[1][l], cache_v[2][l]),
                                             state_ssm_re[l], state_ssm_im[l], lw)
        for g in range(N_ATT_GROUPS):
            pk[g].append(kp[g])
            pv[g].append(vp[g])
            sk[g].append(ks_[g])
            sv[g].append(vs_[g])
        p_mk.append(mk)
        p_mv.append(mv)
        p_re.append(hr)
        p_im.append(hi)
        s_re.append(sr)
        s_im.append(si)
    y_prompt = rmsnorm(hp, norm_f)
    y_sample = rmsnorm(hs, norm_f)
    st = jnp.stack
    return (y_prompt, y_sample,
            st(pk[0]), st(pv[0]), st(pk[1]), st(pv[1]), st(pk[2]), st(pv[2]),
            st(p_mk), st(p_mv), st(p_re), st(p_im),
            st(sk[0]), st(sv[0]), st(sk[1]), st(sv[1]), st(sk[2]), st(sv[2]),
            st(s_re), st(s_im))


_drawn_inputs = setup_inputs


def setup_inputs(seed=0):
    import zlib

    import numpy as np

    out = dict(_drawn_inputs(seed))
    spreads = {}
    factors = {'lam_re': 16.777, 'b_glu': 39.822, 'norm_mem': 2.931, 'b_grp': 4.506, 'b_exp': 5.936}
    for name, (base, spread) in spreads.items():
        noise = np.random.default_rng([zlib.crc32(name.encode()), seed]).standard_normal(out[name].shape)
        drawn = base * np.exp(spread * noise) if base else spread * noise
        out[name] = __import__('jax').numpy.asarray(drawn.astype(out[name].dtype))
    for name, factor in factors.items():
        out[name] = (out[name] * factor).astype(out[name].dtype)
    return out
```

```python
from contextlib import ExitStack

import concourse.bass as bass
import numpy as np
from concourse import mybir

F32 = mybir.dt.float32
U32 = mybir.dt.uint32
I32 = mybir.dt.int32
ALU = mybir.AluOpType
ACT = mybir.ActivationFunctionType
AX = mybir.AxisListType.X

P = 128
D = 1024
KT = D // P
SEQ, NB = 512, 8
TOK = SEQ + NB
HALF = TOK // 2
NCLS = 4
WINDOWS = (128, 512, 2048)
DILS = (1, 4, 16)
NG, NH, DH = 3, 4, 64
ATT = NH * DH
SSMW, SG, SCH, SST = 512, 32, 16, 64
NJ = SG * SST // P
CH = 8
NCH = SEQ // CH
YC = NCH + NB
XC = YC + NB
LEVELS = 6
MEM, MH, MD = 256, 4, 128
NE, NGRP, EPG, FE = 32, 4, 8, 512
FT = FE // P
CAP = 64
MAXP = -(-TOK // CAP)
NT = 5
ROWS = (P, P, P, P, NB)
EPS = 1e-6
BIG = 1e30
ATT_SCALE = DH ** -0.5
MEM_SCALE = MD ** -0.5
TWO_PI = 2 * np.pi
ROUND = 1.5 * 2.0 ** 23
PI_A = 6.28125
PI_B = float(np.float32(np.floor((TWO_PI - PI_A) * 2 ** 22) / 2 ** 22))
PI_C = float(np.float32(TWO_PI - PI_A - PI_B))

T_QKV, T_MQ = 4, 22
N_PROJ, N_MEMT, N_GATE = 26, 8, 24
N_FIRST = N_PROJ + N_MEMT

KB = 256
XN = 13
PROJ = 30
RING = 83
S5 = 91
MK = 187
TOTAL_KB = 207
WBUF = (S5 + 48, S5)

CONSTS = (("ident", P), ("triu", P), ("ones", P), ("smask", CH), ("esel", NB), ("rev4", NGRP),
          ("rev32", NE), ("yrow", NE), ("slot", CAP), ("tokid", NT), ("valid", NT),
          ("passes", MAXP), ("decbias", NG * P), ("eps", 1))
NCONST = sum(n for _, n in CONSTS)


def slope(h):
    return float(2.0 ** (-8.0 * (h + 1) / (NG * NH)))


def wait_from(eng, s, n):
    if n > 0:
        eng.wait_ge(s, n)


def build(nc, t):
    with ExitStack() as ctx:
        arena = ctx.enter_context(nc.sbuf_tensor("arena", [P, TOTAL_KB * KB], F32))
        bank = ctx.enter_context(nc.psum_tensor("bank", [P, 8, 512], F32))
        gather_rows = ctx.enter_context(nc.sbuf_tensor("gather_rows", [CAP, NE], U32))
        gather_cur = ctx.enter_context(nc.sbuf_tensor("gather_cur", [CAP, 2], U32))
        y_rows = ctx.enter_context(nc.sbuf_tensor("y_rows", [P, 2, NT], U32))
        n_pass = ctx.enter_context(nc.sbuf_tensor("n_pass", [1, 1], I32))

        def sem(name):
            return ctx.enter_context(nc.semaphore(name))

        def view(lo, dims):
            n = int(np.prod(dims))
            assert lo + n <= TOTAL_KB * KB, (lo, dims)
            v = arena[:, lo:lo + n]
            if len(dims) > 1:
                names = "abcd"[:len(dims)]
                v = v.rearrange(f"p ({' '.join(names)}) -> p {' '.join(names)}",
                                **dict(zip(names, dims)))
            return v

        def at(kb, *dims):
            return view(int(round(kb * KB)), dims)

        top = [0]

        def keep(*dims):
            v = view(top[0], dims)
            top[0] += int(np.prod(dims))
            assert top[0] <= XN * KB
            return v

        cst = keep(NCONST)
        c, o = {}, 0
        for name, n in CONSTS:
            c[name] = cst[:, o:o + n]
            o += n
        ident, ones, eps_ap = c["ident"], c["ones"], c["eps"]
        dist12 = keep(2 * P)
        ssm_in = keep(3, NJ)
        par = keep(24, NJ)
        dec_cols = keep(N_PROJ, NB)
        stat = keep(64)
        gain1, gain_mem = keep(KT), keep(KT)
        ssm_d, b_glu = keep(4), keep(4)
        apow = keep(2, LEVELS, NJ)
        st_prompt = keep(2, NJ)
        st_dec = keep(2, NJ, NB)
        h0 = keep(2, NJ, NB)
        w_route = keep(KT, NGRP + NE)
        b_route = keep(NGRP + NE)

        xn = at(XN, KT, TOK)
        proj = at(PROJ, N_PROJ, TOK)
        ring = [at(RING, KT, P), at(RING + 4, KT, P)]
        cw = at(S5, 2, NJ, CH + 1, SCH)
        state_in = at(S5 + 18, 2, NJ, P)
        toep = at(S5 + 34, 2, NJ, P)
        ctmp = [at(S5 + 34, NJ * (CH + 1) * SCH), at(S5 + 43, NJ * (CH + 1) * SCH)]
        ba = at(S5 + 52, 2, NJ, CH, SCH)
        brep = at(S5 + 68, 2, NJ, CH, SCH)
        kern = at(S5 + 52, 2, NJ, P)
        b_in, c_in = at(S5 + 84, 2, NJ, SCH), at(S5 + 86, 2, NJ, SCH)
        bbar = at(S5 + 88, 2, NJ, SCH)
        pw = at(S5 + 90, 2, NJ, CH + 1)
        rpw = at(S5 + 91.25, 2, NJ, CH)
        ucomb = at(S5 + 68, 4, CH, XC)
        utok = at(S5 + 78, SG, CH, SCH)
        uch = at(S5 + 52, SG, XC)
        xst = at(S5 + 68, 2, NJ, XC)
        stmp = [at(S5 + 78 + 4 * i, NJ * (NCH - 1)) for i in range(4)]
        sprev = at(S5 + 18, 2, NJ, YC)
        ytok = at(S5 + 78, CH, SSMW)
        ycol = at(S5 + 68, 4, TOK)
        zcol = at(S5, 4, TOK)
        glu = at(S5 + 9, 4, TOK)
        w_glu = at(MK, 4, SSMW)
        sq, sqm = at(S5 + 34, KT, TOK), at(S5 + 52, KT, MEM)
        rms, rmsm = at(S5 + 60, TOK), at(S5 + 63, MEM)
        memn = at(MK, KT, MEM)
        mkv = at(MK + 8, 2 * MH, MEM)
        mk_rows = at(MK + 12, 2, MH * MD)
        mv_rows = at(MK + 16, 2, MH * MD)
        gates = at(S5, N_GATE, TOK)
        v_rows = at(S5 + 49, NG, NCLS, ATT)
        attT = at(S5 + 61, 2, TOK)
        memT = at(S5 + 65.25, MH, TOK)
        ssmT = at(S5 + 73.5, 4, TOK)
        k_rows = [at(S5 + 82, NCLS, ATT), at(S5 + 86, NCLS, ATT)]
        kv_dec = at(S5 + 90, NG, 2, ATT)
        dist0 = at(PROJ, NCLS, SEQ)
        work = S5 + 82
        sc = at(work, 6 * P)
        pr = at(work + 3, 6 * P)
        prT = at(MK, 6 * P)
        pm = [at(work, MEM), at(work + 1, MEM)]
        pmT = [at(MK + 4, MEM), at(MK + 5, MEM)]
        slot_k = [at(PROJ + 40, NG, 2, P), at(PROJ + 47, NG, 2, P)]
        slot_mk = [at(PROJ + 43, MH, MEM), at(PROJ + 50, MH, MEM)]
        slot_v = [at(PROJ + 40, NG, ATT), at(PROJ + 47, NG, ATT)]
        slot_mv = [at(PROJ + 43, 2, MH * MD), at(PROJ + 50, 2, MH * MD)]
        newprod = at(work, NG, 2, NB)
        ds_k = at(work + 0.25, NG, 64)
        ds_m = at(work + 1, 2, MH * NB)
        dsc = at(work + 1.25, NG, P + 1)
        dpd = at(work + 3, NG, 64)
        dpn = at(work + 3.75, NG, 64)
        dpT = at(work + 4.5, NG, 64)
        dm = at(work + 5.25, MEM)
        dmT = at(work + 6.25, 2, MH * NB)
        zero = at(work + 6.5, P)
        w_att, w_ssm, w_mem = at(PROJ, 2, D), at(PROJ + 8, 4, D), at(PROJ + 24, 4, D)
        w_o = [at(XN, 4, D), at(MK, 4, D)]
        x_rows = at(PROJ + 40, NT, D)
        h_rows = at(PROJ, NT, D)
        hn_rows = at(PROJ + 20, NT, D)
        gain2 = at(MK + 16, D)
        gain_f = at(XN + 12, D)
        hnT = [at(XN, KT, P), at(XN + 4, KT, P)]
        rtop = [0]

        def rt(*dims):
            v = view((PROJ + 40) * KB + rtop[0], dims)
            rtop[0] += int(np.prod(dims))
            assert rtop[0] <= 12 * KB
            return v

        lg = rt(NT, NGRP + NE)
        r5 = [rt(NT) for _ in range(12)]
        og, eq4, ex4 = rt(NT, NGRP), rt(NT, NGRP), rt(NT, NGRP)
        el, eq32, tmp32, rank = (rt(NT, NE) for _ in range(4))
        m12 = [rt(NT, NE), rt(NT, NE)]
        mtok = [rt(NT, NE), rt(NT, NE)]
        chosen, count, over = rt(NT, NE), rt(NE), rt(MAXP)
        slotk = [rt(NT), rt(NT)]
        gatek = [rt(NT), rt(NT)]
        row0 = [rt(NT), rt(NT)]
        inpass = [rt(NT), rt(NT)]
        gate_now = [rt(NT), rt(NT)]
        row_now = [rt(NT), rt(NT)]
        hot = [rt(NT, CAP), rt(NT, CAP)]
        wb = [(at(b, KT, FE), at(b + 16, KT, FE), at(b + 32, FT, D)) for b in WBUF]
        xg = [at(MK, D), at(MK + 4, D)]
        xgT = [at(MK + 8, KT, CAP), at(MK + 10, KT, CAP)]
        hT = [at(MK + 12, FT, CAP), at(MK + 13, FT, CAP)]
        sg = [at(MK + 14, FT, CAP), at(MK + 15, FT, CAP)]
        y_sb = [at(XN, D), at(XN + 4, D)]
        yk = [[at(PROJ + 20 + 8 * b + 4 * k, D) for k in range(2)] for b in range(2)]
        fin = [at(PROJ + 52 + 4 * b, D) for b in range(2)]

        names = ("cst", "ssmp", "x", "mem", "win0", "win1", "small", "wglu", "dist0", "kdec0", "kdec1",
                 "vdec0", "vdec1", "wout", "wo", "xr", "gain2", "gainf", "dt", "lrdt", "trig", "sq", "ss",
                 "rms", "xn", "mn", "tile", "evac", "vchain", "achain", "cplx", "job", "jobfree", "toep",
                 "ucomb", "sprev", "states", "yadd", "z", "ssm", "krows", "kout", "krest", "out", "S", "T", "nmax",
                 "exp", "pn", "PT", "ptc", "O", "oc", "gevac", "mS", "mnmax", "mexp", "mpn", "mPT", "mptc",
                 "mO", "moc", "dprod", "dkdone", "dcopy", "drow", "dnmax", "dexp", "dpd", "dback", "dbackc",
                 "dvdone", "doc", "Pj", "Pfree", "merged", "wo_mm", "h", "hss", "hrms", "hn", "hnout", "ht",
                 "hnT", "lg", "gmax", "gexp", "chosen", "rank", "rtab", "npass", "hot", "idxmm", "idx", "xg0",
                 "xg1", "cur", "xt", "xc", "gu", "sg", "hT", "y", "yc", "yo0", "yo1", "w13_0", "w13_1", "w2_0",
                 "w2_1", "yk0", "yk1", "fsum", "fadd", "yrow", "fss", "frms", "fin", "fout0", "fout1")
        s = {n: sem("s_" + n) for n in names + ("held",)}

        block = ctx.enter_context(nc.Block())

        class Jobs:
            def __init__(self):
                self.n = 0

            def take_pe(self, pe):
                wait_from(pe, s["jobfree"], self.n - 3)
                self.n += 1
                return bank[:, 4 + (self.n - 1) % 4, :]

            def take_act(self, act):
                act.wait_ge(s["job"], self.n + 1)
                self.n += 1
                return bank[:, 4 + (self.n - 1) % 4, :]

        J_ST = NJ * 2 // 4
        J_K = SG // 4
        J_UC = 4 * CH // 4
        J_U = -(-SG // 6)
        J_X = 2 * 3
        J_Y = SG // 4
        J_YT = 4 * 2
        J_GLU = 4 * 2
        E_ST = J_ST
        E_K = E_ST + J_K
        E_UC = E_K + J_UC
        E_U = E_UC + J_U
        E_X = E_U + J_X
        E_Y = E_X + J_Y
        E_YT = E_Y + J_YT
        E_GLU = E_YT + J_GLU
        J_KV = NG * 2 * NCLS
        E_KV = E_GLU + J_KV
        E_KVD = E_KV + NG
        E_MEM = E_KVD + 4
        KV = [(g, kv, r) for g in range(NG) for kv in (0, 1) for r in range(NCLS)]

        @block.sync
        def _(sp):
            sp.dma_start(ssm_in, t["ssm_in"]).then_inc(s["ssmp"], 16)
            sp.dma_start(xn, t["xT"]).then_inc(s["x"], 16)
            sp.dma_start(cst, t["consts"]).then_inc(s["cst"], 16)
            with sp.Fori(0, (N_FIRST + N_GATE) // 2) as i2:
                for u in range(2):
                    sp.wait_ge(s["tile"], i2 * 2 + (u + 1))
                    sp.dma_start(ring[u], t["w_stream"][bass.ds(i2 * 2 + u, 1)].rearrange(
                        "o p k c -> (o p) k c")).then_inc(s[f"win{u}"], 16)
            sp.wait_ge(s["moc"], 4 * MH)
            for b in range(2):
                sp.dma_start(slot_k[b], t["k_dec"][b]).then_inc(s[f"kdec{b}"], 16)
                sp.dma_start(slot_mk[b], t["mk_dec"][b]).then_inc(s[f"kdec{b}"], 16)
            sp.dma_start(w_att, t["w_att"]).then_inc(s["wout"], 16)
            for b in range(2, NB):
                sp.wait_ge(s["dkdone"], b - 1)
                sp.dma_start(slot_k[b % 2], t["k_dec"][b]).then_inc(s[f"kdec{b % 2}"], 16)
                sp.dma_start(slot_mk[b % 2], t["mk_dec"][b]).then_inc(s[f"kdec{b % 2}"], 16)
            sp.dma_start(w_ssm, t["w_ssm"]).then_inc(s["wout"], 16)
            sp.dma_start(w_mem, t["w_mem"]).then_inc(s["wout"], 16)
            for b in range(NB):
                if b < 2:
                    sp.wait_ge(s["dkdone"], NB - 1 + b)
                else:
                    sp.wait_ge(s["dvdone"], b - 1)
                for g in range(NG):
                    rows = t[f"cache_swa{g}_v"][b].rearrange("(m q) c -> m q c", q=DILS[g])[:, 0, :]
                    sp.dma_start(slot_v[b % 2][:, g, :], rows).then_inc(s[f"vdec{b % 2}"], 16)
                sp.dma_start(slot_mv[b % 2], t["cache_mem_v"][b].rearrange("(k p) c -> p k c", p=P)
                             ).then_inc(s[f"vdec{b % 2}"], 16)
            sp.dma_start(w_o[0], t["w_o"][:, 0:4, :]).then_inc(s["wo"], 16)
            sp.wait_ge(s["krest"], 16 * (2 * NG + 2))
            sp.dma_start(w_o[1], t["w_o"][:, 4:8, :]).then_inc(s["wo"], 16)
            sp.wait_ge(s["dvdone"], NB)
            for T in range(4):
                sp.dma_start(x_rows[:, T, :], t["x_prompt"].rearrange("(a r) c -> r a c", r=NCLS)[T]
                             ).then_inc(s["xr"], 16)
            sp.dma_start(x_rows[0:NB, 4, :], t["x_sample"]).then_inc(s["xr"], 16)
            sp.dma_start(gain2, t["norm2"].partition_broadcast(P)).then_inc(s["gain2"], 16)
            sp.wait_ge(s["wo_mm"], NT)
            sp.dma_start(gain_f, t["norm_f"].partition_broadcast(P)).then_inc(s["gainf"], 16)
            for T in range(NT):
                sp.wait_ge(s["hn"], T + 1)
                sp.dma_start(t["hn_dram"][T * P:T * P + ROWS[T], :], hn_rows[0:ROWS[T], T, :]
                             ).then_inc(s["hnout"], 16)
            sp.wait_ge(s["npass"], 1)
            n_p = sp.value_load(n_pass[0:1, 0:1], min_val=1, max_val=MAXP)
            with sp.Fori(0, n_p) as p:
                with sp.Fori(0, NE // 2) as e2:
                    for u in range(2):
                        w1, w3, w2 = wb[u]
                        e = e2 * 2 + u
                        for w, name in ((w1, "w1"), (w3, "w3")):
                            if name == "w1":
                                sp.wait_ge(s["gu"], p * NE + e2 * 2 + (u + 1))
                            sp.dma_start(w, t[name][bass.ds(e, 1)].rearrange(
                                "o (k p) f -> p (o k) f", p=P)).then_inc(s[f"w13_{u}"], 16)
                        sp.wait_ge(s["y"], p * NE + e2 * 2 + (u + 1))
                        sp.dma_start(w2, t["w2"][bass.ds(e, 1)].rearrange(
                            "o (f p) d -> p (o f) d", p=P)).then_inc(s[f"w2_{u}"], 16)
            for T in range(NT):
                sp.wait_ge(s["fin"], T + 1)
                if T < 4:
                    sp.dma_start(t["y_prompt"].rearrange("(a r) c -> r a c", r=NCLS)[T], fin[T % 2]
                                 ).then_inc(s[f"fout{T % 2}"], 16)
                else:
                    sp.dma_start(t["y_sample"], fin[T % 2][0:NB, :]).then_inc(s[f"fout{T % 2}"], 16)
            sp.wait_ge(s["fout0"], 3 * 16)
            sp.wait_ge(s["fout1"], 2 * 16)

        @block.gpsimd
        def _(pool):
            for dst, name in ((b_in, "b_in"), (c_in, "c_in"), (h0, "h0")):
                pool.dma_start(dst, t[name]).then_inc(s["small"], 16)
            pool.dma_start(memn, t["memT"]).then_inc(s["mem"], 16)
            for dst, name in ((gain1, "gain1"), (gain_mem, "gain_mem"), (ssm_d, "ssm_d"), (b_glu, "b_glu"),
                              (dist12, "dist12"), (w_route, "w_route")):
                pool.dma_start(dst, t[name]).then_inc(s["small"], 16)
            pool.dma_start(b_route, t["b_route"].partition_broadcast(P)).then_inc(s["small"], 16)

            pool.wait_ge(s["tile"], 2 + 2)
            with pool.Fori(0, NB) as b:
                for g in range(NG):
                    n = (WINDOWS[g] - 1) * ATT
                    for kv in "kv":
                        src = t[f"cache_swa{g}_{kv}"][bass.ds(b, 1)].rearrange("o m c -> o (m c)")
                        dst = t[f"sample_swa{g}_{kv}"][bass.ds(b, 1)].rearrange("o m c -> o (m c)")
                        pool.dma_start(dst[:, 0:n].rearrange("o (q x) -> (o q) x", q=16),
                                       src[:, ATT:ATT + n].rearrange("o (q x) -> (o q) x", q=16)
                                       ).then_inc(s["out"], 16)

            pool.wait_ge(s["job"], E_K)
            pool.memset(ucomb, 0.0).then_inc(s["ucomb"], 1)
            pool.wait_ge(s["evac"], N_PROJ + 2)
            pool.wait_ge(s["ucomb"], 1)
            for k in range(CH):
                lo = (k % NCLS) * P + k // NCLS
                pool.tensor_copy(ucomb[:, :, k, 0:NCH], proj[:, 0:4, lo:lo + P - 1:2]).then_inc(s["ucomb"], 1)
            pool.tensor_copy(ucomb[:, :, 0, NCH:YC], proj[:, 0:4, SEQ:TOK]).then_inc(s["ucomb"], 1)
            pool.tensor_copy(ucomb[:, :, CH - 1, YC:XC], proj[:, 0:4, SEQ:TOK]).then_inc(s["ucomb"], 1)

            pool.wait_ge(s["tile"], 2 + N_FIRST)
            pool.dma_start(w_glu, t["w_glu"]).then_inc(s["wglu"], 16)
            pool.wait_ge(s["states"], 3)
            pool.dma_start(t["st_prompt"], st_prompt).then_inc(s["out"], 16)
            pool.dma_start(t["st_dec"], st_dec).then_inc(s["out"], 16)
            pool.wait_ge(s["yadd"], 4)
            pool.dma_start(dist0, t["dist0"]).then_inc(s["dist0"], 16)
            for g in range(NG):
                for kv, name in ((0, "k"), (1, "v")):
                    pool.wait_ge(s["krows"], 2 * g + kv + 1)
                    src = k_rows[g % 2] if kv == 0 else v_rows[:, g]
                    keep_rows = min(WINDOWS[g], SEQ)
                    a0 = (SEQ - keep_rows) // NCLS
                    pool.dma_start(t[f"prompt_swa{g}_{name}"].rearrange("(a r) c -> a r c", r=NCLS),
                                   src[a0:P]).then_inc(s["kout"], 16)
            pool.wait_ge(s["krows"], 2 * NG + 1)
            for g in range(NG):
                for kv, name in ((0, "k"), (1, "v")):
                    pool.dma_start(t[f"sample_swa{g}_{name}"][:, WINDOWS[g] - 1, :], kv_dec[0:NB, g, kv, :]
                                   ).then_inc(s["krest"], 16)
            pool.wait_ge(s["krows"], 2 * NG + 2)
            pool.dma_start(t["prompt_mem_v"].rearrange("(k p) c -> p k c", p=P), mv_rows).then_inc(s["krest"], 16)
            pool.wait_ge(s["krows"], 2 * NG + 3)
            pool.dma_start(t["prompt_mem_k"].rearrange("(k p) c -> p k c", p=P), mk_rows).then_inc(s["krest"], 16)

            pool.wait_ge(s["hnout"], 16 * NT)
            pool.wait_ge(s["npass"], 1)
            n_p = pool.value_load(n_pass[0:1, 0:1], min_val=1, max_val=MAXP)
            with pool.Fori(0, n_p) as p:
                pool.wait_ge(s["idx"], p + 1)
                pool.sem_inc(s["held"], 1)
                with pool.Fori(0, NE // 2) as e2:
                    for u in range(2):
                        pool.wait_ge(s["xt"], p * NE + e2 * 2 + (u + 1))
                        pool.tensor_copy(gather_cur[:, u:u + 1], gather_rows[:, bass.ds(e2 * 2 + u, 1)]
                                         ).then_inc(s["cur"], 1)
                        pool.wait_ge(s["cur"], p * NE + e2 * 2 + (u + 1))
                        pool.sem_inc(s["held"], 1)
                        pool.indirect_dma_start(
                            out=xg[u][0:CAP, :], out_offset=None, in_=t["hn_dram"],
                            in_offset=bass.IndirectOffsetOnAxis(ap=gather_cur[:, u:u + 1], axis=0)
                        ).then_inc(s[f"xg{u}"], 16)
                for u in range(2):
                    pool.wait_ge(s[f"yo{u}"], p * (16 * NE // 2) + (16 * NE // 2 + 16))
                pool.wait_ge(s["yrow"], p * 2 + 2)
                for T in range(NT):
                    pool.wait_ge(s["fsum"], p * NT + (NT + T - 1 if T >= 2 else NT))
                    pool.sem_inc(s["held"], 1)
                    for k in range(2):
                        pool.indirect_dma_start(
                            out=yk[T % 2][k][0:ROWS[T], :], out_offset=None, in_=t["y_dram"],
                            in_offset=bass.IndirectOffsetOnAxis(ap=y_rows[0:ROWS[T], k, T:T + 1], axis=0)
                        ).then_inc(s[f"yk{T % 2}"], 16)
            pool.wait_ge(s["kout"], 16 * (2 * NG))
            pool.wait_ge(s["krest"], 16 * (2 * NG + 2))
            pool.wait_ge(s["out"], 16 * (2 + 2 * NG * NB))

        @block.tensor
        def _(pe):
            pe.sem_inc(s["tile"], 2)
            pe.sem_inc(s["gu"], 2)
            pe.sem_inc(s["y"], 2)
            pe.sem_inc(s["xt"], 2)

            pe.wait_ge(s["cst"], 16)
            for k in range(KT):
                pe.wait_ge(s["sq"], k + 1)
                for h in range(2):
                    last = pe.matmul(bank[:, h, 0:HALF], ones, sq[:, k, h * HALF:(h + 1) * HALF],
                                     start=k == 0, stop=k == KT - 1)
            last.then_inc(s["ss"], 1)
            for k in range(KT):
                pe.wait_ge(s["sq"], KT + k + 1)
                last = pe.matmul(bank[:, 6, 0:MEM], ones, sqm[:, k, :], start=k == 0, stop=k == KT - 1)
            last.then_inc(s["ss"], 1)

            pe.wait_ge(s["xn"], KT)
            with pe.Fori(0, N_PROJ // 2) as i2:
                for u in range(2):
                    pe.wait_ge(s[f"win{u}"], i2 * 16 + 16)
                    pe.wait_ge(s["evac"], i2 * 2 + (u + 1))
                    for k in range(KT):
                        for h in range(2):
                            last = pe.matmul(bank[:, 2 * u + h, 0:HALF], ring[u][:, k, :],
                                             xn[:, k, h * HALF:(h + 1) * HALF],
                                             start=k == 0, stop=k == KT - 1)
                    last.then_inc(s["tile"], 1)
            pe.wait_ge(s["mn"], KT)
            with pe.Fori(0, N_MEMT // 2) as i2:
                for u in range(2):
                    pe.wait_ge(s[f"win{u}"], i2 * 16 + 16 * (N_PROJ // 2 + 1))
                    pe.wait_ge(s["evac"], i2 * 2 + (N_PROJ + u + 1))
                    for k in range(KT):
                        last = pe.matmul(bank[:, 2 * u, 0:MEM], ring[u][:, k, :], memn[:, k, :],
                                         start=k == 0, stop=k == KT - 1)
                    last.then_inc(s["tile"], 1)

            jobs = Jobs()

            pe.wait_ge(s["cplx"], 1)
            for ri in range(2):
                for j4 in range(NJ // 4):
                    b = jobs.take_pe(pe)
                    for q in range(4):
                        last = pe.transpose(b[:, q * P:(q + 1) * P], ba[:, ri, j4 * 4 + q], ident)
                    last.then_inc(s["job"], 1)
            pe.wait_ge(s["cplx"], 2)
            for j4 in range(NJ // 4):
                for odd in range(2):
                    b = jobs.take_pe(pe)
                    o = 64 * odd
                    for q in range(4):
                        j = j4 * 4 + q
                        for ri in range(2):
                            last = pe.matmul(b[:, q * P:(q + 1) * P], brep[o:o + 64, ri, j],
                                             cw[o:o + 64, ri, j, 0:CH, :], start=ri == 0, stop=ri == 1)
                    last.then_inc(s["job"], 1)
            pe.wait_ge(s["ucomb"], 1 + CH + 2)
            for ct in range(4):
                for k4 in range(2):
                    b = jobs.take_pe(pe)
                    for q in range(4):
                        last = pe.transpose(b[0:XC, q * P:(q + 1) * P], ucomb[:, ct, k4 * 4 + q, :], ident)
                    last.then_inc(s["job"], 1)
            pe.wait_ge(s["jobfree"], E_UC)
            for g0 in range(0, SG, 6):
                b = jobs.take_pe(pe)
                for g in range(g0, min(g0 + 6, SG)):
                    last = pe.transpose(b[:, (g - g0) * XC:(g - g0 + 1) * XC], utok[0:XC, g],
                                        ident[0:XC, 0:XC])
                last.then_inc(s["job"], 1)
            pe.wait_ge(s["jobfree"], E_U)
            for ri in range(2):
                for j0 in range(0, NJ, 6):
                    b = jobs.take_pe(pe)
                    for j in range(j0, min(j0 + 6, NJ)):
                        for o in (0, 64):
                            last = pe.matmul(b[o:o + 64, (j - j0) * XC:(j - j0 + 1) * XC],
                                             state_in[:, ri, j, o:o + 64], uch[:, 2 * j + o // 64, :],
                                             start=True, stop=True, skip_group_check=True)
                    last.then_inc(s["job"], 1)
            pe.wait_ge(s["toep"], CH)
            pe.wait_ge(s["sprev"], 3)
            for j4 in range(NJ // 4):
                for odd in range(2):
                    b = jobs.take_pe(pe)
                    o = 64 * odd
                    for q in range(4):
                        j = j4 * 4 + q
                        out = b[0:YC, q * P:(q + 1) * P]
                        pe.matmul(out, uch[:, 2 * j + odd, 0:YC], toep[:, odd, j, :], start=True, stop=False)
                        for ri in range(2):
                            last = pe.matmul(out, sprev[o:o + 64, ri, j], cw[o:o + 64, ri, j, 1:CH + 1, :],
                                             start=False, stop=ri == 1)
                    last.then_inc(s["job"], 1)
            pe.wait_ge(s["jobfree"], E_Y)
            for ct in range(4):
                for k4 in range(2):
                    b = jobs.take_pe(pe)
                    for q in range(4):
                        last = pe.transpose(b[:, q * YC:(q + 1) * YC], ytok[0:YC, k4 * 4 + q, ct * P:(ct + 1) * P],
                                            ident[0:YC, 0:YC])
                    last.then_inc(s["job"], 1)
            pe.wait_ge(s["wglu"], 16)
            pe.wait_ge(s["z"], 4)
            for ct in range(4):
                for h in range(2):
                    b = jobs.take_pe(pe)
                    for k in range(4):
                        last = pe.matmul(b[:, 0:HALF], w_glu[:, k, ct * P:(ct + 1) * P],
                                         zcol[:, k, h * HALF:(h + 1) * HALF], start=k == 0, stop=k == 3)
                    last.then_inc(s["job"], 1)
            for g, kv, r in KV:
                b = jobs.take_pe(pe)
                for q in range(2):
                    last = pe.transpose(b[:, q * P:(q + 1) * P],
                                        proj[:, T_QKV + 6 * g + 2 + 2 * kv + q, r * P:(r + 1) * P], ident)
                last.then_inc(s["job"], 1)
            for g in range(NG):
                b = jobs.take_pe(pe)
                for q in range(4):
                    last = pe.transpose(b[0:NB, q * P:(q + 1) * P], proj[:, T_QKV + 6 * g + 2 + q, SEQ:TOK], ident)
                last.then_inc(s["job"], 1)
            for kv in (1, 0):
                for m in range(2):
                    b = jobs.take_pe(pe)
                    for q in range(4):
                        last = pe.transpose(b[:, q * P:(q + 1) * P], mkv[:, 4 * kv + q, m * P:(m + 1) * P], ident)
                    last.then_inc(s["job"], 1)

            def gate_tile(i):
                wait_from(pe, s["gevac"], i)
                n = N_FIRST + i
                pe.wait_ge(s[f"win{n % 2}"], 16 * (n // 2 + 1))
                for k in range(KT):
                    for h in range(2):
                        last = pe.matmul(bank[:, h, 0:HALF], ring[n % 2][:, k, :],
                                         xn[:, k, h * HALF:(h + 1) * HALF], start=k == 0, stop=k == KT - 1)
                last.then_inc(s["tile"], 1)

            def scores(it):
                r, h = divmod(it, NH)
                o, q = 64 * (h % 2), h // 2
                wait_from(pe, s["T"], it)
                for g in range(NG):
                    keys = proj[o:o + 64, T_QKV + 6 * g + 2 + q, 0:SEQ] if g == 0 else \
                        proj[o:o + 64, T_QKV + 6 * g + 2 + q, r * P:(r + 1) * P]
                    out = bank[:, 2, :] if g == 0 else bank[:, 3, (g - 1) * P:g * P]
                    last = pe.matmul(out, proj[o:o + 64, T_QKV + 6 * g + q, r * P:(r + 1) * P], keys,
                                     start=True, stop=True)
                last.then_inc(s["S"], 1)

            pe.wait_ge(s["jobfree"], E_MEM)
            pe.wait_ge(s["evac"], 2 + N_FIRST)
            scores(0)
            for it in range(NCLS * NH):
                r, h = divmod(it, NH)
                gate_tile(it)
                pe.wait_ge(s["pn"], it + 1)
                wait_from(pe, s["ptc"], it)
                for q in range(6):
                    last = pe.transpose(bank[:, 4 + q // 4, q % 4 * P:(q % 4 + 1) * P], pr[:, q * P:(q + 1) * P],
                                        ident)
                last.then_inc(s["PT"], 1)
                if it + 1 < NCLS * NH:
                    scores(it + 1)
                pe.wait_ge(s["ptc"], it + 1)
                wait_from(pe, s["oc"], it)
                o = 64 * (h % 2)
                for q in range(6):
                    g, kt = (0, q) if q < 4 else (q - 3, r)
                    last = pe.matmul(bank[o:o + 64, 6, 0:P], v_rows[:, g, kt, h * DH:(h + 1) * DH],
                                     prT[:, q * P:(q + 1) * P], start=q == 0, stop=q == 5)
                last.then_inc(s["O"], 1)

            def mem_scores(it):
                r, h = divmod(it, MH)
                wait_from(pe, s["mexp"], it - 1)
                pe.matmul(bank[:, 2 + it % 2, 0:MEM], proj[:, T_MQ + h, r * P:(r + 1) * P], mkv[:, h, :],
                          start=True, stop=True).then_inc(s["mS"], 1)

            pe.wait_ge(s["ptc"], NCLS * NH)
            pe.wait_ge(s["oc"], NCLS * NH)
            pe.wait_ge(s["T"], NCLS * NH)
            mem_scores(0)
            for it in range(NCLS * MH):
                r, h = divmod(it, MH)
                if it % 2 == 0:
                    gate_tile(NCLS * NH + it // 2)
                pe.wait_ge(s["mpn"], it + 1)
                wait_from(pe, s["mptc"], it - 1)
                for q in range(2):
                    last = pe.transpose(bank[:, 4 + it % 2, q * P:(q + 1) * P], pm[it % 2][:, q * P:(q + 1) * P],
                                        ident)
                last.then_inc(s["mPT"], 1)
                if it + 1 < NCLS * MH:
                    mem_scores(it + 1)
                pe.wait_ge(s["mptc"], it + 1)
                wait_from(pe, s["moc"], it - 1)
                for q in range(2):
                    last = pe.matmul(bank[:, 6 + it % 2, 0:P], mv_rows[:, q, h * MD:(h + 1) * MD],
                                     pmT[it % 2][:, q * P:(q + 1) * P], start=q == 0, stop=q == 1)
                last.then_inc(s["mO"], 1)

            pe.wait_ge(s["moc"], NCLS * MH)
            pe.wait_ge(s["gevac"], N_GATE)
            pe.wait_ge(s["dprod"], 2)
            for half in range(2):
                for g in range(NG):
                    pe.matmul(bank[32 * half:32 * half + 16, 7, g:g + 1], newprod[64 * half:64 * half + 64, g],
                              ones[64 * half:64 * half + 64, 0:1], start=True, stop=True, skip_group_check=True)
            for b in range(NB):
                pe.wait_ge(s[f"kdec{b % 2}"], 32 * (b // 2 + 1))
                for g in range(NG):
                    for h in range(NH):
                        half, hh = h % 2, h // 2
                        col = g * 64 + half * 32 + hh * 8 + b
                        pe.matmul(bank[:, 1 + half, col:col + 1], slot_k[b % 2][64 * half:64 * half + 64, g, hh, :],
                                  dec_cols[64 * half:64 * half + 64, T_QKV + 6 * g + hh, b:b + 1],
                                  start=True, stop=True)
                for h in range(MH):
                    for q in range(2):
                        col = q * 32 + h * 8 + b
                        last = pe.matmul(bank[:, 3, col:col + 1], slot_mk[b % 2][:, h, q * P:(q + 1) * P],
                                         dec_cols[:, T_MQ + h, b:b + 1], start=True, stop=True)
                last.then_inc(s["dkdone"], 1)
            pe.wait_ge(s["dcopy"], 3)
            for g in range(NG):
                pe.transpose(bank[0:64, 4, g * P:(g + 1) * P], ds_k[:, g, :], ident)
            for q in range(2):
                last = pe.transpose(bank[0:32, 5, q * P:(q + 1) * P], ds_m[:, q, :], ident)
            last.then_inc(s["drow"], 1)
            pe.wait_ge(s["dpd"], NG + 1)
            for g in range(NG):
                pe.transpose(bank[:, 4, g * 64:(g + 1) * 64], dsc[0:64, g, 0:P], ident[0:64, 0:64])
            for q in range(2):
                pe.transpose(bank[:, 5, q * 32:(q + 1) * 32], dm[0:32, q * P:(q + 1) * P], ident[0:32, 0:32])
            pe.matmul(bank[0:NB, 7, 0:NG * 64], c["esel"][0:64, :], dpd[0:64], start=True, stop=True
                      ).then_inc(s["dback"], 1)
            pe.wait_ge(s["dbackc"], 3)
            pe.matmul(bank[:, 6, 0:16], zero[0:NB, :], zero[0:NB, 0:16], start=True, stop=False,
                      skip_group_check=True)
            for g in range(NG):
                for h in range(NH):
                    half, hh = h % 2, h // 2
                    pe.matmul(bank[64 * half:64 * half + 64, 6, hh * 8:hh * 8 + 8],
                              kv_dec[0:NB, g, 1, h * DH:(h + 1) * DH],
                              dpn[0:NB, g, half * 32 + hh * 8:half * 32 + hh * 8 + 8], start=False, stop=False,
                              skip_group_check=True)
            for b in range(NB):
                pe.wait_ge(s[f"vdec{b % 2}"], 64 * (b // 2 + 1))
                for g in range(NG):
                    for h in range(NH):
                        half, hh = h % 2, h // 2
                        pe.matmul(bank[64 * half:64 * half + 64, 6, hh * 8 + b:hh * 8 + b + 1],
                                  slot_v[b % 2][:, g, h * DH:(h + 1) * DH],
                                  dpT[:, g, half * 32 + hh * 8 + b:half * 32 + hh * 8 + b + 1],
                                  start=False, stop=False, skip_group_check=True)
                if b == NB - 1:
                    pe.matmul(bank[:, 6, 0:16], zero[0:NB, :], zero[0:NB, 0:16], start=False, stop=True,
                              skip_group_check=True)
                for h in range(MH):
                    for q in range(2):
                        last = pe.matmul(bank[:, 7, 256 + h * 8 + b:257 + h * 8 + b],
                                         slot_mv[b % 2][:, q, h * MD:(h + 1) * MD],
                                         dmT[:, q, h * 8 + b:h * 8 + b + 1], start=q == 0, stop=q == 1)
                last.then_inc(s["dvdone"], 1)

            pe.wait_ge(s["wout"], 48)
            pe.wait_ge(s["doc"], 2)
            branches = ((w_att, attT, 2), (w_ssm, ssmT, 4), (w_mem, memT, 4))
            for j in range(KT):
                for i, (w, src, nk) in enumerate(branches):
                    wait_from(pe, s["Pfree"], 3 * (j - 1) + i + 1 if j else 0)
                    for k in range(nk):
                        for h in range(2):
                            last = pe.matmul(bank[:, 2 * i + h, 0:HALF], w[:, k, j * P:(j + 1) * P],
                                             src[:, k, h * HALF:(h + 1) * HALF], start=k == 0, stop=k == nk - 1)
                    last.then_inc(s["Pj"], 1)
            pe.wait_ge(s["wo"], 32)
            pe.wait_ge(s["merged"], KT)
            for T in range(NT):
                if T == 4:
                    pe.wait_ge(s["h"], 1)
                b0 = (2 * T + 6) % 8
                for half in range(2):
                    for k in range(KT):
                        last = pe.matmul(bank[0:ROWS[T], b0 + half, :], gates[:, 3 * k, T * P:T * P + ROWS[T]],
                                         w_o[k // 4][:, k % 4, half * 512:(half + 1) * 512],
                                         start=k == 0, stop=k == KT - 1)
                last.then_inc(s["wo_mm"], 1)
            pe.wait_ge(s["h"], NT)
            for T in range(NT):
                pe.wait_ge(s["hn"], T + 1)
                wait_from(pe, s["hnT"], T - 1)
                n = ROWS[T]
                for k in range(KT):
                    last = pe.transpose(bank[:, 2 * (T % 2) + k // 4, k % 4 * P:k % 4 * P + n],
                                        hn_rows[0:n, T, k * P:(k + 1) * P], ident[0:n, 0:n])
                last.then_inc(s["ht"], 1)
                pe.wait_ge(s["hnT"], T + 1)
                for k in range(KT):
                    last = pe.matmul(bank[0:n, 4, T * 36:T * 36 + 36], hnT[T % 2][:, k, 0:n], w_route[:, k, :],
                                     start=k == 0, stop=k == KT - 1)
                last.then_inc(s["lg"], 1)
            pe.wait_ge(s["chosen"], 1)
            for T in range(NT):
                out = bank[:, 5, T * NE:(T + 1) * NE]
                for q in range(T):
                    pe.matmul(out, ones, chosen[:, q, :], start=q == 0, stop=False)
                pe.matmul(out, c["triu"], chosen[:, T, :], start=T == 0, stop=True)
            for q in range(NT):
                last = pe.matmul(bank[:, 6, 0:NE], ones, chosen[:, q, :], start=q == 0, stop=q == NT - 1)
            last.then_inc(s["rank"], 1)

            pe.wait_ge(s["npass"], 1)
            n_p = pe.value_load(n_pass[0:1, 0:1], min_val=1, max_val=MAXP)
            with pe.Fori(0, n_p) as p:
                pe.wait_ge(s["hot"], p + 1)
                for k in range(2):
                    for T in range(NT):
                        last = pe.matmul(bank[0:CAP, 7, 0:NE], hot[k][:, T, :], mtok[k][:, T, :],
                                         start=k == 0 and T == 0, stop=k == 1 and T == NT - 1)
                last.then_inc(s["idxmm"], 1)
                pe.wait_ge(s["idx"], p + 1)
                pe.sem_inc(s["held"], 1)
                with pe.Fori(0, NE // 2) as e2:
                    for u in range(2):
                        w1, w3, w2 = wb[u]
                        step = p * NE + e2 * 2
                        loads = p * (NE // 2) + e2
                        pe.wait_ge(s[f"xg{u}"], loads * 16 + 16)
                        pe.wait_ge(s["xc"], step + (u + 1))
                        pe.sem_inc(s["held"], 1)
                        for k in range(KT):
                            last = pe.transpose(bank[:, u, k * CAP:(k + 1) * CAP], xg[u][0:CAP, k * P:(k + 1) * P],
                                                ident[0:CAP, 0:CAP])
                        last.then_inc(s["xt"], 1)
                        pe.wait_ge(s["xc"], step + (u + 3))
                        pe.wait_ge(s["hT"], step + (u + 1))
                        pe.wait_ge(s[f"w13_{u}"], loads * 32 + 32)
                        for i, w in enumerate((w1, w3)):
                            for f in range(FT):
                                for k in range(KT):
                                    lo = (i * FT + f) * CAP
                                    last = pe.matmul(bank[:, 2 + u, lo:lo + CAP], w[:, k, f * P:(f + 1) * P],
                                                     xgT[u][:, k, :], start=k == 0, stop=k == KT - 1)
                        last.then_inc(s["gu"], 1)
                        pe.wait_ge(s["hT"], step + (u + 3))
                        pe.wait_ge(s["yc"], step + (u + 1))
                        pe.wait_ge(s[f"w2_{u}"], loads * 16 + 16)
                        for half in range(2):
                            for f in range(FT):
                                last = pe.matmul(bank[0:CAP, 4 + 2 * u + half, :], hT[u][:, f, :],
                                                 w2[:, f, half * 512:(half + 1) * 512],
                                                 start=f == 0, stop=f == FT - 1)
                        last.then_inc(s["y"], 1)
                pe.wait_ge(s["yc"], p * NE + (NE + 2))

        @block.scalar
        def _(act):
            act.sem_inc(s["evac"], 2)
            act.sem_inc(s["yc"], 2)
            for u in range(2):
                act.sem_inc(s[f"yo{u}"], 16)
            act.wait_ge(s["ssmp"], 16)
            act.activation(par[:, 0], ssm_in[:, 2], ACT.Exp).then_inc(s["dt"], 1)
            act.wait_ge(s["lrdt"], 1)
            act.activation(par[:, 2], par[:, 1], ACT.Exp).then_inc(s["dt"], 1)
            act.wait_ge(s["lrdt"], 2)
            act.activation(par[:, 5], par[:, 4], ACT.Sin).then_inc(s["trig"], 1)
            act.activation(par[:, 6], par[:, 4], ACT.Sin, scale=0.5).then_inc(s["trig"], 1)
            act.wait_ge(s["cst"], 16)
            act.wait_ge(s["ss"], 1)
            for h in range(2):
                act.activation(rms[:, h * HALF:(h + 1) * HALF], bank[:, h, 0:HALF], ACT.Sqrt, bias=eps_ap,
                               scale=1.0 / D).then_inc(s["rms"], 1)
            act.wait_ge(s["ss"], 2)
            act.activation(rmsm, bank[:, 6, 0:MEM], ACT.Sqrt, bias=eps_ap, scale=1.0 / D).then_inc(s["rms"], 1)
            with act.Fori(0, N_PROJ // 2) as i2:
                for u in range(2):
                    act.wait_ge(s["tile"], i2 * 2 + (u + 3))
                    dst = proj[:, bass.ds(i2 * 2 + u, 1), :].rearrange("p o (h t) -> p (o h) t", h=2)
                    act.activation(dst, bank[:, 2 * u:2 * u + 2, 0:HALF], ACT.Copy).then_inc(s["evac"], 1)
            with act.Fori(0, N_MEMT // 2) as i2:
                for u in range(2):
                    act.wait_ge(s["tile"], i2 * 2 + (N_PROJ + u + 3))
                    act.activation(mkv[:, bass.ds(i2 * 2 + u, 1), :].rearrange("p o t -> p (o t)"),
                                   bank[:, 2 * u, 0:MEM], ACT.Copy).then_inc(s["evac"], 1)

            jobs = Jobs()
            for ri in range(2):
                for j4 in range(NJ // 4):
                    b = jobs.take_act(act)
                    act.activation(state_in[:, ri, j4 * 4:j4 * 4 + 4, :].rearrange("p a b -> p (a b)"), b, ACT.Copy
                                   ).then_inc(s["jobfree"], 1)
            for j4 in range(NJ // 4):
                for odd in range(2):
                    b = jobs.take_act(act)
                    act.activation(kern[:, odd, j4 * 4:j4 * 4 + 4, :].rearrange("p a b -> p (a b)"), b, ACT.Copy
                                   ).then_inc(s["jobfree"], 1)
            for ct in range(4):
                for k4 in range(2):
                    b = jobs.take_act(act)
                    for q in range(4):
                        last = act.activation(utok[0:XC, ct * 8:ct * 8 + 8, k4 * 4 + q, :],
                                              b[0:XC, q * P:(q + 1) * P].rearrange("p (g c) -> p g c", g=8),
                                              ACT.Copy)
                    last.then_inc(s["jobfree"], 1)
            act.wait_ge(s["toep"], CH)
            for g0 in range(0, SG, 6):
                b = jobs.take_act(act)
                n = min(6, SG - g0)
                act.activation(uch[:, g0:g0 + n, :].rearrange("p a b -> p (a b)"), b[:, 0:n * XC], ACT.Copy
                               ).then_inc(s["jobfree"], 1)
            for ri in range(2):
                for j0 in range(0, NJ, 6):
                    b = jobs.take_act(act)
                    n = min(6, NJ - j0)
                    act.activation(xst[:, ri, j0:j0 + n, :].rearrange("p a b -> p (a b)"), b[:, 0:n * XC], ACT.Copy
                                   ).then_inc(s["jobfree"], 1)
            act.wait_ge(s["sprev"], 3)
            for j4 in range(NJ // 4):
                for odd in range(2):
                    b = jobs.take_act(act)
                    for q in range(4):
                        g = 2 * (j4 * 4 + q) + odd
                        last = act.activation(ytok[0:YC, :, g * SCH:(g + 1) * SCH],
                                              b[0:YC, q * P:(q + 1) * P].rearrange("p (t c) -> p t c", t=CH),
                                              ACT.Copy)
                    last.then_inc(s["jobfree"], 1)
            act.wait_ge(s["states"], 3)
            for ct in range(4):
                for k4 in range(2):
                    b = jobs.take_act(act)
                    src = b[:, 0:4 * YC].rearrange("p (r n) -> p r n", r=4)
                    dst = ycol[:, ct, 0:SEQ].rearrange("p (r n q) -> p r n q", r=4, q=2)[:, :, :, k4]
                    last = act.activation(dst, src[:, :, 0:NCH], ACT.Copy)
                    if k4 == 0:
                        last.then_inc(s["achain"], 1)
                        last = act.activation(ycol[:, ct, SEQ:TOK], src[:, 0, NCH:YC], ACT.Copy)
                    last.then_inc(s["jobfree"], 1)
            for ct in range(4):
                act.wait_ge(s["yadd"], ct + 1)
                act.activation(zcol[:, ct, :], ycol[:, ct, :], ACT.Gelu_apprx_tanh).then_inc(s["z"], 1)
            act.wait_ge(s["small"], 160)
            for ct in range(4):
                for h in range(2):
                    b = jobs.take_act(act)
                    act.activation(glu[:, ct, h * HALF:(h + 1) * HALF], b[:, 0:HALF], ACT.Sigmoid,
                                   bias=b_glu[:, ct:ct + 1]).then_inc(s["jobfree"], 1)
            for g, kv, r in KV:
                b = jobs.take_act(act)
                if kv == 0 and r == 0 and g == 2:
                    act.wait_ge(s["kout"], 64)
                dst = k_rows[g % 2][:, r, :] if kv == 0 else v_rows[:, g, r, :]
                act.activation(dst, b[:, 0:ATT], ACT.Copy).then_inc(s["jobfree"], 1)
                if r == NCLS - 1:
                    act.wait_ge(s["jobfree"], jobs.n)
                    act.sem_inc(s["krows"], 1)
            for g in range(NG):
                b = jobs.take_act(act)
                act.activation(kv_dec[0:NB, g].rearrange("p a b -> p (a b)"), b[0:NB, :], ACT.Copy
                               ).then_inc(s["jobfree"], 1)
            act.wait_ge(s["jobfree"], jobs.n)
            act.sem_inc(s["krows"], 1)
            for kv in (1, 0):
                for m in range(2):
                    b = jobs.take_act(act)
                    act.activation((mv_rows if kv else mk_rows)[:, m, :], b, ACT.Copy).then_inc(s["jobfree"], 1)
                act.wait_ge(s["jobfree"], jobs.n)
                act.sem_inc(s["krows"], 1)

            def gate_out(i):
                act.wait_ge(s["tile"], 2 + N_FIRST + i + 1)
                act.activation(gates[:, i, :].rearrange("p (h t) -> p h t", h=2), bank[:, 0:2, 0:HALF], ACT.Exp,
                               scale=-1.0).then_inc(s["gevac"], 1)

            act.wait_ge(s["kout"], 16 * (2 * NG))
            for it in range(NCLS * NH):
                act.wait_ge(s["nmax"], it + 1)
                wait_from(act, s["PT"], it)
                act.activation(pr, sc, ACT.Exp, bias=stat[:, 2 * (it % 2) + 1:2 * (it % 2) + 2], scale=ATT_SCALE,
                               accum_out=stat[:, 8 + it % 2:9 + it % 2]).then_inc(s["exp"], 1)
                gate_out(it)
                act.wait_ge(s["PT"], it + 1)
                wait_from(act, s["O"], it)
                act.activation(prT[:, 0:512], bank[:, 4, :], ACT.Copy)
                act.activation(prT[:, 512:768], bank[:, 5, 0:256], ACT.Copy).then_inc(s["ptc"], 1)
            for it in range(NCLS * MH):
                act.wait_ge(s["mnmax"], it + 1)
                wait_from(act, s["mPT"], it - 1)
                if it == 0:
                    act.wait_ge(s["PT"], NCLS * NH)
                act.activation(pm[it % 2], bank[:, 2 + it % 2, 0:MEM], ACT.Exp,
                               bias=stat[:, 16 + it % 2:17 + it % 2], scale=MEM_SCALE,
                               accum_out=stat[:, 18 + it % 2:19 + it % 2]).then_inc(s["mexp"], 1)
                if it % 2 == 0:
                    gate_out(NCLS * NH + it // 2)
                act.wait_ge(s["mPT"], it + 1)
                wait_from(act, s["mO"], it - 1)
                act.activation(pmT[it % 2], bank[:, 4 + it % 2, 0:MEM], ACT.Copy).then_inc(s["mptc"], 1)

            act.wait_ge(s["dnmax"], 2)
            act.activation(dsc[0:64].rearrange("p a b -> p (a b)"), dsc[0:64].rearrange("p a b -> p (a b)"),
                           ACT.Exp, bias=stat[0:64, 25:26], scale=ATT_SCALE, accum_out=stat[0:64, 26:27]
                           ).then_inc(s["dexp"], 1)
            act.activation(dm[0:32, :], bank[0:32, 5, 0:MEM], ACT.Exp, bias=stat[0:32, 29:30], scale=MEM_SCALE,
                           accum_out=stat[0:32, 30:31]).then_inc(s["dexp"], 1)
            act.wait_ge(s["dback"], 1)
            act.activation(dpT.rearrange("p a b -> p (a b)"), bank[:, 4, 0:NG * 64], ACT.Copy).then_inc(s["dbackc"], 1)
            act.activation(dmT.rearrange("p a b -> p (a b)"), bank[:, 5, 0:64], ACT.Copy).then_inc(s["dbackc"], 1)
            act.activation(dpn[0:NB].rearrange("p a b -> p (a b)"), bank[0:NB, 7, 0:NG * 64], ACT.Copy
                           ).then_inc(s["dbackc"], 1)

            for T in range(NT):
                n = ROWS[T]
                act.wait_ge(s["h"], T + 1)
                act.activation(hn_rows[0:n, T, :], h_rows[0:n, T, :], ACT.Square,
                               accum_out=stat[0:n, 32 + T:33 + T]).then_inc(s["hss"], 1)
            act.wait_ge(s["hss"], NT)
            for T in range(NT):
                n = ROWS[T]
                act.activation(stat[0:n, 37 + T:38 + T], stat[0:n, 32 + T:33 + T], ACT.Sqrt, bias=eps_ap[0:n],
                               scale=1.0 / D).then_inc(s["hrms"], 1)
            for T in range(NT):
                n = ROWS[T]
                act.wait_ge(s["ht"], T + 1)
                wait_from(act, s["lg"], T - 1)
                if T == 0:
                    act.wait_ge(s["wo_mm"], NT)
                act.activation(hnT[T % 2][:, 0:4, 0:n],
                               bank[:, 2 * (T % 2), :].rearrange("p (k a) -> p k a", k=4)[:, :, 0:n], ACT.Copy)
                act.activation(hnT[T % 2][:, 4:8, 0:n],
                               bank[:, 2 * (T % 2) + 1, :].rearrange("p (k a) -> p k a", k=4)[:, :, 0:n],
                               ACT.Copy).then_inc(s["hnT"], 1)
            act.wait_ge(s["gmax"], 1)
            act.activation(ex4.rearrange("p a b -> p (a b)"), ex4.rearrange("p a b -> p (a b)"), ACT.Exp
                           ).then_inc(s["gexp"], 1)
            act.wait_ge(s["gmax"], 2)
            act.activation(r5[5], r5[4], ACT.Exp).then_inc(s["gexp"], 1)

            act.wait_ge(s["npass"], 1)
            act.wait_ge(s["lg"], NT)
            n_p = act.value_load(n_pass[0:1, 0:1], min_val=1, max_val=MAXP)
            with act.Fori(0, n_p) as p:
                with act.Fori(0, NE // 2) as e2:
                    for u in range(2):
                        step = p * NE + e2 * 2
                        act.wait_ge(s["gu"], step + (u + 3))
                        act.wait_ge(s["hT"], step + (u + 1))
                        act.activation(sg[u].rearrange("p a b -> p (a b)"), bank[:, 2 + u, 0:FT * CAP], ACT.Silu
                                       ).then_inc(s["sg"], 1)
                        act.wait_ge(s["y"], step + (u + 3))
                        act.wait_ge(s[f"yo{u}"], (p * (NE // 2) + e2) * 16 + 16)
                        for half in range(2):
                            last = act.activation(y_sb[u][0:CAP, half * 512:(half + 1) * 512],
                                                  bank[0:CAP, 4 + 2 * u + half, :], ACT.Copy)
                        last.then_inc(s["yc"], 1)
                        act.wait_ge(s["yc"], step + (u + 3))
                        act.wait_ge(s["fsum"], p * NT + NT)
                        act.dma_start(t["y_slots"][bass.ds(e2 * 2 + u, 1)].rearrange("a c d -> (a c) d"),
                                      y_sb[u][0:CAP, :]).then_inc(s[f"yo{u}"], 16)
            for T in range(NT):
                n = ROWS[T]
                act.wait_ge(s["fsum"], n_p * NT + (T + 1))
                if T >= 2:
                    act.wait_ge(s[f"fout{T % 2}"], 16 * (T // 2))
                act.activation(fin[T % 2][0:n, :], h_rows[0:n, T, :], ACT.Square,
                               accum_out=stat[0:n, 42 + T:43 + T]).then_inc(s["fss"], 1)
                act.wait_ge(s["fss"], T + 1)
                act.activation(stat[0:n, 47 + T:48 + T], stat[0:n, 42 + T:43 + T], ACT.Sqrt, bias=eps_ap[0:n],
                               scale=1.0 / D).then_inc(s["frms"], 1)

        @block.vector
        def _(dve):
            TT, TS, STT = dve.tensor_tensor, dve.tensor_scalar, dve.scalar_tensor_tensor
            chain = [0]

            def then(*ins):
                for i in ins:
                    i.then_inc(s["vchain"], 1)
                chain[0] += len(ins)
                dve.wait_ge(s["vchain"], chain[0])

            dve.sem_inc(s["xc"], 2)
            dve.sem_inc(s["hT"], 2)
            dve.sem_inc(s["fsum"], NT)

            lr, li, dt = ssm_in[:, 0], ssm_in[:, 1], par[:, 0]
            lrdt, mag, ang, red, s1, sh = (par[:, i] for i in range(1, 7))
            dve.wait_ge(s["ssmp"], 16)
            dve.wait_ge(s["dt"], 1)
            TT(lrdt, lr, dt, ALU.mult).then_inc(s["lrdt"], 1)
            then(TT(ang, li, dt, ALU.mult))
            kk = par[:, 7]
            then(TS(kk, ang, 1.0 / TWO_PI, ROUND, ALU.mult, ALU.add))
            then(TS(kk, kk, -ROUND, None, ALU.add))
            then(STT(out=red, in0=kk, scalar=-PI_A, in1=ang, op0=ALU.mult, op1=ALU.add))
            then(STT(out=red, in0=kk, scalar=-PI_B, in1=red, op0=ALU.mult, op1=ALU.add))
            then(STT(out=red, in0=kk, scalar=-PI_C, in1=red, op0=ALU.mult, op1=ALU.add))
            lim = float(np.float32(3.1415925))
            TS(red, red, lim, -lim, ALU.min, ALU.max).then_inc(s["lrdt"], 1)

            dve.wait_ge(s["x"], 16)
            for k in range(KT):
                TT(sq[:, k, :], xn[:, k, :], xn[:, k, :], ALU.mult).then_inc(s["sq"], 1)
            dve.wait_ge(s["mem"], 16)
            for k in range(KT):
                TT(sqm[:, k, :], memn[:, k, :], memn[:, k, :], ALU.mult).then_inc(s["sq"], 1)
            dve.wait_ge(s["small"], 160)
            dve.wait_ge(s["rms"], 2)
            then(dve.reciprocal(rms, rms))
            for k in range(KT):
                STT(out=xn[:, k, :], in0=xn[:, k, :], scalar=gain1[:, k:k + 1], in1=rms, op0=ALU.mult,
                    op1=ALU.mult).then_inc(s["xn"], 1)
            dve.wait_ge(s["rms"], 3)
            then(dve.reciprocal(rmsm, rmsm))
            for k in range(KT):
                STT(out=memn[:, k, :], in0=memn[:, k, :], scalar=gain_mem[:, k:k + 1], in1=rmsm, op0=ALU.mult,
                    op1=ALU.mult).then_inc(s["mn"], 1)

            ar, ai, cosm = par[:, 8], par[:, 9], par[:, 10]
            t1, t2, den, nr, zr, zi = (par[:, i] for i in range(11, 17))
            dve.wait_ge(s["dt"], 2)
            dve.wait_ge(s["trig"], 2)
            then(TT(cosm, sh, sh, ALU.mult), TT(ai, mag, s1, ALU.mult))
            then(TS(cosm, cosm, -2.0, 1.0, ALU.mult, ALU.add))
            then(TT(ar, mag, cosm, ALU.mult), TT(t1, lr, lr, ALU.mult), TT(t2, li, li, ALU.mult))
            then(TT(den, t1, t2, ALU.add), TS(nr, ar, -1.0, None, ALU.add))
            then(dve.reciprocal(den, den), TT(t1, nr, lr, ALU.mult), TT(t2, ai, li, ALU.mult))
            then(TT(zr, t1, t2, ALU.add))
            then(TT(zr, zr, den, ALU.mult), TT(t1, ai, lr, ALU.mult), TT(t2, nr, li, ALU.mult))
            then(TT(zi, t1, t2, ALU.subtract))
            then(TT(zi, zi, den, ALU.mult))

            def cmul(out, a, b, shape, tmp=None, neg_im=False):
                n = int(np.prod(shape))
                names = "abcd"[:len(shape)]
                flat = f"p ({' '.join(names)}) -> p {' '.join(names)}"
                u, v = (x[:, 0:n] for x in (tmp or ctmp))
                if len(shape) > 1:
                    u, v = (x.rearrange(flat, **dict(zip(names, shape))) for x in (u, v))
                then(TT(u, a[1], b[1], ALU.mult), TT(out[0], a[0], b[0], ALU.mult),
                     TT(v, a[0], b[1], ALU.mult), TT(out[1], a[1], b[0], ALU.mult))
                if neg_im:
                    then(TT(out[0], out[0], u, ALU.subtract),
                         STT(out=out[1], in0=out[1], scalar=-1.0, in1=v, op0=ALU.mult, op1=ALU.subtract))
                else:
                    then(TT(out[0], out[0], u, ALU.subtract), TT(out[1], out[1], v, ALU.add))

            def ri(x, *idx):
                return [x[(slice(None), i) + idx] for i in range(2)]

            def wide(x, axis, shape):
                return x.unsqueeze(axis).to_broadcast([P] + list(shape))

            z_ = [wide(x, 2, (NJ, SCH)) for x in (zr, zi)]
            cmul(ri(bbar), z_, ri(b_in), (NJ, SCH))
            then(dve.memset(pw[:, 0, :, 0:1], 1.0), dve.memset(pw[:, 1, :, 0:1], 0.0),
                 dve.tensor_copy(pw[:, 0, :, 1], ar), dve.tensor_copy(pw[:, 1, :, 1], ai))
            cmul(ri(pw, slice(None), 2), ri(pw, slice(None), 1), ri(pw, slice(None), 1), (NJ,))
            cmul(ri(pw, slice(None), slice(3, 5)), ri(pw, slice(None), slice(1, 3)),
                 [wide(x, 2, (NJ, 2)) for x in ri(pw, slice(None), 2)], (NJ, 2))
            cmul(ri(pw, slice(None), slice(5, 9)), ri(pw, slice(None), slice(1, 5)),
                 [wide(x, 2, (NJ, 4)) for x in ri(pw, slice(None), 4)], (NJ, 4))
            then(*[dve.tensor_copy(rpw[:, :, :, i], pw[:, :, :, CH - 1 - i]) for i in range(CH)])
            then(dve.tensor_copy(apow[:, :, 0, :], pw[:, :, :, CH]))
            for lv in range(1, LEVELS):
                cmul(ri(apow, lv), ri(apow, lv - 1), ri(apow, lv - 1), (NJ,))
            full = (NJ, CH, SCH)
            cmul(ri(ba), [wide(x, 3, full) for x in ri(rpw)], [wide(x, 2, full) for x in ri(bbar)], full)
            dve.sem_inc(s["cplx"], 1)
            then(*[dve.tensor_copy(x, wide(y, 2, full)) for x, y in zip(ri(brep), ri(bbar))])
            full = (NJ, CH + 1, SCH)
            cmul(ri(cw), [wide(x, 3, full) for x in ri(pw)], [wide(x, 2, full) for x in ri(c_in)], full, neg_im=True)
            dve.sem_inc(s["cplx"], 1)

            dve.wait_ge(s["evac"], 2 + N_PROJ)
            dve.tensor_copy(dec_cols, proj[:, :, SEQ:TOK]).then_inc(s["dprod"], 1)

            dve.wait_ge(s["jobfree"], E_K)
            dve.wait_ge(s["cst"], 16)
            for k in range(CH):
                w = (CH - k) * SCH
                sm = c["smask"][:, k:k + 1]
                if k == 0:
                    TS(toep, kern, sm, None, ALU.mult).then_inc(s["toep"], 1)
                else:
                    dve.wait_ge(s["toep"], k)
                    STT(out=toep[:, :, :, k * SCH:], in0=kern[:, :, :, 0:w], scalar=sm,
                        in1=toep[:, :, :, k * SCH:], op0=ALU.mult, op1=ALU.add).then_inc(s["toep"], 1)

            dve.wait_ge(s["jobfree"], E_X)
            sh_ = (NJ, NB)
            cmul(ri(st_dec), [wide(x, 2, sh_) for x in (ar, ai)], ri(h0), sh_, tmp=stmp[0:2])
            TT(st_dec, st_dec, xst[:, :, :, YC:XC], ALU.add).then_inc(s["states"], 1)
            for lv in range(LEVELS):
                d = 1 << lv
                w = NCH - d
                u = [x[:, 0:NJ * w].rearrange("p (j n) -> p j n", j=NJ) for x in stmp]
                pr_, pi_ = (wide(x, 2, (NJ, w)) for x in ri(apow, lv))
                xr, xi = xst[:, 0, :, 0:w], xst[:, 1, :, 0:w]
                yr, yi = xst[:, 0, :, d:NCH], xst[:, 1, :, d:NCH]
                then(TT(u[0], xr, pr_, ALU.mult), TT(u[1], xi, pi_, ALU.mult),
                     TT(u[2], xi, pr_, ALU.mult), TT(u[3], xr, pi_, ALU.mult))
                then(TT(yr, yr, u[0], ALU.add), TT(yi, yi, u[2], ALU.add))
                then(TT(yr, yr, u[1], ALU.subtract), TT(yi, yi, u[3], ALU.add))
            dve.memset(sprev[:, :, :, 0:1], 0.0).then_inc(s["sprev"], 1)
            dve.tensor_copy(sprev[:, :, :, NCH:YC], h0).then_inc(s["sprev"], 1)
            for i in range(2):
                last = dve.tensor_copy(sprev[:, i, :, 1:NCH], xst[:, i, :, 0:NCH - 1])
            last.then_inc(s["sprev"], 1)
            for i in range(2):
                dve.tensor_copy(st_prompt[:, i, :], xst[:, i, :, NCH - 1]).then_inc(s["states"], 1)
            for ct in range(4):
                dve.wait_ge(s["jobfree"], E_Y + 2 * (ct + 1))
                STT(out=ycol[:, ct, :], in0=proj[:, ct, :], scalar=ssm_d[:, ct:ct + 1], in1=ycol[:, ct, :],
                    op0=ALU.mult, op1=ALU.add).then_inc(s["yadd"], 1)
            for ct in range(4):
                dve.wait_ge(s["jobfree"], E_YT + 2 * (ct + 1))
                TT(ssmT[:, ct, :], zcol[:, ct, :], glu[:, ct, :], ALU.mult).then_inc(s["ssm"], 1)

            dve.wait_ge(s["kout"], 16 * (2 * NG))
            dve.wait_ge(s["dist0"], 16)

            def o_copy(it):
                r, h = divmod(it, NH)
                o = 64 * (h % 2)
                dve.wait_ge(s["O"], it + 1)
                dve.tensor_copy(attT[o:o + 64, h // 2, r * P:(r + 1) * P], bank[o:o + 64, 6, 0:P]
                                ).then_inc(s["oc"], 1)

            for it in range(NCLS * NH):
                r, h = divmod(it, NH)
                mx, nm, dn, rd = (stat[:, i:i + 1] for i in (2 * (it % 2), 2 * (it % 2) + 1, 8 + it % 2, 10 + it % 2))
                dve.wait_ge(s["S"], it + 1)
                wait_from(dve, s["exp"], it)
                sl = -slope(h) / ATT_SCALE
                STT(out=sc[:, 0:512], in0=dist0[:, r, :], scalar=sl, in1=bank[:, 2, :], op0=ALU.mult,
                    op1=ALU.add).then_inc(s["vchain"], 1)
                STT(out=sc[:, 512:768], in0=dist12, scalar=sl, in1=bank[:, 3, 0:256], op0=ALU.mult,
                    op1=ALU.add).then_inc(s["T"], 1)
                chain[0] += 1
                dve.wait_ge(s["vchain"], chain[0])
                dve.wait_ge(s["T"], it + 1)
                then(dve.tensor_reduce(mx, sc, AX, ALU.max))
                TS(nm, mx, -ATT_SCALE, None, ALU.mult).then_inc(s["nmax"], 1)
                if it:
                    o_copy(it - 1)
                dve.wait_ge(s["exp"], it + 1)
                then(dve.reciprocal(rd, dn))
                TS(pr, pr, rd, None, ALU.mult).then_inc(s["pn"], 1)
            o_copy(NCLS * NH - 1)

            def mo_copy(it):
                r, h = divmod(it, MH)
                dve.wait_ge(s["mO"], it + 1)
                dve.tensor_copy(memT[:, h, r * P:(r + 1) * P], bank[:, 6 + it % 2, 0:P]).then_inc(s["moc"], 1)

            for it in range(NCLS * MH):
                b = it % 2
                mx, nm, dn, rd = (stat[:, i:i + 1] for i in (20 + b, 16 + b, 18 + b, 22 + b))
                dve.wait_ge(s["mS"], it + 1)
                then(dve.tensor_reduce(mx, bank[:, 2 + b, 0:MEM], AX, ALU.max))
                wait_from(dve, s["mexp"], it - 1)
                TS(nm, mx, -MEM_SCALE, None, ALU.mult).then_inc(s["mnmax"], 1)
                if it:
                    mo_copy(it - 1)
                dve.wait_ge(s["mexp"], it + 1)
                then(dve.reciprocal(rd, dn))
                TS(pm[b], pm[b], rd, None, ALU.mult).then_inc(s["mpn"], 1)
            mo_copy(NCLS * MH - 1)

            dve.wait_ge(s["dprod"], 1)
            six = dec_cols[:, T_QKV:T_MQ, :].rearrange("p (g x) b -> p g x b", g=NG)
            TT(newprod, six[:, :, 0:2, :], six[:, :, 2:4, :], ALU.mult).then_inc(s["dprod"], 1)
            then(dve.memset(ds_k, 0.0), dve.memset(zero, 0.0), dve.memset(dsc, 0.0))
            dve.wait_ge(s["dkdone"], NB)
            for half in range(2):
                dve.tensor_copy(ds_k[:, :, half * 32:half * 32 + 16],
                                bank[:, 1 + half, 0:NG * 64].rearrange("p (g r) -> p g r", g=NG)
                                [:, :, half * 32:half * 32 + 16]).then_inc(s["dcopy"], 1)
            dve.tensor_copy(ds_m.rearrange("p a b -> p (a b)"), bank[:, 3, 0:64]).then_inc(s["dcopy"], 1)
            dve.wait_ge(s["drow"], 1)
            ins = [TT(dsc[0:64, :, 0:P], c["decbias"][0:64, :].rearrange("p (g m) -> p g m", g=NG),
                      bank[0:64, 4, 0:NG * P].rearrange("p (g m) -> p g m", g=NG), ALU.add)]
            for half in range(2):
                o = 32 * half
                ins.append(dve.tensor_copy(dsc[o:o + 16, :, P], bank[o:o + 16, 7, 0:NG]))
            then(*ins)
            then(dve.tensor_reduce(stat[0:64, 24:25], dsc[0:64].rearrange("p a b -> p (a b)"), AX, ALU.max),
                 dve.tensor_reduce(stat[0:32, 28:29], bank[0:32, 5, 0:MEM], AX, ALU.max))
            TS(stat[0:64, 25:26], stat[0:64, 24:25], -ATT_SCALE, None, ALU.mult).then_inc(s["dnmax"], 1)
            TS(stat[0:32, 29:30], stat[0:32, 28:29], -MEM_SCALE, None, ALU.mult).then_inc(s["dnmax"], 1)
            dve.wait_ge(s["dexp"], 2)
            then(dve.reciprocal(stat[0:64, 27:28], stat[0:64, 26:27]),
                 dve.reciprocal(stat[0:32, 31:32], stat[0:32, 30:31]))
            then(TS(dsc[0:64].rearrange("p a b -> p (a b)"), dsc[0:64].rearrange("p a b -> p (a b)"),
                    stat[0:64, 27:28], None, ALU.mult))
            TS(dm[0:32, :], dm[0:32, :], stat[0:32, 31:32], None, ALU.mult).then_inc(s["dpd"], 1)
            for g in range(NG):
                TS(dpd[0:64, g, :], ident[0:64, 0:64], dsc[0:64, g, P:P + 1], None, ALU.mult).then_inc(s["dpd"], 1)
            dve.wait_ge(s["dvdone"], NB)
            dve.tensor_copy(attT[:, :, SEQ:TOK], bank[:, 6, 0:16].rearrange("p (q b) -> p q b", q=2)
                            ).then_inc(s["doc"], 1)
            dve.tensor_copy(memT[:, :, SEQ:TOK], bank[:, 7, 256:256 + MH * NB].rearrange("p (h b) -> p h b", h=MH)
                            ).then_inc(s["doc"], 1)

            for j in range(KT):
                for i in range(3):
                    g = gates[:, 3 * j + i, :]
                    then(TS(g, g, 1.0, None, ALU.add))
                    then(dve.reciprocal(g, g))
                    dve.wait_ge(s["Pj"], 3 * j + i + 1)
                    TT(g.rearrange("p (h t) -> p h t", h=2), g.rearrange("p (h t) -> p h t", h=2),
                       bank[:, 2 * i:2 * i + 2, 0:HALF], ALU.mult).then_inc(s["Pfree"], 1)
                    dve.wait_ge(s["Pfree"], 3 * j + i + 1)
                then(TT(gates[:, 3 * j, :], gates[:, 3 * j, :], gates[:, 3 * j + 1, :], ALU.add))
                TT(gates[:, 3 * j, :], gates[:, 3 * j, :], gates[:, 3 * j + 2, :], ALU.add).then_inc(s["merged"], 1)

            dve.wait_ge(s["xr"], 16 * NT)
            for T in range(NT):
                n = ROWS[T]
                b0 = (2 * T + 6) % 8
                dve.wait_ge(s["wo_mm"], T + 1)
                TT(h_rows[0:n, T, :].rearrange("p (h t) -> p h t", h=2),
                   x_rows[0:n, T, :].rearrange("p (h t) -> p h t", h=2), bank[0:n, b0:b0 + 2, :], ALU.add
                   ).then_inc(s["h"], 1)
            dve.wait_ge(s["gain2"], 16)
            dve.wait_ge(s["hrms"], NT)
            for T in range(NT):
                n = ROWS[T]
                then(dve.reciprocal(stat[0:n, 37 + T:38 + T], stat[0:n, 37 + T:38 + T]))
                STT(out=hn_rows[0:n, T, :], in0=h_rows[0:n, T, :], scalar=stat[0:n, 37 + T:38 + T],
                    in1=gain2[0:n, :], op0=ALU.mult, op1=ALU.mult).then_inc(s["hn"], 1)

            then(dve.memset(lg, 0.0))
            dve.wait_ge(s["lg"], NT)
            for T in range(NT):
                last = TT(lg[0:ROWS[T], T, :], b_route[0:ROWS[T], :], bank[0:ROWS[T], 4, T * 36:T * 36 + 36], ALU.add)
                then(last)
            gl, ell = lg[:, :, 0:NGRP], lg[:, :, NGRP:]
            gmx, kmx, pg, v1, df, e2x, v2, k2, gs, de = r5[0], r5[1], r5[2], r5[3], r5[4], r5[5], r5[6], r5[7], \
                r5[8], r5[9]

            def over5(x, n):
                return x.unsqueeze(1).to_broadcast([P, NT, n])

            def first_max(out, x, mx, key, rev, n, kbest):
                then(dve.tensor_reduce(mx, x, AX, ALU.max))
                then(TT(key, x, wide(mx, 2, (NT, n)), ALU.is_equal))
                then(TT(key, key, over5(rev, n), ALU.mult))
                then(dve.tensor_reduce(kbest, key, AX, ALU.max))
                then(TT(out, over5(rev, n), wide(kbest, 2, (NT, n)), ALU.is_equal))

            first_max(og, gl, gmx, eq4, c["rev4"], NGRP, kmx)
            TT(ex4, gl, wide(gmx, 2, (NT, NGRP)), ALU.subtract).then_inc(s["gmax"], 1)
            el4 = el.rearrange("p t (g e) -> p t g e", g=NGRP)
            shape4 = (NT, NGRP, EPG)
            then(TT(el4, ell.rearrange("p t (g e) -> p t g e", g=NGRP), wide(og, 3, shape4), ALU.mult),
                 TS(eq4, og, BIG, -BIG, ALU.mult, ALU.add))
            then(TT(el4, el4, wide(eq4, 3, shape4), ALU.add))
            first_max(m12[0], el, v1, eq32, c["rev32"], NE, kmx)
            then(STT(out=el, in0=m12[0], scalar=-2 * BIG, in1=el, op0=ALU.mult, op1=ALU.add))
            first_max(m12[1], el, v2, eq32, c["rev32"], NE, k2)
            TT(df, v2, v1, ALU.subtract).then_inc(s["gmax"], 1)
            valid = wide(c["valid"], 2, (NT, NE))
            then(*[TT(m, m, valid, ALU.mult) for m in m12])
            then(TT(chosen, m12[0], m12[1], ALU.add))
            dve.sem_inc(s["chosen"], 1)
            dve.wait_ge(s["gexp"], 1)
            then(dve.tensor_reduce(gs, ex4, AX, ALU.add))
            dve.wait_ge(s["gexp"], 2)
            then(dve.reciprocal(pg, gs), TS(de, e2x, 1.0, None, ALU.add))
            then(dve.reciprocal(de, de))
            then(TT(gatek[0], pg, de, ALU.mult))
            then(TT(gatek[1], gatek[0], e2x, ALU.mult))
            then(*[TT(mt, m, wide(c["tokid"], 2, (NT, NE)), ALU.mult) for mt, m in zip(mtok, m12)])
            dve.wait_ge(s["rank"], 1)
            then(dve.tensor_copy(rank.rearrange("p a b -> p (a b)"), bank[:, 5, 0:NT * NE]),
                 dve.tensor_reduce(stat[:, 52:53], bank[:, 6, 0:NE], AX, ALU.max))
            for k in range(2):
                then(TT(tmp32, m12[k], rank, ALU.mult))
                then(dve.tensor_reduce(slotk[k], tmp32, AX, ALU.add))
                then(TT(tmp32, m12[k], over5(c["yrow"], NE), ALU.mult))
                then(dve.tensor_reduce(row0[k], tmp32, AX, ALU.add))
            then(TT(over, c["passes"], stat[:, 52:53].to_broadcast([P, MAXP]), ALU.is_lt))
            then(dve.tensor_reduce(stat[:, 53:54], over, AX, ALU.add))
            dve.tensor_copy(n_pass[:, :], stat[0:1, 53:54]).then_inc(s["npass"], 1)
            dve.wait_ge(s["npass"], 1)
            n_p = dve.value_load(n_pass[0:1, 0:1], min_val=1, max_val=MAXP)
            with dve.Fori(0, n_p) as p:
                for k in range(2):
                    TT(hot[k], over5(c["slot"], CAP), wide(slotk[k], 2, (NT, CAP)), ALU.is_equal
                       ).then_inc(s["rtab"], 1)
                dve.wait_ge(s["rtab"], p * 12 + 2)
                dve.sem_inc(s["hot"], 1)
                for k in range(2):
                    dve.tensor_reduce(inpass[k], hot[k], AX, ALU.add).then_inc(s["rtab"], 1)
                    TT(row_now[k], row0[k], slotk[k], ALU.add).then_inc(s["rtab"], 1)
                dve.wait_ge(s["rtab"], p * 12 + 6)
                for k in range(2):
                    TT(row_now[k], row_now[k], inpass[k], ALU.mult).then_inc(s["rtab"], 1)
                    TT(gate_now[k], gatek[k], inpass[k], ALU.mult).then_inc(s["rtab"], 1)
                    TS(slotk[k], slotk[k], -float(CAP), None, ALU.add).then_inc(s["rtab"], 1)
                dve.wait_ge(s["rtab"], p * 12 + 12)
                for k in range(2):
                    dve.tensor_copy(y_rows[:, k, :], row_now[k]).then_inc(s["yrow"], 1)
                dve.wait_ge(s["idxmm"], p + 1)
                dve.tensor_copy(gather_rows[:, :], bank[0:CAP, 7, 0:NE]).then_inc(s["idx"], 1)
                with dve.Fori(0, NE // 2) as e2:
                    for u in range(2):
                        step = p * NE + e2 * 2
                        dve.wait_ge(s["xt"], step + (u + 3))
                        dve.wait_ge(s["gu"], step + (u + 1))
                        dve.tensor_copy(xgT[u].rearrange("p a b -> p (a b)"), bank[:, u, :]).then_inc(s["xc"], 1)
                        dve.wait_ge(s["sg"], step + (u + 1))
                        dve.wait_ge(s["y"], step + (u + 1))
                        TT(hT[u].rearrange("p a b -> p (a b)"), sg[u].rearrange("p a b -> p (a b)"),
                           bank[:, 2 + u, FT * CAP:2 * FT * CAP], ALU.mult).then_inc(s["hT"], 1)

                for T in range(NT):
                    n = ROWS[T]
                    per = 96 if T % 2 == 0 else 64
                    dve.wait_ge(s[f"yk{T % 2}"], p * per + 32 * (T // 2 + 1))
                    STT(out=h_rows[0:n, T, :], in0=yk[T % 2][0][0:n, :], scalar=gate_now[0][0:n, T:T + 1],
                        in1=h_rows[0:n, T, :], op0=ALU.mult, op1=ALU.add).then_inc(s["fadd"], 1)
                    dve.wait_ge(s["fadd"], p * NT + (T + 1))
                    STT(out=h_rows[0:n, T, :], in0=yk[T % 2][1][0:n, :], scalar=gate_now[1][0:n, T:T + 1],
                        in1=h_rows[0:n, T, :], op0=ALU.mult, op1=ALU.add).then_inc(s["fsum"], 1)

            dve.wait_ge(s["gainf"], 16)
            for T in range(NT):
                n = ROWS[T]
                dve.wait_ge(s["frms"], T + 1)
                then(dve.reciprocal(stat[0:n, 47 + T:48 + T], stat[0:n, 47 + T:48 + T]))
                STT(out=fin[T % 2][0:n, :], in0=h_rows[0:n, T, :], scalar=stat[0:n, 47 + T:48 + T],
                    in1=gain_f[0:n, :], op0=ALU.mult, op1=ALU.mult).then_inc(s["fin"], 1)


def shape_constants():
    c = {}
    i = np.arange(P)
    c["ident"] = np.eye(P)
    c["triu"] = (i[:, None] < i[None, :])
    c["ones"] = np.ones((P, P))
    c["smask"] = (i[:, None] // SCH == np.arange(CH)[None, :])
    row = np.arange(64)
    used = (row % 32) < 16
    esel = np.zeros((P, NB))
    esel[0:64] = (row[:, None] % 8 == np.arange(NB)[None, :]) & used[:, None]
    c["esel"] = esel
    c["rev4"] = np.tile(NGRP - np.arange(NGRP), (P, 1))
    c["rev32"] = np.tile(NE - np.arange(NE), (P, 1))
    c["yrow"] = np.tile(np.arange(NE) * CAP, (P, 1))
    c["slot"] = np.tile(np.arange(CAP), (P, 1))
    c["tokid"] = i[:, None] + P * np.arange(NT)[None, :]
    c["valid"] = c["tokid"] < TOK
    c["passes"] = np.tile(CAP * np.arange(MAXP), (P, 1))
    dec = np.zeros((P, NG, P))
    for r in row[used]:
        h = 2 * (r % 32 // 8) + r // 32
        for g in range(NG):
            dec[r, g] = -slope(g * NH + h) / ATT_SCALE * DILS[g] * (P - np.arange(P))
    c["decbias"] = dec.reshape(P, NG * P)
    c["eps"] = np.full((P, 1), EPS)
    consts = np.concatenate([np.asarray(c[n], np.float32).reshape(P, w) for n, w in CONSTS], axis=1)
    a, b = i[:, None], i[None, :]
    d0 = np.empty((P, NCLS, NCLS, P))
    for r in range(NCLS):
        for k in range(NCLS):
            dist = 4 * (a - b) + r - k
            d0[:, r, k] = np.where((dist >= 0) & (dist <= WINDOWS[0]), dist, BIG)
    ratio = [2.0 ** (-8.0 * g * NH / (NG * NH)) for g in range(NG)]
    dist = 4 * (a - b)
    d1 = np.where(dist >= 0, dist * ratio[1], BIG)
    d2 = np.where((dist >= 0) & (dist % DILS[2] == 0), dist * ratio[2], BIG)
    return (consts, d0.reshape(P, NCLS, SEQ).astype(np.float32),
            np.concatenate([d1, d2], axis=1).astype(np.float32))


def kernel(**inputs):
    import concourse.bacc as bacc
    from concourse.bass_utils import run_bass_kernel_spmd as run

    v = {k: np.asarray(a) for k, a in inputs.items()}
    a = {}

    def feat(w):
        return w.reshape(-1, P, w.shape[-1]).transpose(1, 0, 2)

    def states(x):
        lead = x.shape[:-2]
        y = x.reshape(lead + (NJ, P))
        return np.moveaxis(y, -1, 0)

    xp, xs = v["x_prompt"][0], v["x_sample"][:, 0]
    xcols = np.concatenate([xp.reshape(P, NCLS, D).transpose(1, 0, 2).reshape(SEQ, D), xs], axis=0)
    a["xT"] = xcols.T.reshape(KT, P, TOK).transpose(1, 0, 2)
    a["x_prompt"], a["x_sample"] = xp, xs
    a["memT"] = feat(v["mem_prompt"][0].T)
    w_in = v["w_in"][0]
    ssm0, mq0, gate0 = NG * 3 * ATT, NG * 3 * ATT + SSMW, NG * 3 * ATT + SSMW + MH * MD
    cols = [w_in[:, ssm0:mq0], w_in[:, 0:ssm0], w_in[:, mq0:gate0], v["w_mk"][0], v["w_mv"][0],
            w_in[:, gate0:].reshape(D, 3, KT, P).transpose(0, 2, 1, 3).reshape(D, 3 * D)]
    stream = np.concatenate(cols, axis=1)
    a["w_stream"] = stream.reshape(KT, P, -1, P).transpose(2, 1, 0, 3)
    a["consts"], a["dist0"], a["dist12"] = shape_constants()
    a["gain1"], a["gain_mem"] = v["norm1"][0].reshape(KT, P).T, v["norm_mem"][0].reshape(KT, P).T
    a["norm2"], a["norm_f"] = v["norm2"][0], v["norm_f"]
    ldt = np.broadcast_to(v["log_dt"][0][:, None], (SG, SST))
    a["ssm_in"] = np.stack([states(x) for x in (v["lam_re"][0], v["lam_im"][0], ldt)], axis=1)
    a["b_in"] = np.stack([v[f"ssm_b_{x}"][0].reshape(NJ, P, SCH).transpose(1, 0, 2) for x in ("re", "im")], axis=1)
    a["c_in"] = np.stack([v[f"ssm_c_{x}"][0].transpose(0, 2, 1).reshape(NJ, P, SCH).transpose(1, 0, 2)
                          for x in ("re", "im")], axis=1)
    a["h0"] = np.stack([states(v[f"state_ssm_{x}"][0]).transpose(0, 2, 1) for x in ("re", "im")], axis=1)
    a["ssm_d"], a["b_glu"] = v["ssm_d"][0].reshape(4, P).T, v["b_glu"][0].reshape(4, P).T
    a["w_glu"], a["w_att"], a["w_ssm"] = feat(v["w_glu"][0]), feat(v["w_att_out"][0]), feat(v["w_ssm_out"][0])
    a["w_mem"], a["w_o"] = feat(v["w_mem_out"][0]), feat(v["w_o"][0])
    a["w_route"] = feat(np.concatenate([v["w_grp"][0], v["w_exp"][0]], axis=1))
    a["b_route"] = np.concatenate([v["b_grp"][0], v["b_exp"][0]])
    a["w1"], a["w3"], a["w2"] = v["w1"][0], v["w3"][0], v["w2"][0]
    keys = []
    for g in range(NG):
        for kv in "kv":
            a[f"cache_swa{g}_{kv}"] = v[f"cache_swa{g}_{kv}"][0].reshape(NB, WINDOWS[g], ATT)
        k = v[f"cache_swa{g}_k"][0][:, ::DILS[g]]
        keys.append(k.reshape(NB, P, 2, 2, DH).transpose(0, 3, 4, 2, 1).reshape(NB, P, 2, P))
    a["k_dec"] = np.stack(keys, axis=2)
    a["mk_dec"] = v["cache_mem_k"][0].transpose(0, 3, 2, 1)
    a["cache_mem_v"] = v["cache_mem_v"][0].reshape(NB, MEM, MH * MD)

    outs = {"y_prompt": (SEQ, D), "y_sample": (NB, D), "prompt_mem_k": (MEM, MH * MD),
            "prompt_mem_v": (MEM, MH * MD), "st_prompt": (P, 2, NJ), "st_dec": (P, 2, NJ, NB)}
    for g in range(NG):
        for kv in "kv":
            outs[f"prompt_swa{g}_{kv}"] = (min(WINDOWS[g], SEQ), ATT)
            outs[f"sample_swa{g}_{kv}"] = (NB, WINDOWS[g], ATT)

    nc = bacc.Bacc("TRN2", target_bir_lowering=False, num_devices=1)
    arrays, t = {}, {}
    for name, x in a.items():
        x = np.ascontiguousarray(x)
        arrays["in_" + name] = x
        t[name] = nc.dram_tensor("in_" + name, x.shape, F32, kind="ExternalInput").ap()
    for name, shape in outs.items():
        t[name] = nc.dram_tensor("out_" + name, shape, F32, kind="ExternalOutput").ap()
    t["hn_dram"] = nc.dram_tensor("hn_dram", (TOK, D), F32).ap()
    t["y_dram"] = nc.dram_tensor("y_dram", (NE * CAP, D), F32).ap()
    t["y_slots"] = t["y_dram"].rearrange("(e s) d -> e s d", e=NE)
    build(nc, t)
    got = run(nc, [arrays], core_ids=[0]).results[0]
    o = {name: got["out_" + name] for name in outs}

    def swa(kind, g, kv):
        x = o[f"{kind}_swa{g}_{kv}"]
        return x.reshape(1, 1 if kind == "prompt" else NB, -1, NH, DH)

    def st_p(i):
        return np.ascontiguousarray(o["st_prompt"][:, i].T).reshape(1, 1, SG, SST)

    def st_d(i):
        return np.ascontiguousarray(o["st_dec"][:, i].transpose(2, 1, 0)).reshape(1, NB, SG, SST)

    return (o["y_prompt"].reshape(1, SEQ, D), o["y_sample"].reshape(NB, 1, D),
            *[swa("prompt", g, kv) for g in range(NG) for kv in "kv"],
            o["prompt_mem_k"].reshape(1, 1, MEM, MH, MD), o["prompt_mem_v"].reshape(1, 1, MEM, MH, MD),
            st_p(0), st_p(1),
            *[swa("sample", g, kv) for g in range(NG) for kv in "kv"],
            st_d(0), st_d(1))
```

```python
from contextlib import ExitStack

import concourse.bass as bass
import numpy as np
from concourse import mybir

F32 = mybir.dt.float32
U32 = mybir.dt.uint32
I32 = mybir.dt.int32
ALU = mybir.AluOpType
ACT = mybir.ActivationFunctionType
AX = mybir.AxisListType.X

P = 128
D = 1024
KT = D // P
SEQ, NB = 512, 8
TOK = SEQ + NB
HALF = TOK // 2
NCLS = 4
WINDOWS = (128, 512, 2048)
DILS = (1, 4, 16)
NG, NH, DH = 3, 4, 64
ATT = NH * DH
SSMW, SG, SCH, SST = 512, 32, 16, 64
NJ = SG * SST // P
CH = 8
NCH = SEQ // CH
YC = NCH + NB
XC = YC + NB
LEVELS = 6
MEM, MH, MD = 256, 4, 128
NE, NGRP, EPG, FE = 32, 4, 8, 512
FT = FE // P
CAP = 64
SSM_BANK = (6, 6, 6, 0, 2, 0, 2, 0)
NSLOT = 4
MAXP = -(-TOK // CAP)
NT = 5
ROWS = (P, P, P, P, NB)
EPS = 1e-6
BIG = 1e30
ATT_SCALE = DH ** -0.5
MEM_SCALE = MD ** -0.5
TWO_PI = 2 * np.pi
ROUND = 1.5 * 2.0 ** 23
PI_A = 6.28125
PI_B = float(np.float32(np.floor((TWO_PI - PI_A) * 2 ** 22) / 2 ** 22))
PI_C = float(np.float32(TWO_PI - PI_A - PI_B))

T_QKV, T_MQ = 4, 22
N_EARLY = 12
N_PROJ, N_MEMT, N_GATE = 26, 8, 24
N_FIRST = N_PROJ + N_MEMT

KB = 256
XN = 13
PROJ = 30
RING = 83
S5 = 91
MK = 187
TOTAL_KB = 207
WBUF = (S5 + 48, S5)

CONSTS = (("ident", P), ("triu", P), ("ones", P), ("smask", CH), ("esel", NB), ("rev4", NGRP),
          ("rev32", NE), ("yrow", NE), ("slot", CAP), ("tokid", NT), ("valid", 1),
          ("passes", MAXP), ("decbias", NG * P), ("eps", 1))
NCONST = sum(n for _, n in CONSTS)


def slope(h):
    return float(2.0 ** (-8.0 * (h + 1) / (NG * NH)))


def wait_from(eng, s, n):
    if n > 0:
        eng.wait_ge(s, n)


def build(nc, t):
    with ExitStack() as ctx:
        arena = ctx.enter_context(nc.sbuf_tensor("arena", [P, TOTAL_KB * KB], F32))
        bank = ctx.enter_context(nc.psum_tensor("bank", [P, 8, 512], F32))
        gather_rows = ctx.enter_context(nc.sbuf_tensor("gather_rows", [CAP, NE], U32))
        gather_cur = ctx.enter_context(nc.sbuf_tensor("gather_cur", [CAP, 2], U32))
        y_rows = ctx.enter_context(nc.sbuf_tensor("y_rows", [P, 2, NT], U32))
        n_pass = ctx.enter_context(nc.sbuf_tensor("n_pass", [1, 1], I32))

        def sem(name):
            return ctx.enter_context(nc.semaphore(name))

        def view(lo, dims):
            n = int(np.prod(dims))
            assert lo + n <= TOTAL_KB * KB, (lo, dims)
            v = arena[:, lo:lo + n]
            if len(dims) > 1:
                names = "abcd"[:len(dims)]
                v = v.rearrange(f"p ({' '.join(names)}) -> p {' '.join(names)}",
                                **dict(zip(names, dims)))
            return v

        def at(kb, *dims):
            return view(int(round(kb * KB)), dims)

        top = [0]

        def keep(*dims):
            v = view(top[0], dims)
            top[0] += int(np.prod(dims))
            assert top[0] <= XN * KB
            return v

        cst = keep(NCONST)
        c, o = {}, 0
        for name, n in CONSTS:
            c[name] = cst[:, o:o + n]
            o += n
        ident, ones, eps_ap = c["ident"], c["ones"], c["eps"]
        dist12 = keep(2 * P)
        ssm_in = keep(3, NJ)
        par = keep(24, NJ)
        dec_cols = keep(N_PROJ, NB)
        stat = keep(64)
        gain1, gain_mem = keep(KT), keep(KT)
        ssm_d, b_glu = keep(4), keep(4)
        apow = keep(2, LEVELS, NJ)
        st_prompt = keep(2, NJ)
        st_dec = keep(2, NJ, NB)
        h0 = keep(2, NJ, NB)
        w_route = keep(KT, NGRP + NE)
        b_route = keep(NGRP + NE)

        xn = at(XN, KT, TOK)
        proj = at(PROJ, N_PROJ, TOK)
        ring = [at(RING, KT, P), at(RING + 4, KT, P)]
        cw = at(S5, 2, NJ, CH + 1, SCH)
        state_in = at(S5 + 18, 2, NJ, P)
        toep = at(S5 + 34, 2, NJ, P)
        ctmp = [at(S5 + 34, NJ * (CH + 1) * SCH), at(S5 + 43, NJ * (CH + 1) * SCH)]
        ba = at(S5 + 52, 2, NJ, CH, SCH)
        brep = at(S5 + 68, 2, NJ, CH, SCH)
        kern = at(S5 + 52, 2, NJ, P)
        b_in, c_in = at(S5 + 84, 2, NJ, SCH), at(S5 + 86, 2, NJ, SCH)
        bbar = at(S5 + 88, 2, NJ, SCH)
        pw = at(S5 + 90, 2, NJ, CH + 1)
        rpw = at(S5 + 91.25, 2, NJ, CH)
        ucomb = at(S5 + 68, 4, CH, XC)
        utok = at(S5 + 78, SG, CH, SCH)
        uch = at(S5 + 52, SG, XC)
        xst = at(S5 + 68, 2, NJ, XC)
        stmp = [at(S5 + 78 + 4 * i, NJ * (NCH - 1)) for i in range(4)]
        sprev = at(S5 + 18, 2, NJ, YC)
        ytok = at(S5 + 78, CH, SSMW)
        ycol = at(S5 + 68, 4, TOK)
        zcol = at(S5, 4, TOK)
        glu = at(S5 + 9, 4, TOK)
        w_glu = at(MK, 4, SSMW)
        xraw = at(S5, KT, TOK)
        sq, sqm = at(S5 + 34, KT, TOK), at(MK + 8, KT, MEM)
        rms, rmsm = at(S5 + 60, TOK), at(MK + 16, MEM)
        memn = at(MK, KT, MEM)
        mkv = at(MK + 8, 2 * MH, MEM)
        mk_rows = at(MK + 12, 2, MH * MD)
        mv_rows = at(MK + 16, 2, MH * MD)
        gates = at(S5, N_GATE, TOK)
        v_rows = at(S5 + 49, NG, NCLS, ATT)
        attT = at(S5 + 61, 2, TOK)
        memT = at(S5 + 65.25, MH, TOK)
        ssmT = at(S5 + 73.5, 4, TOK)
        k_rows = [at(S5 + x, NCLS, ATT) for x in (82, 86, 18)]
        kv_dec = at(S5 + 90, NG, 2, ATT)
        dist0 = at(PROJ, NCLS, SEQ)
        work = S5 + 82
        sc = at(work, 6 * P)
        pr = at(work + 3, 6 * P)
        prT = at(MK, 6 * P)
        pm = [at(work, MEM), at(work + 1, MEM)]
        pmT = [at(MK + 4, MEM), at(MK + 5, MEM)]
        slot = [PROJ + 16 + 7 * i for i in range(NSLOT)]
        slot_k = [at(x, NG, 2, P) for x in slot]
        slot_mk = [at(x + 3, MH, MEM) for x in slot]
        slot_v = [at(x, NG, ATT) for x in slot]
        slot_mv = [at(x + 3, 2, MH * MD) for x in slot]
        dq = at(S5 + 49, NG, 2, NB * 32)
        dmq = at(S5 + 55, MH, NB * 32)
        newprod = at(XN + 16.25, NG, 2, 32)
        dsc = at(S5 + 59, NG * P + NG)
        dm = at(work + 6, MEM)
        dpd = at(work + 7, NG, 64)
        dpn = at(MK + 16, NG, 64)
        dpv = at(work, NG, 64 * NB)
        dmpv = at(PROJ + 45, 2, MH, 32 * NB)
        do_rows, dmo_rows = at(S5 + 59, P), at(work + 6, P)
        w_att, w_ssm, w_mem = at(RING, 2, D), at(PROJ, 4, D), at(XN, 4, D)
        w_o = [at(PROJ + 20, 4, D), at(MK, 4, D)]
        x_rows = at(PROJ + 40, NT, D)
        h_rows = at(PROJ, NT, D)
        hn_rows = x_rows
        gain2 = at(MK + 16, D)
        gain_f = at(XN + 12, D)
        hnT = [at(S5 + 80, KT, P), at(S5 + 84, KT, P)]
        rtop = [0]

        def rt(*dims):
            v = view((PROJ + 20) * KB + rtop[0], dims)
            rtop[0] += int(np.prod(dims))
            assert rtop[0] <= 12 * KB
            return v

        lg = rt(NT, NGRP + NE)
        r5 = [rt(NT) for _ in range(12)]
        og, eq4, ex4 = rt(NT, NGRP), rt(NT, NGRP), rt(NT, NGRP)
        el, eq32, tmp32, rank = (rt(NT, NE) for _ in range(4))
        m12 = [rt(NT, NE), rt(NT, NE)]
        mtok = [rt(NT, NE), rt(NT, NE)]
        chosen, count, over = rt(NT, NE), rt(NT, NE), rt(MAXP)
        slotk = [rt(NT), rt(NT)]
        gatek = [rt(NT), rt(NT)]
        row0 = [rt(NT), rt(NT)]
        inpass = [rt(NT), rt(NT)]
        gate_now = [rt(NT), rt(NT)]
        row_now = [rt(NT), rt(NT)]
        hot = [rt(NT, CAP), rt(NT, CAP)]
        wb = [(at(b, 2, KT, FE), at(b + 32, 2, 2, D)) for b in WBUF]
        xg = [at(MK, D), at(MK + 4, D)]
        xgT = [at(MK + 8, KT, CAP), at(MK + 10, KT, CAP)]
        hT = [at(MK + 12, 2, P), at(MK + 13, 2, P)]
        sg = [at(MK + 14, FE // 2), at(MK + 15, FE // 2)]
        hidden = [at(MK + 16, FE // 2), at(MK + 17, FE // 2)]
        y_sb = [at(XN, D // 2), at(XN + 2, D // 2)]
        yk = [[at(PROJ + x, D) for x in pair] for pair in ((40, 44), (48, 52), (56, 36))]
        squares = at(PROJ + 32, D)

        names = ("cst", "ssmp", "x0", "x1", "gain1", "xraw", "uscaled", "mem", "win0", "win1", "small", "wglu",
                 "dist0", "wssm", "wout", "wo", "xr", "xr_last", "gain2", "gainf", "dt", "lrdt", "trig", "sq",
                 "ss", "rms", "xn", "mn", "tile", "evac", "vchain", "cplx", "job", "jobfree", "toep", "ucomb",
                 "sprev", "states", "yadd", "z", "ssm", "krows", "kout", "krest", "out", "S", "T", "nmax",
                 "exp", "pn", "PT", "ptc", "O", "oc", "gevac", "gsig", "mS", "mnmax", "mexp", "mpn", "mPT",
                 "mptc", "mO", "moc", "dprod", "dkdone", "dnmax", "dexp", "dpd", "dback", "dbackc", "dvdone",
                 "dout", "dturn", "doc", "Sj", "Sfree", "Pj", "Pfree", "merged", "wo_mm", "h_moved", "h", "hss",
                 "hrms", "hn", "hnout", "ht", "hnT", "lg", "gmax", "gexp", "chosen", "rank", "rtab", "npass",
                 "hot", "idxmm", "idx", "xg0", "xg1", "cur", "xt", "xc", "w1x", "gu", "sg", "hid", "ht2", "hT", "y",
                 "yc", "yo0", "yo1", "w13_0", "w13_1", "w2_0", "w2_1", "yk0", "yk1", "yk2", "fsum", "fadd",
                 "yrow", "fss", "frms", "fin", "fout")
        s = {n: sem("s_" + n) for n in names + ("held",)}
        kdec = [sem(f"s_kdec{i}") for i in range(NSLOT)]
        vdec = [sem(f"s_vdec{i}") for i in range(NSLOT)]

        block = ctx.enter_context(nc.Block())

        class Jobs:
            def __init__(self):
                self.n = 0

            def take_pe(self, pe):
                wait_from(pe, s["jobfree"], self.n - 3)
                self.n += 1
                return bank[:, 4 + (self.n - 1) % 4, :]

            def take_act(self, act):
                act.wait_ge(s["job"], self.n + 1)
                self.n += 1
                return bank[:, 4 + (self.n - 1) % 4, :]

        J_ST = NJ * 2 // 4
        J_K = SG // 4
        J_UC = 4 * CH // 4
        J_U = -(-SG // 6)
        J_X = 2 * 3
        J_Y = SG // 4
        J_YT = 4 * 2
        J_GLU = 4 * 2
        E_ST = J_ST
        E_K = E_ST + J_K
        E_UC = E_K + J_UC
        E_U = E_UC + J_U
        E_X = E_U + J_X
        E_Y = E_X + J_Y
        E_YT = E_Y + J_YT
        J_KV = NG * 2 * NCLS
        E_KV = E_YT + J_KV
        E_KVD = E_KV + NG
        E_MEM = E_KVD + 4
        E_GLU = E_MEM + J_GLU
        KV = [(g, kv, r) for g in range(NG) for kv in (0, 1) for r in range(NCLS)]

        def load_keys(eng, b):
            i = b % NSLOT
            eng.dma_start(slot_k[i], t["k_dec"][b]).then_inc(kdec[i], 16)
            eng.dma_start(slot_mk[i], t["mk_dec"][b]).then_inc(kdec[i], 16)

        @block.sync
        def _(sp):
            def load_w13(u, e, n):
                for i, (name, used) in enumerate((("w1", "w1x"), ("w3", "gu"))):
                    sp.wait_ge(s[used], n * 2 + 2)
                    sp.dma_start(wb[u][0][:, i], t[name][bass.ds(e, 1)].rearrange(
                        "o (p k) f -> p (o k) f", p=P)).then_inc(s[f"w13_{u}"], 16)

            def load_w2(u, e, n):
                sp.wait_ge(s["y"], n * 2 + 2)
                sp.dma_start(wb[u][1], t["w2"][bass.ds(e, 1)].rearrange(
                    "o (q p j) d -> p (o q) j d", q=2, p=P)).then_inc(s[f"w2_{u}"], 16)

            def load_expert(u, e, n):
                load_w13(u, e, n)
                load_w2(u, e, n)

            sp.dma_start(ssm_in, t["ssm_in"]).then_inc(s["ssmp"], 16)
            for half in range(2):
                k = slice(half * KT // 2, (half + 1) * KT // 2)
                sp.dma_start(xraw[:, k], t["xT"][:, k]).then_inc(s[f"x{half}"], 16)
                if half == 0:
                    sp.dma_start(cst, t["consts"]).then_inc(s["cst"], 16)
            with sp.Fori(0, (N_FIRST + N_GATE) // 2) as i2:
                for u in range(2):
                    sp.wait_ge(s["tile"], i2 * 2 + (u + 1))
                    sp.dma_start(ring[u], t["w_stream"][bass.ds(i2 * 2 + u, 1)].rearrange(
                        "o p k c -> (o p) k c")).then_inc(s[f"win{u}"], 16)
            for b in range(NSLOT, NB):
                sp.wait_ge(s["dkdone"], MH * (b - NSLOT + 1))
                load_keys(sp, b)
            for b in range(NB):
                i = b % NSLOT
                if b < NSLOT:
                    sp.wait_ge(s["dkdone"], MH * (b + NSLOT + 1))
                else:
                    sp.wait_ge(s["dvdone"], MH * (b - NSLOT + 1))
                for g in range(NG):
                    rows = t[f"cache_swa{g}_v"][b].rearrange("(m q) c -> m q c", q=DILS[g])[:, 0, :]
                    sp.dma_start(slot_v[i][:, g, :], rows).then_inc(vdec[i], 16)
                sp.dma_start(slot_mv[i], t["cache_mem_v"][b].rearrange("(k p) c -> p k c", p=P)
                             ).then_inc(vdec[i], 16)
                if b == NSLOT - 1:
                    sp.dma_start(w_att, t["w_att"]).then_inc(s["wout"], 16)
                    sp.dma_start(w_mem, t["w_mem"]).then_inc(s["wout"], 16)
            sp.wait_ge(s["krest"], 16 * (2 * NG + 2))
            sp.dma_start(w_o[1], t["w_o"][:, 4:8, :]).then_inc(s["wo"], 16)
            sp.wait_ge(s["dvdone"], MH * NB)
            sp.dma_start(w_o[0], t["w_o"][:, 0:4, :]).then_inc(s["wo"], 16)
            for T in range(3):
                sp.dma_start(x_rows[:, T, :], t["x_prompt"].rearrange("(a r) c -> r a c", r=NCLS)[T]
                             ).then_inc(s["xr"], 16)
            sp.dma_start(gain2, t["norm2"].partition_broadcast(P)).then_inc(s["gain2"], 16)
            sp.wait_ge(s["merged"], KT)
            sp.dma_start(x_rows[:, 3, :], t["x_prompt"].rearrange("(a r) c -> r a c", r=NCLS)[3]
                         ).then_inc(s["xr_last"], 16)
            sp.dma_start(x_rows[0:NB, 4, :], t["x_sample"]).then_inc(s["xr_last"], 16)
            load_w13(0, 0, 0)
            sp.dma_start(gain_f, t["norm_f"].partition_broadcast(P)).then_inc(s["gainf"], 16)

            def store_normed(T):
                sp.wait_ge(s["hn"], T + 1)
                sp.dma_start(t["hn_dram"][T * P:T * P + ROWS[T], :], hn_rows[0:ROWS[T], T, :]
                             ).then_inc(s["hnout"], 16)

            for T in range(NT - 1):
                store_normed(T)
            sp.wait_ge(s["wo_mm"], NT + 1)
            load_w13(1, 1, 1)
            store_normed(NT - 1)
            sp.wait_ge(s["lg"], NT)
            load_w2(0, 0, 0)
            load_w2(1, 1, 1)
            with sp.Fori(0, NE // 2 - 1) as e2:
                for u in range(2):
                    load_expert(u, e2 * 2 + (u + 2), e2 * 2 + (u + 2))
            sp.wait_ge(s["npass"], 1)
            n_p = sp.value_load(n_pass[0:1, 0:1], min_val=1, max_val=MAXP)
            with sp.If(n_p > 1):
                with sp.Fori(1, n_p) as p:
                    with sp.Fori(0, NE // 2) as e2:
                        for u in range(2):
                            load_expert(u, e2 * 2 + u, p * NE + e2 * 2 + u)
            for T in range(NT):
                sp.wait_ge(s["fin"], T + 1)
                if T < 4:
                    sp.dma_start(t["y_prompt"].rearrange("(a r) c -> r a c", r=NCLS)[T], h_rows[:, T, :]
                                 ).then_inc(s["fout"], 16)
                else:
                    sp.dma_start(t["y_sample"], h_rows[0:NB, T, :]).then_inc(s["fout"], 16)
            sp.wait_ge(s["fout"], 16 * NT)

        @block.gpsimd
        def _(pool):
            def shift_caches(b0, b1, first):
                with pool.Fori(0, b1 - b0) as i:
                    for part, (groups, kv) in enumerate((((2,), "k"), ((0, 1), "k"), ((2,), "v"), ((0, 1), "v"))):
                        pool.wait_ge(s["tile"], i * 4 + (2 + first + part))
                        pool.sem_inc(s["held"], 1)
                        for g in groups:
                            n = (WINDOWS[g] - 1) * ATT
                            src = t[f"cache_swa{g}_{kv}"][bass.ds(i + b0, 1)].rearrange("o m c -> o (m c)")
                            dst = t[f"sample_swa{g}_{kv}"][bass.ds(i + b0, 1)].rearrange("o m c -> o (m c)")
                            pool.dma_start(dst[:, 0:n].rearrange("o (q x) -> (o q) x", q=16),
                                           src[:, ATT:ATT + n].rearrange("o (q x) -> (o q) x", q=16)
                                           ).then_inc(s["out"], 16)

            pool.dma_start(gain1, t["gain1"]).then_inc(s["gain1"], 16)
            for dst, name in ((b_in, "b_in"), (c_in, "c_in"), (h0, "h0")):
                pool.dma_start(dst, t[name]).then_inc(s["small"], 16)
            pool.dma_start(memn, t["memT"]).then_inc(s["mem"], 16)
            for dst, name in ((gain_mem, "gain_mem"), (ssm_d, "ssm_d"), (b_glu, "b_glu"),
                              (dist12, "dist12"), (w_route, "w_route")):
                pool.dma_start(dst, t[name]).then_inc(s["small"], 16)
            pool.dma_start(b_route, t["b_route"].partition_broadcast(P)).then_inc(s["small"], 16)

            shift_caches(0, 2, 3)
            pool.wait_ge(s["job"], E_K)
            pool.memset(ucomb, 0.0).then_inc(s["ucomb"], 1)
            pool.wait_ge(s["uscaled"], 1)
            pool.wait_ge(s["ucomb"], 1)
            for k in range(CH):
                lo = (k % NCLS) * P + k // NCLS
                pool.tensor_copy(ucomb[:, :, k, 0:NCH], proj[:, 0:4, lo:lo + P - 1:2]).then_inc(s["ucomb"], 1)
            pool.tensor_copy(ucomb[:, :, 0, NCH:YC], proj[:, 0:4, SEQ:TOK]).then_inc(s["ucomb"], 1)
            pool.tensor_copy(ucomb[:, :, CH - 1, YC:XC], proj[:, 0:4, SEQ:TOK]).then_inc(s["ucomb"], 1)

            shift_caches(2, 4, N_EARLY + 2)
            pool.wait_ge(s["tile"], 2 + N_FIRST)
            pool.dma_start(w_glu, t["w_glu"]).then_inc(s["wglu"], 16)
            pool.wait_ge(s["states"], 3)
            pool.dma_start(t["st_prompt"], st_prompt).then_inc(s["out"], 16)
            pool.dma_start(t["st_dec"], st_dec).then_inc(s["out"], 16)
            pool.wait_ge(s["yadd"], 4)
            pool.dma_start(dist0, t["dist0"]).then_inc(s["dist0"], 16)
            for g in range(NG):
                for kv, name in ((0, "k"), (1, "v")):
                    pool.wait_ge(s["krows"], 2 * g + kv + 1)
                    src = k_rows[g] if kv == 0 else v_rows[:, g]
                    keep_rows = min(WINDOWS[g], SEQ)
                    a0 = (SEQ - keep_rows) // NCLS
                    pool.dma_start(t[f"prompt_swa{g}_{name}"].rearrange("(a r) c -> a r c", r=NCLS),
                                   src[a0:P]).then_inc(s["kout"], 16)
            pool.wait_ge(s["krows"], 2 * NG + 1)
            for g in range(NG):
                for kv, name in ((0, "k"), (1, "v")):
                    pool.dma_start(t[f"sample_swa{g}_{name}"][:, WINDOWS[g] - 1, :], kv_dec[0:NB, g, kv, :]
                                   ).then_inc(s["krest"], 16)
            pool.wait_ge(s["krows"], 2 * NG + 2)
            pool.dma_start(t["prompt_mem_v"].rearrange("(k p) c -> p k c", p=P), mv_rows).then_inc(s["krest"], 16)
            pool.wait_ge(s["krows"], 2 * NG + 3)
            pool.dma_start(t["prompt_mem_k"].rearrange("(k p) c -> p k c", p=P), mk_rows).then_inc(s["krest"], 16)

            shift_caches(4, NB, N_FIRST + 1)

            pool.wait_ge(s["hnout"], 16 * NT)
            pool.wait_ge(s["npass"], 1)
            n_p = pool.value_load(n_pass[0:1, 0:1], min_val=1, max_val=MAXP)
            with pool.Fori(0, n_p) as p:
                pool.wait_ge(s["idx"], p + 1)
                pool.sem_inc(s["held"], 1)
                with pool.Fori(0, NE // 2) as e2:
                    for u in range(2):
                        pool.wait_ge(s["xt"], p * NE + e2 * 2 + (u + 1))
                        pool.tensor_copy(gather_cur[:, u:u + 1], gather_rows[:, bass.ds(e2 * 2 + u, 1)]
                                         ).then_inc(s["cur"], 1)
                        pool.wait_ge(s["cur"], p * NE + e2 * 2 + (u + 1))
                        pool.sem_inc(s["held"], 1)
                        pool.indirect_dma_start(
                            out=xg[u][0:CAP, :], out_offset=None, in_=t["hn_dram"],
                            in_offset=bass.IndirectOffsetOnAxis(ap=gather_cur[:, u:u + 1], axis=0)
                        ).then_inc(s[f"xg{u}"], 16)
                for u in range(2):
                    pool.wait_ge(s[f"yo{u}"], p * (16 * NE // 2) + (16 * NE // 2 + 16))
                pool.wait_ge(s["yrow"], p * 2 + 2)
                for T in range(NT):
                    pool.wait_ge(s["fsum"], p * NT + (NT + T - 2 if T >= 3 else NT))
                    pool.sem_inc(s["held"], 1)
                    for k in range(2):
                        pool.indirect_dma_start(
                            out=yk[T % 3][k][0:ROWS[T], :], out_offset=None, in_=t["y_dram"],
                            in_offset=bass.IndirectOffsetOnAxis(ap=y_rows[0:ROWS[T], k, T:T + 1], axis=0)
                        ).then_inc(s[f"yk{T % 3}"], 16)
            pool.wait_ge(s["kout"], 16 * (2 * NG))
            pool.wait_ge(s["krest"], 16 * (2 * NG + 2))
            pool.wait_ge(s["out"], 16 * (2 + 2 * NG * NB))

        @block.tensor
        def _(pe):
            pe.sem_inc(s["tile"], 2)
            pe.sem_inc(s["w1x"], 4)
            pe.sem_inc(s["gu"], 4)
            pe.sem_inc(s["y"], 4)
            pe.sem_inc(s["xt"], 2)
            pe.sem_inc(s["ht2"], 2)

            pe.wait_ge(s["cst"], 16)
            for k in range(KT):
                pe.wait_ge(s["sq"], k + 1)
                for h in range(2):
                    last = pe.matmul(bank[:, 4 + h, 0:HALF], ones, sq[:, k, h * HALF:(h + 1) * HALF],
                                     start=k == 0, stop=k == KT - 1)
            last.then_inc(s["ss"], 1)
            def x_tiles(first, count, x=xn):
                with pe.Fori(0, count // 2) as i2:
                    for u in range(2):
                        pe.wait_ge(s[f"win{u}"], i2 * 16 + (8 * first + 16))
                        pe.wait_ge(s["evac"], i2 * 2 + (first + u + 1))
                        for k in range(KT):
                            for h in range(2):
                                last = pe.matmul(bank[:, 2 * u + h, 0:HALF], ring[u][:, k, :],
                                                 x[:, k, h * HALF:(h + 1) * HALF],
                                                 start=k == 0, stop=k == KT - 1)
                        last.then_inc(s["tile"], 1)

            pe.wait_ge(s["xraw"], KT)
            x_tiles(0, T_QKV, xraw)
            for k in range(KT):
                pe.wait_ge(s["sq"], KT + k + 1)
                last = pe.matmul(bank[:, 6, 0:MEM], ones, sqm[:, k, :], start=k == 0, stop=k == KT - 1)
            last.then_inc(s["ss"], 1)

            pe.wait_ge(s["xn"], KT)
            x_tiles(T_QKV, N_EARLY - T_QKV)
            jobs = Jobs()

            pe.wait_ge(s["cplx"], 1)
            for ri in range(2):
                for j4 in range(NJ // 4):
                    b = jobs.take_pe(pe)
                    for q in range(4):
                        last = pe.transpose(b[:, q * P:(q + 1) * P], ba[:, ri, j4 * 4 + q], ident)
                    last.then_inc(s["job"], 1)
            pe.wait_ge(s["cplx"], 2)
            for j4 in range(NJ // 4):
                for odd in range(2):
                    b = jobs.take_pe(pe)
                    o = 64 * odd
                    for q in range(4):
                        j = j4 * 4 + q
                        for ri in range(2):
                            last = pe.matmul(b[:, q * P:(q + 1) * P], brep[o:o + 64, ri, j],
                                             cw[o:o + 64, ri, j, 0:CH, :], start=ri == 0, stop=ri == 1)
                    last.then_inc(s["job"], 1)
            x_tiles(N_EARLY, T_MQ - N_EARLY)

            pe.wait_ge(s["ucomb"], 1 + CH + 2)
            for ct in range(4):
                for k4 in range(2):
                    b = jobs.take_pe(pe)
                    for q in range(4):
                        last = pe.transpose(b[0:XC, q * P:(q + 1) * P], ucomb[:, ct, k4 * 4 + q, :], ident)
                    last.then_inc(s["job"], 1)
            pe.wait_ge(s["jobfree"], E_UC)
            for g0 in range(0, SG, 6):
                b = jobs.take_pe(pe)
                for g in range(g0, min(g0 + 6, SG)):
                    last = pe.transpose(b[:, (g - g0) * XC:(g - g0 + 1) * XC], utok[0:XC, g],
                                        ident[0:XC, 0:XC])
                last.then_inc(s["job"], 1)
            pe.wait_ge(s["jobfree"], E_U)
            for ri in range(2):
                for j0 in range(0, NJ, 6):
                    b = jobs.take_pe(pe)
                    for j in range(j0, min(j0 + 6, NJ)):
                        for o in (0, 64):
                            last = pe.matmul(b[o:o + 64, (j - j0) * XC:(j - j0 + 1) * XC],
                                             state_in[:, ri, j, o:o + 64], uch[:, 2 * j + o // 64, :],
                                             start=True, stop=True, skip_group_check=True)
                    last.then_inc(s["job"], 1)
            x_tiles(T_MQ, N_PROJ - T_MQ)
            pe.wait_ge(s["mn"], KT)
            with pe.Fori(0, N_MEMT // 2) as i2:
                for u in range(2):
                    pe.wait_ge(s[f"win{u}"], i2 * 16 + 16 * (N_PROJ // 2 + 1))
                    pe.wait_ge(s["evac"], i2 * 2 + (N_PROJ + u + 1))
                    for k in range(KT):
                        last = pe.matmul(bank[:, 2 * u, 0:MEM], ring[u][:, k, :], memn[:, k, :],
                                         start=k == 0, stop=k == KT - 1)
                    last.then_inc(s["tile"], 1)
            pe.wait_ge(s["toep"], CH)
            pe.wait_ge(s["sprev"], 3)
            for j4 in range(NJ // 4):
                for odd in range(2):
                    b = jobs.take_pe(pe)
                    o = 64 * odd
                    for q in range(4):
                        j = j4 * 4 + q
                        out = b[0:YC, q * P:(q + 1) * P]
                        pe.matmul(out, uch[:, 2 * j + odd, 0:YC], toep[:, odd, j, :], start=True, stop=False)
                        for ri in range(2):
                            last = pe.matmul(out, sprev[o:o + 64, ri, j], cw[o:o + 64, ri, j, 1:CH + 1, :],
                                             start=False, stop=ri == 1)
                    last.then_inc(s["job"], 1)
            pe.wait_ge(s["jobfree"], E_Y)
            for ct in range(4):
                for k4 in range(2):
                    b = jobs.take_pe(pe)
                    for q in range(4):
                        last = pe.transpose(b[:, q * YC:(q + 1) * YC], ytok[0:YC, k4 * 4 + q, ct * P:(ct + 1) * P],
                                            ident[0:YC, 0:YC])
                    last.then_inc(s["job"], 1)
            for g, kv, r in KV:
                b = jobs.take_pe(pe)
                for q in range(2):
                    last = pe.transpose(b[:, q * P:(q + 1) * P],
                                        proj[:, T_QKV + 6 * g + 2 + 2 * kv + q, r * P:(r + 1) * P], ident)
                last.then_inc(s["job"], 1)
            for g in range(NG):
                b = jobs.take_pe(pe)
                for q in range(4):
                    last = pe.transpose(b[0:NB, q * P:(q + 1) * P], proj[:, T_QKV + 6 * g + 2 + q, SEQ:TOK], ident)
                last.then_inc(s["job"], 1)
            for kv in (1, 0):
                for m in range(2):
                    b = jobs.take_pe(pe)
                    for q in range(4):
                        last = pe.transpose(b[:, q * P:(q + 1) * P], mkv[:, 4 * kv + q, m * P:(m + 1) * P], ident)
                    last.then_inc(s["job"], 1)

            pe.wait_ge(s["wglu"], 16)
            pe.wait_ge(s["z"], 4)
            for ct in range(4):
                for h in range(2):
                    b = jobs.take_pe(pe)
                    for k in range(4):
                        last = pe.matmul(b[:, 0:HALF], w_glu[:, k, ct * P:(ct + 1) * P],
                                         zcol[:, k, h * HALF:(h + 1) * HALF], start=k == 0, stop=k == 3)
                    last.then_inc(s["job"], 1)

            def gate_tile(i):
                wait_from(pe, s["gevac"], i)
                n = N_FIRST + i
                pe.wait_ge(s[f"win{n % 2}"], 16 * (n // 2 + 1))
                for k in range(KT):
                    for h in range(2):
                        last = pe.matmul(bank[:, h, 0:HALF], ring[n % 2][:, k, :],
                                         xn[:, k, h * HALF:(h + 1) * HALF], start=k == 0, stop=k == KT - 1)
                last.then_inc(s["tile"], 1)

            def scores(it):
                r, h = divmod(it, NH)
                o, q = 64 * (h % 2), h // 2
                wait_from(pe, s["T"], it)
                for g in range(NG):
                    keys = proj[o:o + 64, T_QKV + 6 * g + 2 + q, 0:SEQ] if g == 0 else \
                        proj[o:o + 64, T_QKV + 6 * g + 2 + q, r * P:(r + 1) * P]
                    out = bank[:, 2, :] if g == 0 else bank[:, 3, (g - 1) * P:g * P]
                    last = pe.matmul(out, proj[o:o + 64, T_QKV + 6 * g + q, r * P:(r + 1) * P], keys,
                                     start=True, stop=True)
                last.then_inc(s["S"], 1)

            pe.wait_ge(s["jobfree"], E_GLU)
            pe.wait_ge(s["evac"], 2 + N_FIRST)
            scores(0)
            for it in range(NCLS * NH):
                r, h = divmod(it, NH)
                gate_tile(it)
                pe.wait_ge(s["pn"], it + 1)
                wait_from(pe, s["ptc"], it)
                for q in range(6):
                    last = pe.transpose(bank[:, 4 + q // 4, q % 4 * P:(q % 4 + 1) * P], pr[:, q * P:(q + 1) * P],
                                        ident)
                last.then_inc(s["PT"], 1)
                if it + 1 < NCLS * NH:
                    scores(it + 1)
                pe.wait_ge(s["ptc"], it + 1)
                wait_from(pe, s["oc"], it)
                o = 64 * (h % 2)
                for q in range(6):
                    g, kt = (0, q) if q < 4 else (q - 3, r)
                    last = pe.matmul(bank[o:o + 64, 6, 0:P], v_rows[:, g, kt, h * DH:(h + 1) * DH],
                                     prT[:, q * P:(q + 1) * P], start=q == 0, stop=q == 5)
                last.then_inc(s["O"], 1)

            def mem_scores(it):
                r, h = divmod(it, MH)
                wait_from(pe, s["mexp"], it - 1)
                pe.matmul(bank[:, 2 + it % 2, 0:MEM], proj[:, T_MQ + h, r * P:(r + 1) * P], mkv[:, h, :],
                          start=True, stop=True).then_inc(s["mS"], 1)

            pe.wait_ge(s["ptc"], NCLS * NH)
            pe.wait_ge(s["oc"], NCLS * NH)
            pe.wait_ge(s["T"], NCLS * NH)
            mem_scores(0)
            mem_scores(1)
            for pair in range(NCLS * MH // 2):
                its = (2 * pair, 2 * pair + 1)
                gate_tile(NCLS * NH + pair)
                for it in its:
                    pe.wait_ge(s["mpn"], it + 1)
                    wait_from(pe, s["mptc"], it - 1)
                    for q in range(2):
                        last = pe.transpose(bank[:, 4 + it % 2, q * P:(q + 1) * P],
                                            pm[it % 2][:, q * P:(q + 1) * P], ident)
                    last.then_inc(s["mPT"], 1)
                if its[1] + 1 < NCLS * MH:
                    mem_scores(its[0] + 2)
                    mem_scores(its[1] + 2)
                for it in its:
                    h = it % MH
                    pe.wait_ge(s["mptc"], it + 1)
                    wait_from(pe, s["moc"], it - 1)
                    for q in range(2):
                        last = pe.matmul(bank[:, 6 + it % 2, 0:P], mv_rows[:, q, h * MD:(h + 1) * MD],
                                         pmT[it % 2][:, q * P:(q + 1) * P], start=q == 0, stop=q == 1)
                    last.then_inc(s["mO"], 1)

            def ssm_out(j):
                if j == 0:
                    pe.wait_ge(s["wssm"], 16)
                    pe.wait_ge(s["ssm"], 4)
                wait_from(pe, s["Sfree"], (0, 1, 2, 0, 0, 4, 5, 6)[j])
                for k in range(4):
                    for h in range(2):
                        last = pe.matmul(bank[:, SSM_BANK[j] + h, 0:HALF], w_ssm[:, k, j * P:(j + 1) * P],
                                         ssmT[:, k, h * HALF:(h + 1) * HALF], start=k == 0, stop=k == 3)
                last.then_inc(s["Sj"], 1)

            pe.wait_ge(s["moc"], NCLS * MH)
            pe.wait_ge(s["gevac"], N_GATE)
            pe.wait_ge(s["dprod"], 2)
            for g in range(NG):
                for hh in range(2):
                    pe.matmul(bank[32 * hh:32 * hh + 32, 4, g:g + 1], newprod[:, g, hh, :],
                              ones[:, 0:1], start=True, stop=True, skip_group_check=True)
            for b in range(NB):
                i = b % NSLOT
                pe.wait_ge(kdec[i], 32 * (b // NSLOT + 1))
                for g in range(NG):
                    for hh in range(2):
                        pe.matmul(bank[32 * hh:32 * hh + 32, g, 0:P], dq[:, g, hh, b * 32:(b + 1) * 32],
                                  slot_k[i][:, g, hh, :], start=b == 0, stop=b == NB - 1, skip_group_check=True)
                for h in range(MH):
                    pe.matmul(bank[32 * h:32 * h + 32, 3, 0:MEM], dmq[:, h, b * 32:(b + 1) * 32],
                              slot_mk[i][:, h, :], start=b == 0, stop=b == NB - 1, skip_group_check=True
                              ).then_inc(s["dkdone"], 1)
                if b in (3, 5, 7):
                    ssm_out(b // 2 - 1)
            pe.wait_ge(s["dpd"], NG + 1)
            for g in range(NG):
                pe.transpose(bank[:, 4, g * 64:(g + 1) * 64], dsc[0:64, g * P:(g + 1) * P], ident[0:64, 0:64])
            pe.wait_ge(s["Sfree"], 3)
            pe.matmul(bank[0:NB, 7, 0:NG * 64], c["esel"][0:64, :], dpd[0:64], start=True, stop=True)
            for q in range(2):
                last = pe.transpose(bank[:, 5, q * P:(q + 1) * P], dm[:, q * P:(q + 1) * P], ident)
            last.then_inc(s["dback"], 1)
            pe.wait_ge(s["dbackc"], 3)
            for g in range(NG):
                for hh in range(2):
                    pe.matmul(bank[32 * hh:32 * hh + 32, 6, 0:P], dpn[0:NB, g, 32 * hh:32 * hh + 32],
                              kv_dec[0:NB, g, 1, hh * P:(hh + 1) * P], start=g == 0, stop=False,
                              skip_group_check=True)
            for b in range(NB):
                i = b % NSLOT
                pe.wait_ge(vdec[i], 64 * (b // NSLOT + 1))
                for g in range(NG):
                    for hh in range(2):
                        pe.matmul(bank[32 * hh:32 * hh + 32, 6, 0:P],
                                  dpv[:, g, 32 * hh * NB + b:32 * (hh + 1) * NB:NB],
                                  slot_v[i][:, g, hh * P:(hh + 1) * P], start=False,
                                  stop=b == NB - 1 and g == NG - 1, skip_group_check=True)
                for q in range(2):
                    for h in range(MH):
                        last = pe.matmul(bank[32 * h:32 * h + 32, 7, 0:P], dmpv[:, q, h, b:32 * NB:NB],
                                         slot_mv[i][:, q, h * MD:(h + 1) * MD], start=b == 0 and q == 0,
                                         stop=b == NB - 1 and q == 1, skip_group_check=True)
                        if q == 1:
                            last.then_inc(s["dvdone"], 1)
                if b == 3:
                    ssm_out(3)
                    ssm_out(4)
                if b == 5:
                    ssm_out(5)
            ssm_out(6)
            ssm_out(7)
            pe.wait_ge(s["dout"], 2)
            pe.transpose(bank[:, 4, 0:64], do_rows[0:64, :], ident[0:64, 0:64])
            pe.transpose(bank[:, 5, 0:P], dmo_rows, ident).then_inc(s["dturn"], 1)

            pe.wait_ge(s["wout"], 32)
            pe.wait_ge(s["doc"], 3)
            pe.wait_ge(s["Sfree"], KT)
            for j in range(KT):
                for i, (w, src, nk) in enumerate(((w_att, attT, 2), (w_mem, memT, 4))):
                    wait_from(pe, s["Pfree"], 2 * (j - 1) + i + 1 if j else 0)
                    for k in range(nk):
                        for h in range(2):
                            last = pe.matmul(bank[:, 4 * i + h, 0:HALF], w[:, k, j * P:(j + 1) * P],
                                             src[:, k, h * HALF:(h + 1) * HALF], start=k == 0, stop=k == nk - 1)
                    last.then_inc(s["Pj"], 1)
            def turn_rows(T):
                n = ROWS[T]
                pe.wait_ge(s["hn"], T + 1)
                wait_from(pe, s["hnT"], T)
                for k in range(KT):
                    last = pe.transpose(bank[:, 4 + k // 4, k % 4 * P:k % 4 * P + n],
                                        hn_rows[0:n, T, k * P:(k + 1) * P], ident[0:n, 0:n])
                last.then_inc(s["ht"], 1)

            def router(T):
                n = ROWS[T]
                pe.wait_ge(s["hnT"], T + 1)
                for k in range(KT):
                    last = pe.matmul(bank[0:n, 6, T * (NGRP + NE):(T + 1) * (NGRP + NE)],
                                     hnT[T % 2][:, k, 0:n], w_route[:, k, :],
                                     start=k == 0, stop=k == KT - 1)
                last.then_inc(s["lg"], 1)

            pe.wait_ge(s["wo"], 32)
            pe.wait_ge(s["merged"], KT)
            for T in range(NT):
                wait_from(pe, s["h"], T - 1)
                order = [(half, k) for half in range(2) for k in range(KT)] if T < NT - 1 else \
                    [(half, k) for k in range(KT) for half in range(2)]
                for half, k in order:
                    o = 64 * half if T == NT - 1 else 0
                    last = pe.matmul(bank[o:o + ROWS[T], 2 * (T % 2) + half, :],
                                     gates[:, 3 * k, T * P:T * P + ROWS[T]],
                                     w_o[k // 4][:, k % 4, half * 512:(half + 1) * 512],
                                     start=k == 0, stop=k == KT - 1)
                    if k == KT - 1 and (half == 1 or T == NT - 1):
                        last.then_inc(s["wo_mm"], 1)
                if T >= 1:
                    turn_rows(T - 1)
                if T >= 2:
                    router(T - 2)
            turn_rows(NT - 1)
            router(NT - 2)
            router(NT - 1)
            pe.wait_ge(s["chosen"], 1)
            pe.matmul(bank[:, 5, 0:NT * NE], c["triu"], chosen.rearrange("p a b -> p (a b)"), start=True, stop=True)
            pe.matmul(bank[:, 4, 0:NT * NE], ones, chosen.rearrange("p a b -> p (a b)"), start=True, stop=True
                      ).then_inc(s["rank"], 1)

            pe.wait_ge(s["npass"], 1)
            n_p = pe.value_load(n_pass[0:1, 0:1], min_val=1, max_val=MAXP)
            with pe.Fori(0, n_p) as p:
                pe.wait_ge(s["hot"], p + 1)
                for k in range(2):
                    for T in range(NT):
                        last = pe.matmul(bank[0:CAP, 7, 0:NE], hot[k][:, T, :], mtok[k][:, T, :],
                                         start=k == 0 and T == 0, stop=k == 1 and T == NT - 1)
                last.then_inc(s["idxmm"], 1)
                pe.wait_ge(s["idx"], p + 1)
                pe.sem_inc(s["held"], 1)
                with pe.Fori(0, NE // 2) as e2:
                    for u in range(2):
                        w13, w2 = wb[u]
                        step = p * NE + e2 * 2
                        loads = p * (NE // 2) + e2
                        pe.wait_ge(s[f"xg{u}"], loads * 16 + 16)
                        pe.wait_ge(s["xc"], step + (u + 1))
                        pe.sem_inc(s["held"], 1)
                        for k in range(KT):
                            last = pe.transpose(bank[:, u, k * CAP:(k + 1) * CAP], xg[u][0:CAP, k:D:KT],
                                                ident[0:CAP, 0:CAP])
                        last.then_inc(s["xt"], 1)
                        pe.wait_ge(s["xc"], step + (u + 3))
                        pe.wait_ge(s["hid"], step + (u + 1))
                        pe.wait_ge(s[f"w13_{u}"], loads * 32 + 32)
                        for i in range(2):
                            for k in range(KT):
                                for q in range(2):
                                    last = pe.matmul(bank[64 * q:64 * q + CAP, 2 + u, i * FE // 2:(i + 1) * FE // 2],
                                                     xgT[u][:, k, :], w13[:, i, k, q * FE // 2:(q + 1) * FE // 2],
                                                     start=k == 0, stop=k == KT - 1)
                                    if k == KT - 1:
                                        last.then_inc(s[("w1x", "gu")[i]], 1)
                        pe.wait_ge(s["hT"], step + (u + 1))
                        pe.wait_ge(s["hid"], step + (u + 3))
                        for j in range(2):
                            last = pe.transpose(bank[:, 4 + u, j * P:(j + 1) * P], hidden[u][:, j:FE // 2:2], ident)
                        last.then_inc(s["ht2"], 1)
                        pe.wait_ge(s["hT"], step + (u + 3))
                        pe.wait_ge(s["yc"], step + (u + 1))
                        pe.wait_ge(s[f"w2_{u}"], loads * 16 + 16)
                        for f in range(FT):
                            for q in range(2):
                                last = pe.matmul(bank[64 * q:64 * q + CAP, 6 + u, :],
                                                 hT[u][:, f % 2, f // 2 * CAP:(f // 2 + 1) * CAP],
                                                 w2[:, f // 2, f % 2, q * 512:(q + 1) * 512],
                                                 start=f == 0, stop=f == FT - 1)
                                if f == FT - 1:
                                    last.then_inc(s["y"], 1)
                pe.wait_ge(s["yc"], p * NE + (NE + 2))

        @block.scalar
        def _(act):
            act.sem_inc(s["evac"], 2)
            act.sem_inc(s["yc"], 2)
            for u in range(2):
                act.sem_inc(s[f"yo{u}"], 16)
            act.wait_ge(s["ssmp"], 16)
            act.activation(par[:, 0], ssm_in[:, 2], ACT.Exp).then_inc(s["dt"], 1)
            act.wait_ge(s["lrdt"], 1)
            act.activation(par[:, 2], par[:, 1], ACT.Exp).then_inc(s["dt"], 1)
            act.wait_ge(s["lrdt"], 2)
            act.activation(par[:, 5], par[:, 4], ACT.Sin).then_inc(s["trig"], 1)
            act.activation(par[:, 6], par[:, 4], ACT.Sin, scale=0.5).then_inc(s["trig"], 1)
            act.wait_ge(s["cst"], 16)
            act.wait_ge(s["ss"], 1)
            for h in range(2):
                act.activation(rms[:, h * HALF:(h + 1) * HALF], bank[:, 4 + h, 0:HALF], ACT.Sqrt, bias=eps_ap,
                               scale=1.0 / D).then_inc(s["rms"], 1)
            def x_tiles(first, count):
                with act.Fori(0, count // 2) as i2:
                    for u in range(2):
                        act.wait_ge(s["tile"], i2 * 2 + (first + u + 3))
                        dst = proj[:, bass.ds(i2 * 2 + (first + u), 1), :].rearrange("p o (h t) -> p (o h) t", h=2)
                        act.activation(dst, bank[:, 2 * u:2 * u + 2, 0:HALF], ACT.Copy).then_inc(s["evac"], 1)

            x_tiles(0, T_QKV)
            act.wait_ge(s["ss"], 2)
            act.activation(rmsm, bank[:, 6, 0:MEM], ACT.Sqrt, bias=eps_ap, scale=1.0 / D).then_inc(s["rms"], 1)
            x_tiles(T_QKV, N_EARLY - T_QKV)
            jobs = Jobs()
            for ri in range(2):
                for j4 in range(NJ // 4):
                    b = jobs.take_act(act)
                    act.activation(state_in[:, ri, j4 * 4:j4 * 4 + 4, :].rearrange("p a b -> p (a b)"), b, ACT.Copy
                                   ).then_inc(s["jobfree"], 1)
            for j4 in range(NJ // 4):
                for odd in range(2):
                    b = jobs.take_act(act)
                    act.activation(kern[:, odd, j4 * 4:j4 * 4 + 4, :].rearrange("p a b -> p (a b)"), b, ACT.Copy
                                   ).then_inc(s["jobfree"], 1)
            x_tiles(N_EARLY, T_MQ - N_EARLY)

            for ct in range(4):
                for k4 in range(2):
                    b = jobs.take_act(act)
                    act.activation(utok[0:XC, ct * 8:ct * 8 + 8, k4 * 4:k4 * 4 + 4, :].rearrange("p g k c -> p k g c"),
                                   b[0:XC, :].rearrange("p (k g c) -> p k g c", k=4, g=8), ACT.Copy
                                   ).then_inc(s["jobfree"], 1)
            act.wait_ge(s["toep"], CH)
            for g0 in range(0, SG, 6):
                b = jobs.take_act(act)
                n = min(6, SG - g0)
                act.activation(uch[:, g0:g0 + n, :].rearrange("p a b -> p (a b)"), b[:, 0:n * XC], ACT.Copy
                               ).then_inc(s["jobfree"], 1)
            for ri in range(2):
                for j0 in range(0, NJ, 6):
                    b = jobs.take_act(act)
                    n = min(6, NJ - j0)
                    act.activation(xst[:, ri, j0:j0 + n, :].rearrange("p a b -> p (a b)"), b[:, 0:n * XC], ACT.Copy
                                   ).then_inc(s["jobfree"], 1)
            x_tiles(T_MQ, N_PROJ - T_MQ)
            with act.Fori(0, N_MEMT // 2) as i2:
                for u in range(2):
                    act.wait_ge(s["tile"], i2 * 2 + (N_PROJ + u + 3))
                    act.activation(mkv[:, bass.ds(i2 * 2 + u, 1), :].rearrange("p o t -> p (o t)"),
                                   bank[:, 2 * u, 0:MEM], ACT.Copy).then_inc(s["evac"], 1)
            act.wait_ge(s["sprev"], 3)
            for j4 in range(NJ // 4):
                for odd in range(2):
                    b = jobs.take_act(act)
                    dst = ytok[0:YC].rearrange("p t (j o c) -> p o j t c", o=2, c=SCH)[:, odd, j4 * 4:j4 * 4 + 4]
                    act.activation(dst, b[0:YC, :].rearrange("p (j t c) -> p j t c", j=4, t=CH), ACT.Copy
                                   ).then_inc(s["jobfree"], 1)
            act.wait_ge(s["states"], 3)
            for ct in range(4):
                for k4 in range(2):
                    b = jobs.take_act(act)
                    src = b[:, 0:4 * YC].rearrange("p (r n) -> p r n", r=4)
                    dst = ycol[:, ct, 0:SEQ].rearrange("p (r n q) -> p r n q", r=4, q=2)[:, :, :, k4]
                    last = act.activation(dst, src[:, :, 0:NCH], ACT.Copy)
                    if k4 == 0:
                        last = act.activation(ycol[:, ct, SEQ:TOK], src[:, 0, NCH:YC], ACT.Copy)
                    last.then_inc(s["jobfree"], 1)
            for ct in range(4):
                act.wait_ge(s["yadd"], ct + 1)
                act.activation(zcol[:, ct, :], ycol[:, ct, :], ACT.Gelu_apprx_tanh).then_inc(s["z"], 1)
            for g, kv, r in KV:
                b = jobs.take_act(act)
                dst = k_rows[g][:, r, :] if kv == 0 else v_rows[:, g, r, :]
                act.activation(dst, b[:, 0:ATT], ACT.Copy).then_inc(s["jobfree"], 1)
                if r == NCLS - 1:
                    act.wait_ge(s["jobfree"], jobs.n)
                    act.sem_inc(s["krows"], 1)
            for g in range(NG):
                b = jobs.take_act(act)
                act.activation(kv_dec[0:NB, g].rearrange("p a b -> p (a b)"), b[0:NB, :], ACT.Copy
                               ).then_inc(s["jobfree"], 1)
            act.wait_ge(s["jobfree"], jobs.n)
            act.sem_inc(s["krows"], 1)
            for kv in (1, 0):
                for m in range(2):
                    b = jobs.take_act(act)
                    act.activation((mv_rows if kv else mk_rows)[:, m, :], b, ACT.Copy).then_inc(s["jobfree"], 1)
                act.wait_ge(s["jobfree"], jobs.n)
                act.sem_inc(s["krows"], 1)

            act.wait_ge(s["small"], 144)
            for ct in range(4):
                for h in range(2):
                    b = jobs.take_act(act)
                    act.activation(glu[:, ct, h * HALF:(h + 1) * HALF], b[:, 0:HALF], ACT.Sigmoid,
                                   bias=b_glu[:, ct:ct + 1]).then_inc(s["jobfree"], 1)

            def gate_out(i):
                act.wait_ge(s["tile"], 2 + N_FIRST + i + 1)
                act.activation(gates[:, i, :].rearrange("p (h t) -> p h t", h=2), bank[:, 0:2, 0:HALF], ACT.Copy
                               ).then_inc(s["gevac"], 1)

            act.wait_ge(s["kout"], 16 * (2 * NG))
            for it in range(NCLS * NH):
                act.wait_ge(s["nmax"], it + 1)
                wait_from(act, s["PT"], it)
                act.activation(pr, sc, ACT.Exp, bias=stat[:, 2 * (it % 2) + 1:2 * (it % 2) + 2], scale=ATT_SCALE,
                               accum_out=stat[:, 8 + it % 2:9 + it % 2]).then_inc(s["exp"], 1)
                gate_out(it)
                act.wait_ge(s["PT"], it + 1)
                wait_from(act, s["O"], it)
                act.activation(prT[:, 0:512], bank[:, 4, :], ACT.Copy)
                act.activation(prT[:, 512:768], bank[:, 5, 0:256], ACT.Copy).then_inc(s["ptc"], 1)
            act.wait_ge(s["oc"], NCLS * NH)
            for b in range(NSLOT):
                load_keys(act, b)
            act.dma_start(w_ssm, t["w_ssm"]).then_inc(s["wssm"], 16)
            for pair in range(NCLS * MH // 2):
                its = (2 * pair, 2 * pair + 1)
                for it in its:
                    act.wait_ge(s["mnmax"], it + 1)
                    wait_from(act, s["mPT"], it - 1)
                    if it == 0:
                        act.wait_ge(s["PT"], NCLS * NH)
                    act.activation(pm[it % 2], bank[:, 2 + it % 2, 0:MEM], ACT.Exp,
                                   bias=stat[:, 16 + it % 2:17 + it % 2], scale=MEM_SCALE,
                                   accum_out=stat[:, 18 + it % 2:19 + it % 2]).then_inc(s["mexp"], 1)
                gate_out(NCLS * NH + pair)
                for it in its:
                    act.wait_ge(s["mPT"], it + 1)
                    wait_from(act, s["mO"], it - 1)
                    act.activation(pmT[it % 2], bank[:, 4 + it % 2, 0:MEM], ACT.Copy).then_inc(s["mptc"], 1)

            act.wait_ge(s["gevac"], N_GATE)
            act.activation(gates.rearrange("p a b -> p (a b)"), gates.rearrange("p a b -> p (a b)"), ACT.Sigmoid
                           ).then_inc(s["gsig"], 1)
            act.wait_ge(s["dnmax"], 2)
            act.activation(dsc[0:64], dsc[0:64], ACT.Exp, bias=stat[0:64, 25:26], scale=ATT_SCALE,
                           accum_out=stat[0:64, 26:27]).then_inc(s["dexp"], 1)
            act.activation(dm, bank[:, 3, 0:MEM], ACT.Exp, bias=stat[:, 29:30], scale=MEM_SCALE,
                           accum_out=stat[:, 30:31]).then_inc(s["dexp"], 1)
            act.wait_ge(s["dback"], 1)
            act.wait_ge(s["krest"], 16 * (2 * NG + 2))
            act.activation(dpn[0:NB].rearrange("p a b -> p (a b)"), bank[0:NB, 7, 0:NG * 64], ACT.Copy
                           ).then_inc(s["dbackc"], 1)
            act.wait_ge(s["dvdone"], MH * NB)
            act.activation(do_rows[0:64], bank[0:64, 6, 0:P], ACT.Copy).then_inc(s["dout"], 1)
            act.activation(dmo_rows, bank[:, 7, 0:P], ACT.Copy).then_inc(s["dout"], 1)

            def turned(T):
                n = ROWS[T]
                act.wait_ge(s["ht"], T + 1)
                wait_from(act, s["lg"], T - 1)
                for half in range(2):
                    last = act.activation(hnT[T % 2][:, 4 * half:4 * half + 4, 0:n],
                                          bank[:, 4 + half, :].rearrange("p (k a) -> p k a", k=4)[:, :, 0:n],
                                          ACT.Copy)
                last.then_inc(s["hnT"], 1)

            for T in range(NT):
                n = ROWS[T]
                if T == NT - 1:
                    act.wait_ge(s["wo_mm"], NT + 1)
                    act.activation(h_rows[0:n, T, 512:D], bank[64:64 + n, 2 * (T % 2) + 1, :], ACT.Copy
                                   ).then_inc(s["h_moved"], 1)
                act.wait_ge(s["h"], T + 1)
                act.activation(hn_rows[0:n, T, :], h_rows[0:n, T, :], ACT.Square,
                               accum_out=stat[0:n, 32 + T:33 + T]).then_inc(s["hss"], 1)
                act.wait_ge(s["hss"], T + 1)
                act.activation(stat[0:n, 37 + T:38 + T], stat[0:n, 32 + T:33 + T], ACT.Sqrt, bias=eps_ap[0:n],
                               scale=1.0 / D).then_inc(s["hrms"], 1)
                if T >= 1:
                    turned(T - 1)
            turned(NT - 1)
            act.wait_ge(s["gmax"], 1)
            act.activation(ex4.rearrange("p a b -> p (a b)"), ex4.rearrange("p a b -> p (a b)"), ACT.Exp
                           ).then_inc(s["gexp"], 1)
            act.wait_ge(s["gmax"], 2)
            act.activation(r5[5], r5[4], ACT.Exp).then_inc(s["gexp"], 1)

            act.wait_ge(s["npass"], 1)
            act.wait_ge(s["lg"], NT)
            n_p = act.value_load(n_pass[0:1, 0:1], min_val=1, max_val=MAXP)
            with act.Fori(0, n_p) as p:
                with act.Fori(0, NE // 2) as e2:
                    for u in range(2):
                        step = p * NE + e2 * 2
                        act.wait_ge(s["gu"], p * (2 * NE) + e2 * 4 + (2 * u + 6))
                        act.wait_ge(s["hid"], step + (u + 1))
                        act.activation(sg[u], bank[:, 2 + u, 0:FE // 2], ACT.Silu).then_inc(s["sg"], 1)
                        act.wait_ge(s["y"], p * (2 * NE) + e2 * 4 + (2 * u + 6))
                        act.wait_ge(s[f"yo{u}"], (p * (NE // 2) + e2) * 16 + 16)
                        act.activation(y_sb[u], bank[:, 6 + u, :], ACT.Copy).then_inc(s["yc"], 1)
                        act.wait_ge(s["yc"], step + (u + 3))
                        act.wait_ge(s["fsum"], p * NT + NT)
                        act.dma_start(t["y_slots"][bass.ds(e2 * 2 + u, 1)].rearrange(
                            "a c (q d) -> (a q) c d", q=2), y_sb[u]).then_inc(s[f"yo{u}"], 16)
            for T in range(NT):
                n = ROWS[T]
                act.wait_ge(s["fsum"], n_p * NT + (T + 1))
                act.activation(squares[0:n, :], h_rows[0:n, T, :], ACT.Square,
                               accum_out=stat[0:n, 42 + T:43 + T]).then_inc(s["fss"], 1)
                act.wait_ge(s["fss"], T + 1)
                act.activation(stat[0:n, 47 + T:48 + T], stat[0:n, 42 + T:43 + T], ACT.Sqrt, bias=eps_ap[0:n],
                               scale=1.0 / D).then_inc(s["frms"], 1)

        @block.vector
        def _(dve):
            TT, TS, STT = dve.tensor_tensor, dve.tensor_scalar, dve.scalar_tensor_tensor
            chain = [0]

            def then(*ins):
                for i in ins:
                    i.then_inc(s["vchain"], 1)
                chain[0] += len(ins)
                dve.wait_ge(s["vchain"], chain[0])

            dve.sem_inc(s["xc"], 2)
            dve.sem_inc(s["hid"], 2)
            dve.sem_inc(s["hT"], 2)
            dve.sem_inc(s["fsum"], NT)

            lr, li, dt = ssm_in[:, 0], ssm_in[:, 1], par[:, 0]
            lrdt, mag, ang, red, s1, sh = (par[:, i] for i in range(1, 7))
            dve.wait_ge(s["ssmp"], 16)
            dve.wait_ge(s["dt"], 1)
            TT(lrdt, lr, dt, ALU.mult).then_inc(s["lrdt"], 1)
            then(TT(ang, li, dt, ALU.mult))
            kk = par[:, 7]
            then(TS(kk, ang, 1.0 / TWO_PI, ROUND, ALU.mult, ALU.add))
            then(TS(kk, kk, -ROUND, None, ALU.add))
            then(STT(out=red, in0=kk, scalar=-PI_A, in1=ang, op0=ALU.mult, op1=ALU.add))
            then(STT(out=red, in0=kk, scalar=-PI_B, in1=red, op0=ALU.mult, op1=ALU.add))
            then(STT(out=red, in0=kk, scalar=-PI_C, in1=red, op0=ALU.mult, op1=ALU.add))
            lim = float(np.float32(3.1415925))
            TS(red, red, lim, -lim, ALU.min, ALU.max).then_inc(s["lrdt"], 1)

            for k in range(KT):
                if k % (KT // 2) == 0:
                    dve.wait_ge(s[f"x{k // (KT // 2)}"], 16)
                TT(sq[:, k, :], xraw[:, k, :], xraw[:, k, :], ALU.mult).then_inc(s["sq"], 1)
            dve.wait_ge(s["gain1"], 16)
            dve.wait_ge(s["sq"], KT)
            for k in range(KT):
                TS(xraw[:, k, :], xraw[:, k, :], gain1[:, k:k + 1], None, ALU.mult).then_inc(s["xraw"], 1)
            dve.wait_ge(s["mem"], 16)
            for k in range(KT):
                TT(sqm[:, k, :], memn[:, k, :], memn[:, k, :], ALU.mult).then_inc(s["sq"], 1)
            dve.wait_ge(s["rms"], 2)
            then(dve.reciprocal(rms, rms))
            dve.wait_ge(s["xraw"], KT)
            for k in range(KT):
                TT(xn[:, k, :], xraw[:, k, :], rms, ALU.mult).then_inc(s["xn"], 1)
            ar, ai, cosm = par[:, 8], par[:, 9], par[:, 10]
            t1, t2, den, nr, zr, zi = (par[:, i] for i in range(11, 17))
            dve.wait_ge(s["dt"], 2)
            dve.wait_ge(s["trig"], 2)
            then(TT(cosm, sh, sh, ALU.mult), TT(ai, mag, s1, ALU.mult))
            then(TS(cosm, cosm, -2.0, 1.0, ALU.mult, ALU.add))
            then(TT(ar, mag, cosm, ALU.mult), TT(t1, lr, lr, ALU.mult), TT(t2, li, li, ALU.mult))
            then(TT(den, t1, t2, ALU.add), TS(nr, ar, -1.0, None, ALU.add))
            then(dve.reciprocal(den, den), TT(t1, nr, lr, ALU.mult), TT(t2, ai, li, ALU.mult))
            then(TT(zr, t1, t2, ALU.add))
            then(TT(zr, zr, den, ALU.mult), TT(t1, ai, lr, ALU.mult), TT(t2, nr, li, ALU.mult))
            then(TT(zi, t1, t2, ALU.subtract))
            then(TT(zi, zi, den, ALU.mult))

            def cmul(out, a, b, shape, tmp=None, neg_im=False):
                n = int(np.prod(shape))
                names = "abcd"[:len(shape)]
                flat = f"p ({' '.join(names)}) -> p {' '.join(names)}"
                u, v = (x[:, 0:n] for x in (tmp or ctmp))
                if len(shape) > 1:
                    u, v = (x.rearrange(flat, **dict(zip(names, shape))) for x in (u, v))
                then(TT(u, a[1], b[1], ALU.mult), TT(out[0], a[0], b[0], ALU.mult),
                     TT(v, a[0], b[1], ALU.mult), TT(out[1], a[1], b[0], ALU.mult))
                if neg_im:
                    then(TT(out[0], out[0], u, ALU.subtract),
                         STT(out=out[1], in0=out[1], scalar=-1.0, in1=v, op0=ALU.mult, op1=ALU.subtract))
                else:
                    then(TT(out[0], out[0], u, ALU.subtract), TT(out[1], out[1], v, ALU.add))

            def ri(x, *idx):
                return [x[(slice(None), i) + idx] for i in range(2)]

            def wide(x, axis, shape):
                return x.unsqueeze(axis).to_broadcast([P] + list(shape))

            z_ = [wide(x, 2, (NJ, SCH)) for x in (zr, zi)]
            dve.wait_ge(s["small"], 144)
            cmul(ri(bbar), z_, ri(b_in), (NJ, SCH))
            then(dve.memset(pw[:, 0, :, 0:1], 1.0), dve.memset(pw[:, 1, :, 0:1], 0.0),
                 dve.tensor_copy(pw[:, 0, :, 1], ar), dve.tensor_copy(pw[:, 1, :, 1], ai))
            cmul(ri(pw, slice(None), 2), ri(pw, slice(None), 1), ri(pw, slice(None), 1), (NJ,))
            cmul(ri(pw, slice(None), slice(3, 5)), ri(pw, slice(None), slice(1, 3)),
                 [wide(x, 2, (NJ, 2)) for x in ri(pw, slice(None), 2)], (NJ, 2))
            cmul(ri(pw, slice(None), slice(5, 9)), ri(pw, slice(None), slice(1, 5)),
                 [wide(x, 2, (NJ, 4)) for x in ri(pw, slice(None), 4)], (NJ, 4))
            then(*[dve.tensor_copy(rpw[:, :, :, i], pw[:, :, :, CH - 1 - i]) for i in range(CH)])
            then(dve.tensor_copy(apow[:, :, 0, :], pw[:, :, :, CH]))
            for lv in range(1, LEVELS):
                cmul(ri(apow, lv), ri(apow, lv - 1), ri(apow, lv - 1), (NJ,))
            dve.wait_ge(s["evac"], 2 + T_QKV)
            dve.wait_ge(s["xn"], KT)
            then(*[TT(proj[:, ct, :], proj[:, ct, :], rms, ALU.mult) for ct in range(T_QKV)])
            dve.sem_inc(s["uscaled"], 1)
            full = (NJ, CH, SCH)
            cmul(ri(ba), [wide(x, 3, full) for x in ri(rpw)], [wide(x, 2, full) for x in ri(bbar)], full)
            dve.sem_inc(s["cplx"], 1)
            dve.wait_ge(s["rms"], 3)
            then(dve.reciprocal(rmsm, rmsm))
            for k in range(KT):
                STT(out=memn[:, k, :], in0=memn[:, k, :], scalar=gain_mem[:, k:k + 1], in1=rmsm, op0=ALU.mult,
                    op1=ALU.mult).then_inc(s["mn"], 1)

            then(*[dve.tensor_copy(x, wide(y, 2, full)) for x, y in zip(ri(brep), ri(bbar))])
            full = (NJ, CH + 1, SCH)
            cmul(ri(cw), [wide(x, 3, full) for x in ri(pw)], [wide(x, 2, full) for x in ri(c_in)], full, neg_im=True)
            dve.sem_inc(s["cplx"], 1)

            dve.wait_ge(s["jobfree"], E_K)
            dve.wait_ge(s["cst"], 16)
            for k in range(CH):
                w = (CH - k) * SCH
                sm = c["smask"][:, k:k + 1]
                if k == 0:
                    TS(toep, kern, sm, None, ALU.mult).then_inc(s["toep"], 1)
                else:
                    dve.wait_ge(s["toep"], k)
                    STT(out=toep[:, :, :, k * SCH:], in0=kern[:, :, :, 0:w], scalar=sm,
                        in1=toep[:, :, :, k * SCH:], op0=ALU.mult, op1=ALU.add).then_inc(s["toep"], 1)

            dve.wait_ge(s["jobfree"], E_X)
            sh_ = (NJ, NB)
            cmul(ri(st_dec), [wide(x, 2, sh_) for x in (ar, ai)], ri(h0), sh_, tmp=stmp[0:2])
            TT(st_dec, st_dec, xst[:, :, :, YC:XC], ALU.add).then_inc(s["states"], 1)
            for lv in range(LEVELS):
                d = 1 << lv
                w = NCH - d
                u = [x[:, 0:NJ * w].rearrange("p (j n) -> p j n", j=NJ) for x in stmp]
                pr_, pi_ = (wide(x, 2, (NJ, w)) for x in ri(apow, lv))
                xr, xi = xst[:, 0, :, 0:w], xst[:, 1, :, 0:w]
                yr, yi = xst[:, 0, :, d:NCH], xst[:, 1, :, d:NCH]
                then(TT(u[0], xr, pr_, ALU.mult), TT(u[1], xi, pi_, ALU.mult),
                     TT(u[2], xi, pr_, ALU.mult), TT(u[3], xr, pi_, ALU.mult))
                then(TT(yr, yr, u[0], ALU.add), TT(yi, yi, u[2], ALU.add))
                then(TT(yr, yr, u[1], ALU.subtract), TT(yi, yi, u[3], ALU.add))
            dve.memset(sprev[:, :, :, 0:1], 0.0).then_inc(s["sprev"], 1)
            dve.tensor_copy(sprev[:, :, :, NCH:YC], h0).then_inc(s["sprev"], 1)
            for i in range(2):
                last = dve.tensor_copy(sprev[:, i, :, 1:NCH], xst[:, i, :, 0:NCH - 1])
            last.then_inc(s["sprev"], 1)
            for i in range(2):
                dve.tensor_copy(st_prompt[:, i, :], xst[:, i, :, NCH - 1]).then_inc(s["states"], 1)
            dve.wait_ge(s["evac"], 2 + N_PROJ)
            dve.tensor_copy(dec_cols, proj[:, :, SEQ:TOK]).then_inc(s["dprod"], 1)

            for ct in range(4):
                dve.wait_ge(s["jobfree"], E_Y + 2 * (ct + 1))
                STT(out=ycol[:, ct, :], in0=proj[:, ct, :], scalar=ssm_d[:, ct:ct + 1], in1=ycol[:, ct, :],
                    op0=ALU.mult, op1=ALU.add).then_inc(s["yadd"], 1)
            for ct in range(4):
                dve.wait_ge(s["jobfree"], E_MEM + 2 * (ct + 1))
                TT(ssmT[:, ct, :], zcol[:, ct, :], glu[:, ct, :], ALU.mult).then_inc(s["ssm"], 1)

            dve.wait_ge(s["kout"], 16 * (2 * NG))
            dve.wait_ge(s["dist0"], 16)

            def o_copy(it):
                r, h = divmod(it, NH)
                o = 64 * (h % 2)
                dve.wait_ge(s["O"], it + 1)
                dve.tensor_copy(attT[o:o + 64, h // 2, r * P:(r + 1) * P], bank[o:o + 64, 6, 0:P]
                                ).then_inc(s["oc"], 1)

            for it in range(NCLS * NH):
                r, h = divmod(it, NH)
                mx, nm, dn, rd = (stat[:, i:i + 1] for i in (2 * (it % 2), 2 * (it % 2) + 1, 8 + it % 2, 10 + it % 2))
                dve.wait_ge(s["S"], it + 1)
                wait_from(dve, s["exp"], it)
                sl = -slope(h) / ATT_SCALE
                STT(out=sc[:, 0:512], in0=dist0[:, r, :], scalar=sl, in1=bank[:, 2, :], op0=ALU.mult,
                    op1=ALU.add).then_inc(s["vchain"], 1)
                STT(out=sc[:, 512:768], in0=dist12, scalar=sl, in1=bank[:, 3, 0:256], op0=ALU.mult,
                    op1=ALU.add).then_inc(s["T"], 1)
                chain[0] += 1
                dve.wait_ge(s["vchain"], chain[0])
                dve.wait_ge(s["T"], it + 1)
                then(dve.tensor_reduce(mx, sc, AX, ALU.max))
                TS(nm, mx, -ATT_SCALE, None, ALU.mult).then_inc(s["nmax"], 1)
                if it:
                    o_copy(it - 1)
                dve.wait_ge(s["exp"], it + 1)
                then(dve.reciprocal(rd, dn))
                TS(pr, pr, rd, None, ALU.mult).then_inc(s["pn"], 1)
            o_copy(NCLS * NH - 1)

            dve.wait_ge(s["dprod"], 1)
            then(dve.memset(dq, 0.0), dve.memset(dmq, 0.0), dve.memset(newprod, 0.0))
            six = dec_cols[:, T_QKV:T_MQ, :].rearrange("p (g x) b -> p g x b", g=NG)
            ins = [dve.tensor_copy(dmq[:, :, 0:NB * 33 - 32:33], dec_cols[:, T_MQ:N_PROJ, :])]
            for half in range(2):
                hp, lo = slice(64 * half, 64 * half + 64), 8 * half
                ins.append(dve.tensor_copy(dq[hp, :, :, lo:lo + NB * 33 - 32:33], six[hp, :, 0:2, :]))
                ins.append(TT(newprod[hp, :, :, lo:lo + NB], six[hp, :, 0:2, :], six[hp, :, 2:4, :], ALU.mult))
            then(*ins)
            dve.sem_inc(s["dprod"], 1)

            def mo_copy(it):
                r, h = divmod(it, MH)
                dve.wait_ge(s["mO"], it + 1)
                dve.tensor_copy(memT[:, h, r * P:(r + 1) * P], bank[:, 6 + it % 2, 0:P]).then_inc(s["moc"], 1)

            for it in range(NCLS * MH):
                b = it % 2
                mx, nm, dn, rd = (stat[:, i:i + 1] for i in (20 + b, 16 + b, 18 + b, 22 + b))
                dve.wait_ge(s["mS"], it + 1)
                then(dve.tensor_reduce(mx, bank[:, 2 + b, 0:MEM], AX, ALU.max))
                wait_from(dve, s["mexp"], it - 1)
                TS(nm, mx, -MEM_SCALE, None, ALU.mult).then_inc(s["mnmax"], 1)
                if it >= 2:
                    mo_copy(it - 2)
                dve.wait_ge(s["mexp"], it + 1)
                then(dve.reciprocal(rd, dn))
                TS(pm[b], pm[b], rd, None, ALU.mult).then_inc(s["mpn"], 1)
            for it in range(NCLS * MH - 2, NCLS * MH):
                mo_copy(it)

            def times_gate(tile, b0):
                g = gates[:, tile, :].rearrange("p (h t) -> p h t", h=2)
                return TT(g, g, bank[:, b0:b0 + 2, 0:HALF], ALU.mult)

            def ssm_merge(j):
                dve.wait_ge(s["Sj"], j + 1)
                times_gate(3 * j + 1, SSM_BANK[j]).then_inc(s["Sfree"], 1)

            then(dve.memset(dpv, 0.0), dve.memset(dmpv, 0.0))
            dve.wait_ge(s["gsig"], 1)
            ssm_merge(0)
            ssm_merge(1)
            dve.wait_ge(s["dkdone"], MH * NB)
            then(TT(dsc[0:64, 0:NG * P].rearrange("p (g m) -> p g m", g=NG),
                    c["decbias"][0:64, :].rearrange("p (g m) -> p g m", g=NG), bank[0:64, 0:NG, 0:P], ALU.add),
                 dve.tensor_copy(dsc[0:64, NG * P:], bank[0:64, 4, 0:NG]),
                 dve.tensor_reduce(stat[:, 28:29], bank[:, 3, 0:MEM], AX, ALU.max))
            then(dve.tensor_reduce(stat[0:64, 24:25], dsc[0:64], AX, ALU.max))
            TS(stat[0:64, 25:26], stat[0:64, 24:25], -ATT_SCALE, None, ALU.mult).then_inc(s["dnmax"], 1)
            TS(stat[:, 29:30], stat[:, 28:29], -MEM_SCALE, None, ALU.mult).then_inc(s["dnmax"], 1)
            dve.wait_ge(s["dexp"], 2)
            then(dve.reciprocal(stat[0:64, 27:28], stat[0:64, 26:27]),
                 dve.reciprocal(stat[:, 31:32], stat[:, 30:31]))
            then(TS(dsc[0:64], dsc[0:64], stat[0:64, 27:28], None, ALU.mult))
            TS(dm, dm, stat[:, 31:32], None, ALU.mult).then_inc(s["dpd"], 1)
            for g in range(NG):
                TS(dpd[0:64, g, :], ident[0:64, 0:64], dsc[0:64, NG * P + g:NG * P + g + 1], None, ALU.mult
                   ).then_inc(s["dpd"], 1)
            ssm_merge(2)
            dve.wait_ge(s["dback"], 1)
            dve.tensor_copy(dpv.rearrange("p g (r x) -> p (g r) x", r=8)[:, :, 0:NB * NB:NB + 1],
                            bank[:, 4, 0:NG * 64].rearrange("p (r b) -> p r b", b=NB)).then_inc(s["dbackc"], 1)
            dve.tensor_copy(dmpv.rearrange("p q h x -> p (q h) x")[:, :, 0:NB * NB:NB + 1],
                            bank[:, 5, 0:2 * P].rearrange("p (r b) -> p r b", b=32)[:, :, 0:NB]
                            ).then_inc(s["dbackc"], 1)
            for j in range(3, KT):
                ssm_merge(j)
            dve.wait_ge(s["dturn"], 1)
            for half in range(2):
                hp = slice(64 * half, 64 * half + 64)
                dve.tensor_copy(attT[hp, :, SEQ:TOK],
                                bank[hp, 4, 0:64].rearrange("p (q r) -> p q r", q=2)[:, :, 8 * half:8 * half + NB]
                                ).then_inc(s["doc"], 1)
            dve.tensor_copy(memT[:, :, SEQ:TOK],
                            bank[:, 5, 0:P].rearrange("p (h r) -> p h r", h=MH)[:, :, 0:NB]).then_inc(s["doc"], 1)

            dve.wait_ge(s["Sfree"], KT)
            for j in range(KT):
                for i, branch in enumerate((0, 2)):
                    dve.wait_ge(s["Pj"], 2 * j + i + 1)
                    times_gate(3 * j + branch, 4 * i).then_inc(s["Pfree"], 1)
                    dve.wait_ge(s["Pfree"], 2 * j + i + 1)
                then(TT(gates[:, 3 * j, :], gates[:, 3 * j, :], gates[:, 3 * j + 1, :], ALU.add))
                TT(gates[:, 3 * j, :], gates[:, 3 * j, :], gates[:, 3 * j + 2, :], ALU.add).then_inc(s["merged"], 1)

            dve.wait_ge(s["xr"], 16 * 3)
            dve.wait_ge(s["gain2"], 16)
            for T in range(NT):
                n = ROWS[T]
                b0 = 2 * (T % 2)
                if T == 3:
                    dve.wait_ge(s["xr_last"], 32)
                if T < NT - 1:
                    dve.wait_ge(s["wo_mm"], T + 1)
                    TT(h_rows[0:n, T, :].rearrange("p (h t) -> p h t", h=2),
                       x_rows[0:n, T, :].rearrange("p (h t) -> p h t", h=2), bank[0:n, b0:b0 + 2, :], ALU.add
                       ).then_inc(s["h"], 1)
                else:
                    dve.wait_ge(s["wo_mm"], NT + 1)
                    dve.wait_ge(s["h_moved"], 1)
                    then(TT(h_rows[0:n, T, 0:512], x_rows[0:n, T, 0:512], bank[0:n, b0, :], ALU.add))
                    TT(h_rows[0:n, T, 512:D], x_rows[0:n, T, 512:D], h_rows[0:n, T, 512:D], ALU.add
                       ).then_inc(s["h"], 1)
                dve.wait_ge(s["hrms"], T + 1)
                then(dve.reciprocal(stat[0:n, 37 + T:38 + T], stat[0:n, 37 + T:38 + T]))
                STT(out=hn_rows[0:n, T, :], in0=h_rows[0:n, T, :], scalar=stat[0:n, 37 + T:38 + T],
                    in1=gain2[0:n, :], op0=ALU.mult, op1=ALU.mult).then_inc(s["hn"], 1)

            then(dve.memset(lg, 0.0))
            dve.wait_ge(s["lg"], NT)
            width = NGRP + NE
            then(TT(lg[:, 0:4, :], b_route.unsqueeze(1).to_broadcast([P, 4, width]),
                    bank[:, 6, 0:4 * width].rearrange("p (t e) -> p t e", t=4), ALU.add),
                 TT(lg[0:NB, 4, :], b_route[0:NB, :], bank[0:NB, 6, 4 * width:5 * width], ALU.add))
            gl, ell = lg[:, :, 0:NGRP], lg[:, :, NGRP:]
            gmx, kmx, pg, v1, df, e2x, v2, k2, gs, de = r5[0], r5[1], r5[2], r5[3], r5[4], r5[5], r5[6], r5[7], \
                r5[8], r5[9]

            def over5(x, n):
                return x.unsqueeze(1).to_broadcast([P, NT, n])

            def first_max(out, x, mx, key, rev, n, kbest):
                then(dve.tensor_reduce(mx, x, AX, ALU.max))
                then(TT(key, x, wide(mx, 2, (NT, n)), ALU.is_equal))
                then(TT(key, key, over5(rev, n), ALU.mult))
                then(dve.tensor_reduce(kbest, key, AX, ALU.max))
                then(TT(out, over5(rev, n), wide(kbest, 2, (NT, n)), ALU.is_equal))

            first_max(og, gl, gmx, eq4, c["rev4"], NGRP, kmx)
            TT(ex4, gl, wide(gmx, 2, (NT, NGRP)), ALU.subtract).then_inc(s["gmax"], 1)
            el4 = el.rearrange("p t (g e) -> p t g e", g=NGRP)
            shape4 = (NT, NGRP, EPG)
            then(TT(el4, ell.rearrange("p t (g e) -> p t g e", g=NGRP), wide(og, 3, shape4), ALU.mult),
                 TS(eq4, og, BIG, -BIG, ALU.mult, ALU.add))
            then(TT(el4, el4, wide(eq4, 3, shape4), ALU.add))
            first_max(m12[0], el, v1, eq32, c["rev32"], NE, kmx)
            then(STT(out=el, in0=m12[0], scalar=-2 * BIG, in1=el, op0=ALU.mult, op1=ALU.add))
            first_max(m12[1], el, v2, eq32, c["rev32"], NE, k2)
            TT(df, v2, v1, ALU.subtract).then_inc(s["gmax"], 1)
            then(*[TS(m[:, NT - 1, :], m[:, NT - 1, :], c["valid"], None, ALU.mult) for m in m12])
            then(TT(chosen, m12[0], m12[1], ALU.add))
            dve.sem_inc(s["chosen"], 1)
            then(*[TT(mt, m, wide(c["tokid"], 2, (NT, NE)), ALU.mult) for mt, m in zip(mtok, m12)])
            dve.wait_ge(s["rank"], 1)
            tile_count = bank[:, 4, 0:NT * NE].rearrange("p (t e) -> p t e", t=NT)
            then(dve.tensor_copy(rank.rearrange("p a b -> p (a b)"), bank[:, 5, 0:NT * NE]),
                 dve.tensor_copy(count[:, 0, :], tile_count[:, 0, :]))
            for T in range(1, NT):
                then(TT(count[:, T, :], count[:, T - 1, :], tile_count[:, T, :], ALU.add))
            then(TT(rank[:, 1:, :], rank[:, 1:, :], count[:, 0:NT - 1, :], ALU.add),
                 dve.tensor_reduce(stat[:, 52:53], count[:, NT - 1, :], AX, ALU.max))
            then(TT(over, c["passes"], stat[:, 52:53].to_broadcast([P, MAXP]), ALU.is_lt),
                 *[TT(x, m, rank, ALU.mult) for x, m in zip((tmp32, eq32), m12)])
            then(dve.tensor_reduce(stat[:, 53:54], over, AX, ALU.add),
                 *[dve.tensor_reduce(x, y, AX, ALU.add) for x, y in zip(slotk, (tmp32, eq32))])
            dve.tensor_copy(n_pass[:, :], stat[0:1, 53:54]).then_inc(s["npass"], 1)
            dve.wait_ge(s["gexp"], 2)
            dve.wait_ge(s["npass"], 1)
            n_p = dve.value_load(n_pass[0:1, 0:1], min_val=1, max_val=MAXP)
            with dve.Fori(0, n_p) as p:
                for k in range(2):
                    TT(hot[k], over5(c["slot"], CAP), wide(slotk[k], 2, (NT, CAP)), ALU.is_equal
                       ).then_inc(s["rtab"], 1)
                dve.wait_ge(s["rtab"], p * 22 + 2)
                dve.sem_inc(s["hot"], 1)
                dve.wait_ge(s["idxmm"], p + 1)
                dve.tensor_copy(gather_rows[:, :], bank[0:CAP, 7, 0:NE]).then_inc(s["idx"], 1)
                for k in range(2):
                    dve.tensor_reduce(inpass[k], hot[k], AX, ALU.add).then_inc(s["rtab"], 1)
                    TT((tmp32, eq32)[k], m12[k], over5(c["yrow"], NE), ALU.mult).then_inc(s["rtab"], 1)
                dve.tensor_reduce(gs, ex4, AX, ALU.add).then_inc(s["rtab"], 1)
                TS(de, e2x, 1.0, None, ALU.add).then_inc(s["rtab"], 1)
                dve.wait_ge(s["rtab"], p * 22 + 8)
                for k in range(2):
                    dve.tensor_reduce(row0[k], (tmp32, eq32)[k], AX, ALU.add).then_inc(s["rtab"], 1)
                dve.reciprocal(pg, gs).then_inc(s["rtab"], 1)
                dve.reciprocal(de, de).then_inc(s["rtab"], 1)
                dve.wait_ge(s["rtab"], p * 22 + 12)
                for k in range(2):
                    TT(row_now[k], row0[k], slotk[k], ALU.add).then_inc(s["rtab"], 1)
                TT(gatek[0], pg, de, ALU.mult).then_inc(s["rtab"], 1)
                dve.wait_ge(s["rtab"], p * 22 + 15)
                for k in range(2):
                    TT(row_now[k], row_now[k], inpass[k], ALU.mult).then_inc(s["rtab"], 1)
                    TS(slotk[k], slotk[k], -float(CAP), None, ALU.add).then_inc(s["rtab"], 1)
                TT(gatek[1], gatek[0], e2x, ALU.mult).then_inc(s["rtab"], 1)
                dve.wait_ge(s["rtab"], p * 22 + 20)
                for k in range(2):
                    TT(gate_now[k], gatek[k], inpass[k], ALU.mult).then_inc(s["rtab"], 1)
                    dve.tensor_copy(y_rows[:, k, :], row_now[k]).then_inc(s["yrow"], 1)
                dve.wait_ge(s["rtab"], p * 22 + 22)
                dve.sem_inc(s["held"], 1)
                with dve.Fori(0, NE // 2) as e2:
                    for u in range(2):
                        step = p * NE + e2 * 2
                        dve.wait_ge(s["xt"], step + (u + 3))
                        dve.wait_ge(s["gu"], p * (2 * NE) + e2 * 4 + (2 * u + 2))
                        dve.tensor_copy(xgT[u].rearrange("p a b -> p (a b)"), bank[:, u, :]).then_inc(s["xc"], 1)
                        dve.wait_ge(s["sg"], step + (u + 1))
                        dve.wait_ge(s["ht2"], step + (u + 1))
                        TT(hidden[u], sg[u], bank[:, 2 + u, FE // 2:FE], ALU.mult).then_inc(s["hid"], 1)
                        dve.wait_ge(s["ht2"], step + (u + 3))
                        dve.wait_ge(s["y"], p * (2 * NE) + e2 * 4 + (2 * u + 2))
                        dve.tensor_copy(hT[u].rearrange("p a b -> p (a b)"), bank[:, 4 + u, 0:2 * P]
                                        ).then_inc(s["hT"], 1)

                for T in range(NT):
                    n = ROWS[T]
                    per = 32 * len(range(T % 3, NT, 3))
                    dve.wait_ge(s[f"yk{T % 3}"], p * per + 32 * (T // 3 + 1))
                    STT(out=h_rows[0:n, T, :], in0=yk[T % 3][0][0:n, :], scalar=gate_now[0][0:n, T:T + 1],
                        in1=h_rows[0:n, T, :], op0=ALU.mult, op1=ALU.add).then_inc(s["fadd"], 1)
                    dve.wait_ge(s["fadd"], p * NT + (T + 1))
                    STT(out=h_rows[0:n, T, :], in0=yk[T % 3][1][0:n, :], scalar=gate_now[1][0:n, T:T + 1],
                        in1=h_rows[0:n, T, :], op0=ALU.mult, op1=ALU.add).then_inc(s["fsum"], 1)

            dve.wait_ge(s["gainf"], 16)
            for T in range(NT):
                n = ROWS[T]
                dve.wait_ge(s["frms"], T + 1)
                then(dve.reciprocal(stat[0:n, 47 + T:48 + T], stat[0:n, 47 + T:48 + T]))
                STT(out=h_rows[0:n, T, :], in0=h_rows[0:n, T, :], scalar=stat[0:n, 47 + T:48 + T],
                    in1=gain_f[0:n, :], op0=ALU.mult, op1=ALU.mult).then_inc(s["fin"], 1)


def shape_constants():
    c = {}
    i = np.arange(P)
    c["ident"] = np.eye(P)
    c["triu"] = (i[:, None] < i[None, :])
    c["ones"] = np.ones((P, P))
    c["smask"] = (i[:, None] // SCH == np.arange(CH)[None, :])
    row = np.arange(64)
    used = (row % 32) < 16
    esel = np.zeros((P, NB))
    esel[0:64] = (row[:, None] % 8 == np.arange(NB)[None, :]) & used[:, None]
    c["esel"] = esel
    c["rev4"] = np.tile(NGRP - np.arange(NGRP), (P, 1))
    c["rev32"] = np.tile(NE - np.arange(NE), (P, 1))
    c["yrow"] = np.tile(np.arange(NE) * CAP, (P, 1))
    c["slot"] = np.tile(np.arange(CAP), (P, 1))
    c["tokid"] = i[:, None] + P * np.arange(NT)[None, :]
    c["valid"] = c["tokid"][:, NT - 1:] < TOK
    c["passes"] = np.tile(CAP * np.arange(MAXP), (P, 1))
    dec = np.zeros((P, NG * P))
    for r in row[used]:
        h = 2 * (r // 32) + r % 32 // 8
        for g in range(NG):
            dec[r, g * P:(g + 1) * P] = -slope(g * NH + h) / ATT_SCALE * DILS[g] * (P - np.arange(P))
    c["decbias"] = dec
    c["eps"] = np.full((P, 1), EPS)
    consts = np.concatenate([np.asarray(c[n], np.float32).reshape(P, w) for n, w in CONSTS], axis=1)
    a, b = i[:, None], i[None, :]
    d0 = np.empty((P, NCLS, NCLS, P))
    for r in range(NCLS):
        for k in range(NCLS):
            dist = 4 * (a - b) + r - k
            d0[:, r, k] = np.where((dist >= 0) & (dist <= WINDOWS[0]), dist, BIG)
    ratio = [2.0 ** (-8.0 * g * NH / (NG * NH)) for g in range(NG)]
    dist = 4 * (a - b)
    d1 = np.where(dist >= 0, dist * ratio[1], BIG)
    d2 = np.where((dist >= 0) & (dist % DILS[2] == 0), dist * ratio[2], BIG)
    return (consts, d0.reshape(P, NCLS, SEQ).astype(np.float32),
            np.concatenate([d1, d2], axis=1).astype(np.float32))


def kernel(**inputs):
    import concourse.bacc as bacc
    from concourse.bass_utils import run_bass_kernel_spmd as run

    v = {k: np.asarray(a) for k, a in inputs.items()}
    a = {}

    def feat(w):
        return w.reshape(-1, P, w.shape[-1]).transpose(1, 0, 2)

    def states(x):
        lead = x.shape[:-2]
        y = x.reshape(lead + (NJ, P))
        return np.moveaxis(y, -1, 0)

    xp, xs = v["x_prompt"][0], v["x_sample"][:, 0]
    xcols = np.concatenate([xp.reshape(P, NCLS, D).transpose(1, 0, 2).reshape(SEQ, D), xs], axis=0)
    a["xT"] = xcols.T.reshape(KT, P, TOK).transpose(1, 0, 2)
    a["x_prompt"], a["x_sample"] = xp, xs
    a["memT"] = feat(v["mem_prompt"][0].T)
    w_in = v["w_in"][0]
    ssm0, mq0, gate0 = NG * 3 * ATT, NG * 3 * ATT + SSMW, NG * 3 * ATT + SSMW + MH * MD
    cols = [w_in[:, ssm0:mq0], w_in[:, 0:ssm0], w_in[:, mq0:gate0], v["w_mk"][0], v["w_mv"][0],
            w_in[:, gate0:].reshape(D, 3, KT, P).transpose(0, 2, 1, 3).reshape(D, 3 * D)]
    stream = np.concatenate(cols, axis=1)
    a["w_stream"] = stream.reshape(KT, P, -1, P).transpose(2, 1, 0, 3)
    a["consts"], a["dist0"], a["dist12"] = shape_constants()
    a["gain1"], a["gain_mem"] = v["norm1"][0].reshape(KT, P).T, v["norm_mem"][0].reshape(KT, P).T
    a["norm2"], a["norm_f"] = v["norm2"][0], v["norm_f"]
    ldt = np.broadcast_to(v["log_dt"][0][:, None], (SG, SST))
    a["ssm_in"] = np.stack([states(x) for x in (v["lam_re"][0], v["lam_im"][0], ldt)], axis=1)
    a["b_in"] = np.stack([v[f"ssm_b_{x}"][0].reshape(NJ, P, SCH).transpose(1, 0, 2) for x in ("re", "im")], axis=1)
    a["c_in"] = np.stack([v[f"ssm_c_{x}"][0].transpose(0, 2, 1).reshape(NJ, P, SCH).transpose(1, 0, 2)
                          for x in ("re", "im")], axis=1)
    a["h0"] = np.stack([states(v[f"state_ssm_{x}"][0]).transpose(0, 2, 1) for x in ("re", "im")], axis=1)
    a["ssm_d"], a["b_glu"] = v["ssm_d"][0].reshape(4, P).T, v["b_glu"][0].reshape(4, P).T
    a["w_glu"], a["w_att"], a["w_ssm"] = feat(v["w_glu"][0]), feat(v["w_att_out"][0]), feat(v["w_ssm_out"][0])
    a["w_mem"], a["w_o"] = feat(v["w_mem_out"][0]), feat(v["w_o"][0])
    a["w_route"] = feat(np.concatenate([v["w_grp"][0], v["w_exp"][0]], axis=1))
    a["b_route"] = np.concatenate([v["b_grp"][0], v["b_exp"][0]])
    a["w1"], a["w3"], a["w2"] = v["w1"][0], v["w3"][0], v["w2"][0]
    keys = []
    for g in range(NG):
        for kv in "kv":
            a[f"cache_swa{g}_{kv}"] = v[f"cache_swa{g}_{kv}"][0].reshape(NB, WINDOWS[g], ATT)
        k = v[f"cache_swa{g}_k"][0][:, ::DILS[g]]
        keys.append(k.reshape(NB, P, 2, 2, DH).transpose(0, 3, 4, 2, 1).reshape(NB, P, 2, P))
    a["k_dec"] = np.stack(keys, axis=2)
    a["mk_dec"] = v["cache_mem_k"][0].transpose(0, 3, 2, 1)
    a["cache_mem_v"] = v["cache_mem_v"][0].reshape(NB, MEM, MH * MD)

    outs = {"y_prompt": (SEQ, D), "y_sample": (NB, D), "prompt_mem_k": (MEM, MH * MD),
            "prompt_mem_v": (MEM, MH * MD), "st_prompt": (P, 2, NJ), "st_dec": (P, 2, NJ, NB)}
    for g in range(NG):
        for kv in "kv":
            outs[f"prompt_swa{g}_{kv}"] = (min(WINDOWS[g], SEQ), ATT)
            outs[f"sample_swa{g}_{kv}"] = (NB, WINDOWS[g], ATT)

    nc = bacc.Bacc("TRN2", target_bir_lowering=False, num_devices=1)
    arrays, t = {}, {}
    for name, x in a.items():
        x = np.ascontiguousarray(x)
        arrays["in_" + name] = x
        t[name] = nc.dram_tensor("in_" + name, x.shape, F32, kind="ExternalInput").ap()
    for name, shape in outs.items():
        t[name] = nc.dram_tensor("out_" + name, shape, F32, kind="ExternalOutput").ap()
    t["hn_dram"] = nc.dram_tensor("hn_dram", (TOK, D), F32).ap()
    t["y_dram"] = nc.dram_tensor("y_dram", (NE * CAP, D), F32).ap()
    t["y_slots"] = t["y_dram"].rearrange("(e s) d -> e s d", e=NE)
    build(nc, t)
    got = run(nc, [arrays], core_ids=[0]).results[0]
    o = {name: got["out_" + name] for name in outs}

    def swa(kind, g, kv):
        x = o[f"{kind}_swa{g}_{kv}"]
        return x.reshape(1, 1 if kind == "prompt" else NB, -1, NH, DH)

    def st_p(i):
        return np.ascontiguousarray(o["st_prompt"][:, i].T).reshape(1, 1, SG, SST)

    def st_d(i):
        return np.ascontiguousarray(o["st_dec"][:, i].transpose(2, 1, 0)).reshape(1, NB, SG, SST)

    return (o["y_prompt"].reshape(1, SEQ, D), o["y_sample"].reshape(NB, 1, D),
            *[swa("prompt", g, kv) for g in range(NG) for kv in "kv"],
            o["prompt_mem_k"].reshape(1, 1, MEM, MH, MD), o["prompt_mem_v"].reshape(1, 1, MEM, MH, MD),
            st_p(0), st_p(1),
            *[swa("sample", g, kv) for g in range(NG) for kv in "kv"],
            st_d(0), st_d(1))
```
